# Optimizing a Trainium2 kernel written in Bass

```python
import math
import jax, jax.numpy as jnp
from jax import lax
import numpy as np

D_MODEL = 1024
BATCH = 1
SEQ = 512
DEPTH = 1

N_MIXERS = 2
RMS_EPS = 1e-6
DN_HEAD_DIM = 128
DN_HEADS = D_MODEL // DN_HEAD_DIM
DN_WIDTH = DN_HEADS * DN_HEAD_DIM
DN_CONV = 4
DN_CHUNK = 64
DN_IN = 4 * DN_WIDTH + 2 * DN_HEADS
SWA_HEAD_DIM = 64
SWA_HEADS = D_MODEL // SWA_HEAD_DIM
SWA_KV_HEADS = SWA_HEADS // 8
SWA_GROUP = SWA_HEADS // SWA_KV_HEADS
SWA_QKV = (SWA_HEADS + 2 * SWA_KV_HEADS) * SWA_HEAD_DIM
WINDOW = 128
SWA_BLOCK = WINDOW
NUM_BUCKETS = 32
MAX_DISTANCE = 128
D_FF = 4 * D_MODEL
N_DN_LAYERS = (DEPTH + N_MIXERS - 1) // N_MIXERS
N_SWA_LAYERS = DEPTH // N_MIXERS


def rms_norm(x, w):
    xf = x.astype(jnp.float32)
    y = xf * lax.rsqrt(jnp.mean(xf * xf, axis=-1, keepdims=True) + RMS_EPS)
    return (y * w.astype(jnp.float32)).astype(x.dtype)

def l2_normalize(t):
    return t * lax.rsqrt(jnp.sum(t * t, axis=-1, keepdims=True) + RMS_EPS)

def causal_depthwise_conv(x, w):
    k = w.shape[0]
    return lax.conv_general_dilated(
        x, w[:, None, :].astype(x.dtype), window_strides=(1,), padding=[(k - 1, 0)],
        dimension_numbers=('NWC', 'WIO', 'NWC'), feature_group_count=x.shape[-1])

def chunk_gated_delta_rule(q, k, v, beta, g):
    B, S, H, DK = q.shape
    DV = v.shape[-1]
    C = DN_CHUNK
    N = S // C

    def to_chunks(t):
        return t.reshape(B, N, C, H, -1).transpose(0, 3, 1, 2, 4)

    q = to_chunks(q) * (DK ** -0.5)
    k = to_chunks(k)
    v = to_chunks(v)
    beta = beta.reshape(B, N, C, H).transpose(0, 3, 1, 2)
    gc = jnp.cumsum(g.reshape(B, N, C, H).transpose(0, 3, 1, 2), axis=-1)
    causal = jnp.tril(jnp.ones((C, C), dtype=bool))
    strict = jnp.tril(jnp.ones((C, C), dtype=bool), -1)
    decay = jnp.exp(jnp.where(causal, gc[..., :, None] - gc[..., None, :], -jnp.inf))
    k_beta = k * beta[..., None]
    lower = jnp.where(strict, jnp.einsum('bhnid,bhnjd->bhnij', k_beta, k) * decay, 0.0)
    eye = jnp.eye(C, dtype=jnp.float32)
    rhs = jnp.concatenate([v * beta[..., None], k_beta * jnp.exp(gc)[..., None]], axis=-1)
    sol = lax.linalg.triangular_solve(lower + eye, rhs, left_side=True, lower=True, unit_diagonal=True)
    u, w = sol[..., :DV], sol[..., DV:]
    attn = jnp.einsum('bhnid,bhnjd->bhnij', q, k) * decay
    q_dec = q * jnp.exp(gc)[..., None]
    k_dec = k * jnp.exp(gc[..., -1:] - gc)[..., None]
    g_last = jnp.exp(gc[..., -1])
    xs = tuple(jnp.moveaxis(t, 2, 0) for t in (q_dec, k_dec, u, w, attn, g_last))

    def step(state, inp):
        q_c, k_c, u_c, w_c, a_c, gl = inp
        v_new = u_c - jnp.einsum('bhck,bhkv->bhcv', w_c, state)
        o_c = jnp.einsum('bhck,bhkv->bhcv', q_c, state) + jnp.einsum('bhij,bhjv->bhiv', a_c, v_new)
        state = state * gl[..., None, None] + jnp.einsum('bhck,bhcv->bhkv', k_c, v_new)
        return state, o_c

    s0 = jnp.zeros((B, H, DK, DV), jnp.float32)
    _, o = lax.scan(step, s0, xs)
    return o.transpose(1, 0, 3, 2, 4).reshape(B, S, H, DV)

def gated_deltanet(h, w_in, conv_w, a_log, dt_bias, norm_w, w_out):
    B, S, _ = h.shape
    proj = h @ w_in
    qkv = jax.nn.silu(causal_depthwise_conv(proj[..., :3 * DN_WIDTH], conv_w))
    z = proj[..., 3 * DN_WIDTH:4 * DN_WIDTH]
    b = proj[..., 4 * DN_WIDTH:4 * DN_WIDTH + DN_HEADS]
    a = proj[..., 4 * DN_WIDTH + DN_HEADS:]
    q, k, v = jnp.split(qkv.astype(jnp.float32), 3, axis=-1)
    q = l2_normalize(q.reshape(B, S, DN_HEADS, DN_HEAD_DIM))
    k = l2_normalize(k.reshape(B, S, DN_HEADS, DN_HEAD_DIM))
    v = v.reshape(B, S, DN_HEADS, DN_HEAD_DIM)
    beta = jax.nn.sigmoid(b.astype(jnp.float32))
    g = -jnp.exp(a_log.astype(jnp.float32)) * jax.nn.softplus(a.astype(jnp.float32) + dt_bias.astype(jnp.float32))
    o = chunk_gated_delta_rule(q, k, v, beta, g)
    zf = z.reshape(B, S, DN_HEADS, DN_HEAD_DIM).astype(jnp.float32)
    o = o * lax.rsqrt(jnp.mean(o * o, axis=-1, keepdims=True) + RMS_EPS) * norm_w.astype(jnp.float32) * jax.nn.silu(zf)
    return o.reshape(B, S, DN_WIDTH).astype(h.dtype) @ w_out

def t5_causal_bucket(dist):
    n = jnp.maximum(dist, 0)
    max_exact = NUM_BUCKETS // 2
    large = max_exact + (jnp.log(jnp.maximum(n, 1).astype(jnp.float32) / max_exact)
                         / math.log(MAX_DISTANCE / max_exact) * (NUM_BUCKETS - max_exact)).astype(jnp.int32)
    large = jnp.minimum(large, NUM_BUCKETS - 1)
    return jnp.where(n < max_exact, n, large)

def sliding_window_sink_attention(h, w_qkv, b_qkv, sinks, w_out, b_out, rel_bias):
    B, S, _ = h.shape
    NB = S // SWA_BLOCK
    qkv = h @ w_qkv + b_qkv
    q = qkv[..., :SWA_HEADS * SWA_HEAD_DIM].reshape(B, NB, SWA_BLOCK, SWA_KV_HEADS, SWA_GROUP, SWA_HEAD_DIM)
    k = qkv[..., SWA_HEADS * SWA_HEAD_DIM:(SWA_HEADS + SWA_KV_HEADS) * SWA_HEAD_DIM]
    v = qkv[..., (SWA_HEADS + SWA_KV_HEADS) * SWA_HEAD_DIM:]
    k = k.reshape(B, NB, SWA_BLOCK, SWA_KV_HEADS, SWA_HEAD_DIM)
    v = v.reshape(B, NB, SWA_BLOCK, SWA_KV_HEADS, SWA_HEAD_DIM)
    pad = ((0, 0), (1, 0), (0, 0), (0, 0), (0, 0))
    kk = jnp.concatenate([jnp.pad(k[:, :-1], pad), k], axis=2)
    vv = jnp.concatenate([jnp.pad(v[:, :-1], pad), v], axis=2)
    logits = jnp.einsum('bnqhgd,bnkhd->bnhgqk', q, kk).astype(jnp.float32) * (SWA_HEAD_DIM ** -0.5)
    qi = jnp.arange(SWA_BLOCK)[:, None]
    kj = jnp.arange(2 * SWA_BLOCK)[None, :]
    dist = qi + SWA_BLOCK - kj
    bias = rel_bias[t5_causal_bucket(dist)].astype(jnp.float32)
    bias = bias.transpose(2, 0, 1).reshape(SWA_KV_HEADS, SWA_GROUP, SWA_BLOCK, 2 * SWA_BLOCK)
    key_pos = jnp.arange(NB)[:, None] * SWA_BLOCK - SWA_BLOCK + kj
    valid = ((dist >= 0) & (dist < WINDOW))[None] & (key_pos >= 0)[:, None, :]
    logits = jnp.where(valid[None, :, None, None], logits + bias, -jnp.inf)
    sink = sinks.astype(jnp.float32).reshape(SWA_KV_HEADS, SWA_GROUP)[None, None, :, :, None, None]
    m = jnp.maximum(jnp.max(logits, axis=-1, keepdims=True), sink)
    p = jnp.exp(logits - m)
    p = p / (jnp.sum(p, axis=-1, keepdims=True) + jnp.exp(sink - m))
    out = jnp.einsum('bnhgqk,bnkhd->bnqhgd', p.astype(vv.dtype), vv)
    out = out.reshape(B, S, SWA_HEADS * SWA_HEAD_DIM)
    return out @ w_out + b_out

def squared_relu_mlp(h, w_up, w_down):
    return jnp.square(jax.nn.relu(h @ w_up)) @ w_down

def first_inputs(seed: int = 0) -> dict:
    key = jax.random.key(seed)
    ks = jax.random.split(key, 18)
    f32 = jnp.float32

    def nrm(k, shape, scale):
        return jax.random.normal(k, shape, f32) * scale

    x = nrm(ks[0], (BATCH, SEQ, D_MODEL), 1.0)
    norm_mix = 1.0 + nrm(ks[1], (DEPTH, D_MODEL), 0.02)
    norm_mlp = 1.0 + nrm(ks[2], (DEPTH, D_MODEL), 0.02)
    norm_final = 1.0 + nrm(ks[3], (D_MODEL,), 0.02)
    dn_w_in = nrm(ks[4], (N_DN_LAYERS, D_MODEL, DN_IN), D_MODEL ** -0.5)
    dn_conv_w = nrm(ks[5], (N_DN_LAYERS, DN_CONV, 3 * DN_WIDTH), DN_CONV ** -0.5)
    dn_a_log = jnp.log(jax.random.uniform(ks[6], (N_DN_LAYERS, DN_HEADS), f32, 1.0, 16.0))
    dt = jnp.exp(jax.random.uniform(ks[7], (N_DN_LAYERS, DN_HEADS), f32, math.log(1e-3), math.log(1e-1)))
    dn_dt_bias = dt + jnp.log(-jnp.expm1(-dt))
    dn_norm_w = 1.0 + nrm(ks[8], (N_DN_LAYERS, DN_HEAD_DIM), 0.02)
    dn_w_out = nrm(ks[9], (N_DN_LAYERS, DN_WIDTH, D_MODEL), DN_WIDTH ** -0.5)
    swa_w_qkv = nrm(ks[10], (N_SWA_LAYERS, D_MODEL, SWA_QKV), D_MODEL ** -0.5)
    swa_b_qkv = nrm(ks[11], (N_SWA_LAYERS, SWA_QKV), 0.02)
    swa_sinks = nrm(ks[12], (N_SWA_LAYERS, SWA_HEADS), 0.5)
    swa_w_out = nrm(ks[13], (N_SWA_LAYERS, SWA_HEADS * SWA_HEAD_DIM, D_MODEL), (SWA_HEADS * SWA_HEAD_DIM) ** -0.5)
    swa_b_out = nrm(ks[14], (N_SWA_LAYERS, D_MODEL), 0.02)
    rel_bias = nrm(ks[15], (NUM_BUCKETS, SWA_HEADS), 0.5)
    mlp_w_up = nrm(ks[16], (DEPTH, D_MODEL, D_FF), D_MODEL ** -0.5)
    mlp_w_down = nrm(ks[17], (DEPTH, D_FF, D_MODEL), D_FF ** -0.5)
    return {'x': x, 'norm_mix': norm_mix, 'norm_mlp': norm_mlp, 'norm_final': norm_final,
            'dn_w_in': dn_w_in, 'dn_conv_w': dn_conv_w, 'dn_a_log': dn_a_log, 'dn_dt_bias': dn_dt_bias,
            'dn_norm_w': dn_norm_w, 'dn_w_out': dn_w_out,
            'swa_w_qkv': swa_w_qkv, 'swa_b_qkv': swa_b_qkv, 'swa_sinks': swa_sinks,
            'swa_w_out': swa_w_out, 'swa_b_out': swa_b_out, 'rel_bias': rel_bias,
            'mlp_w_up': mlp_w_up, 'mlp_w_down': mlp_w_down}

def first_block(x, norm_mix, norm_mlp, norm_final, dn_w_in, dn_conv_w, dn_a_log, dn_dt_bias, dn_norm_w,
              dn_w_out, swa_w_qkv, swa_b_qkv, swa_sinks, swa_w_out, swa_b_out, rel_bias,
              mlp_w_up, mlp_w_down):
    for i in range(DEPTH):
        h = rms_norm(x, norm_mix[i])
        j = i // N_MIXERS
        if i % N_MIXERS == 0:
            y = gated_deltanet(h, dn_w_in[j], dn_conv_w[j], dn_a_log[j], dn_dt_bias[j], dn_norm_w[j], dn_w_out[j])
        else:
            y = sliding_window_sink_attention(h, swa_w_qkv[j], swa_b_qkv[j], swa_sinks[j], swa_w_out[j],
                                              swa_b_out[j], rel_bias)
        x = x + y
        x = x + squared_relu_mlp(rms_norm(x, norm_mlp[i]), mlp_w_up[i], mlp_w_down[i])
    return rms_norm(x, norm_final)


NSA_HEADS = 8
NSA_KV_GROUPS = 2
NSA_HPG = NSA_HEADS // NSA_KV_GROUPS
NSA_HEAD_DIM = 64
NSA_WIDTH = NSA_HEADS * NSA_HEAD_DIM
NSA_KV_WIDTH = NSA_KV_GROUPS * NSA_HEAD_DIM
CMP_BLOCK = 32
CMP_STRIDE = 16
CMP_HIDDEN = 128
SLC_BLOCK = 64
SLC_TOPK = 16
WINDOW_2 = 512
N_BRANCH = 3
FORCED_SCORE = 1.0e4
MLA_HEADS = 8
MLA_NOPE_DIM = 64
MLA_ROPE_DIM = 32
MLA_V_DIM = 64
MLA_WIDTH = MLA_HEADS * MLA_V_DIM
MLA_Q_RANK = 256
MLA_KV_RANK = 128
MIX_WIDTH = NSA_WIDTH + MLA_WIDTH
Q_BLOCK = 128
ROPE_THETA = 10000.0
NORM_EPS = 1e-6
NEG_INF = -1e30

IN_SIZES = (
    NSA_WIDTH,
    NSA_KV_WIDTH, NSA_KV_WIDTH,
    NSA_KV_WIDTH, NSA_KV_WIDTH,
    NSA_KV_WIDTH, NSA_KV_WIDTH,
    NSA_HEADS * N_BRANCH,
    NSA_WIDTH,
    MLA_Q_RANK,
    MLA_KV_RANK,
    MLA_ROPE_DIM,
    MLA_WIDTH,
)
IN_WIDTH = sum(IN_SIZES)
IN_OFFSETS = tuple(int(o) for o in np.cumsum(IN_SIZES)[:-1])


def rms_norm_2(x, g):
    xf = x.astype(jnp.float32)
    y = xf * lax.rsqrt(jnp.mean(xf * xf, axis=-1, keepdims=True) + NORM_EPS)
    return (y * g.astype(jnp.float32)).astype(x.dtype)

def rope(x, pos):
    half = x.shape[-1] // 2
    inv = ROPE_THETA ** (-jnp.arange(half, dtype=jnp.float32) / half)
    ang = pos.astype(jnp.float32)[..., None] * inv
    cos = jnp.cos(ang)[:, :, None, :]
    sin = jnp.sin(ang)[:, :, None, :]
    xf = x.astype(jnp.float32)
    x1, x2 = xf[..., :half], xf[..., half:]
    out = jnp.concatenate([x1 * cos - x2 * sin, x2 * cos + x1 * sin], axis=-1)
    return out.astype(x.dtype)

def masked_softmax(s, mask):
    s = jnp.where(mask, s.astype(jnp.float32), NEG_INF)
    p = jax.nn.softmax(s, axis=-1)
    return jnp.where(mask, p, 0.0)

def compress(kv, cmp_pos, w1, w2):
    B, S, G, D = kv.shape
    r = CMP_BLOCK // CMP_STRIDE
    ns = S // CMP_STRIDE
    sub = kv.reshape(B, ns, CMP_STRIDE, G, D)
    nc = ns - r + 1
    blocks = jnp.concatenate([sub[:, j:j + nc] for j in range(r)], axis=2)
    blocks = blocks + cmp_pos[None, None, :, None, :]
    flat = blocks.transpose(0, 1, 3, 2, 4).reshape(B, nc, G, CMP_BLOCK * D)
    return jax.nn.silu(flat @ w1) @ w2

def cmp_to_slc_matrix(nc, nslc):
    start = np.arange(nc)[:, None] * CMP_STRIDE
    bstart = np.arange(nslc)[None, :] * SLC_BLOCK
    ov = np.minimum(start + CMP_BLOCK, bstart + SLC_BLOCK) - np.maximum(start, bstart)
    return (np.clip(ov, 0, None) / CMP_BLOCK).astype(np.float32)

def nsa_attention(q, k_cmp, v_cmp, k_slc, v_slc, k_win, v_win, gate_logits, positions,
                  cmp_pos, cmp_k_w1, cmp_k_w2, cmp_v_w1, cmp_v_w2):
    B, S = q.shape[:2]
    G, HPG, dk = NSA_KV_GROUPS, NSA_HPG, NSA_HEAD_DIM
    scale = dk ** -0.5
    nqb = S // Q_BLOCK
    t = np.arange(S)
    qg = rope(q.reshape(B, S, NSA_HEADS, dk), positions).reshape(B, S, G, HPG, dk)

    kc = compress(k_cmp.reshape(B, S, G, dk), cmp_pos, cmp_k_w1, cmp_k_w2)
    vc = compress(v_cmp.reshape(B, S, G, dk), cmp_pos, cmp_v_w1, cmp_v_w2)
    nc = kc.shape[1]
    cmp_end = np.arange(nc) * CMP_STRIDE + CMP_BLOCK - 1
    kc = rope(kc, positions[:, cmp_end])
    s_cmp = jnp.einsum('bsghd,bngd->bghsn', qg, kc).astype(jnp.float32) * scale
    p_cmp = masked_softmax(s_cmp, cmp_end[None, :] <= t[:, None])
    o_cmp = jnp.einsum('bghsn,bngd->bsghd', p_cmp.astype(vc.dtype), vc)

    nslc = S // SLC_BLOCK
    m = jnp.asarray(cmp_to_slc_matrix(nc, nslc))
    imp = jnp.einsum('bghsn,nj->bgsj', p_cmp, m)
    blk = np.arange(nslc)[None, :]
    cur = (t // SLC_BLOCK)[:, None]
    forced = (blk == 0) | (blk == cur) | (blk == cur - 1)
    imp = jnp.where(forced, FORCED_SCORE, jnp.where(blk > cur, -FORCED_SCORE, imp))
    n_sel = min(SLC_TOPK, nslc)
    _, sel_idx = lax.top_k(imp, n_sel)

    kb = rope(k_slc.reshape(B, S, G, dk), positions).reshape(B, nslc, SLC_BLOCK, G, dk).transpose(0, 3, 1, 2, 4)
    vb = v_slc.reshape(B, nslc, SLC_BLOCK, G, dk).transpose(0, 3, 1, 2, 4)
    q_chunks = qg.reshape(B, nqb, Q_BLOCK, G, HPG, dk).transpose(1, 0, 3, 2, 4, 5)
    idx_chunks = sel_idx.reshape(B, G, nqb, Q_BLOCK, n_sel).transpose(2, 0, 1, 3, 4)
    t_chunks = jnp.arange(S, dtype=jnp.int32).reshape(nqb, Q_BLOCK)
    gather = jax.vmap(jax.vmap(lambda blocks, ix: blocks[ix]))
    sb_offsets = jnp.arange(SLC_BLOCK, dtype=jnp.int32)

    def slc_block(args):
        qc, ic, tc = args
        kg = gather(kb, ic)
        vg = gather(vb, ic)
        s = jnp.einsum('bgqhd,bgqnkd->bgqhnk', qc, kg).astype(jnp.float32) * scale
        key_pos = ic[..., None] * SLC_BLOCK + sb_offsets
        mask = (key_pos <= tc[None, None, :, None, None]).reshape(B, G, Q_BLOCK, 1, n_sel * SLC_BLOCK)
        p = masked_softmax(s.reshape(B, G, Q_BLOCK, HPG, n_sel * SLC_BLOCK), mask)
        p = p.reshape(B, G, Q_BLOCK, HPG, n_sel, SLC_BLOCK)
        return jnp.einsum('bgqhnk,bgqnkd->bqghd', p.astype(vg.dtype), vg)

    o_slc = lax.map(slc_block, (q_chunks, idx_chunks, t_chunks))
    o_slc = o_slc.transpose(1, 0, 2, 3, 4, 5).reshape(B, S, G, HPG, dk)

    n_back = WINDOW_2 // Q_BLOCK

    def band(a):
        ap = jnp.pad(a, ((0, 0), (WINDOW_2, 0), (0, 0), (0, 0)))
        ab = ap.reshape(B, nqb + n_back, Q_BLOCK, G, dk)
        return jnp.concatenate([ab[:, j:j + nqb] for j in range(n_back + 1)], axis=2)

    kband = band(rope(k_win.reshape(B, S, G, dk), positions))
    vband = band(v_win.reshape(B, S, G, dk))
    qw = qg.reshape(B, nqb, Q_BLOCK, G, HPG, dk)
    s_win = jnp.einsum('bnqghd,bnkgd->bnghqk', qw, kband).astype(jnp.float32) * scale
    q_idx = np.arange(nqb)[:, None] * Q_BLOCK + np.arange(Q_BLOCK)[None, :]
    k_idx = np.arange(nqb)[:, None] * Q_BLOCK - WINDOW_2 + np.arange((n_back + 1) * Q_BLOCK)[None, :]
    diff = q_idx[:, :, None] - k_idx[:, None, :]
    win_mask = (diff >= 0) & (diff < WINDOW_2) & (k_idx[:, None, :] >= 0)
    p_win = masked_softmax(s_win, win_mask[None, :, None, None])
    o_win = jnp.einsum('bnghqk,bnkgd->bnqghd', p_win.astype(vband.dtype), vband).reshape(B, S, G, HPG, dk)

    g = jax.nn.sigmoid(gate_logits.astype(jnp.float32)).reshape(B, S, G, HPG, N_BRANCH).astype(q.dtype)
    o = g[..., 0:1] * o_cmp + g[..., 1:2] * o_slc + g[..., 2:3] * o_win
    return o.reshape(B, S, NSA_WIDTH)

def mla_attention(c_q, c_kv, k_rope, positions, q_norm_g, w_q_up, kv_norm_g, w_kv_up):
    B, S = c_q.shape[:2]
    H = MLA_HEADS
    nqb = S // Q_BLOCK
    q = (rms_norm_2(c_q, q_norm_g) @ w_q_up).reshape(B, S, H, MLA_NOPE_DIM + MLA_ROPE_DIM)
    q_nope = q[..., :MLA_NOPE_DIM]
    q_rot = rope(q[..., MLA_NOPE_DIM:], positions)
    kv = (rms_norm_2(c_kv, kv_norm_g) @ w_kv_up).reshape(B, S, H, MLA_NOPE_DIM + MLA_V_DIM)
    k_nope, v = kv[..., :MLA_NOPE_DIM], kv[..., MLA_NOPE_DIM:]
    k_rot = rope(k_rope[:, :, None, :], positions)[:, :, 0]
    scale = (MLA_NOPE_DIM + MLA_ROPE_DIM) ** -0.5
    qn_c = q_nope.reshape(B, nqb, Q_BLOCK, H, MLA_NOPE_DIM).transpose(1, 0, 2, 3, 4)
    qr_c = q_rot.reshape(B, nqb, Q_BLOCK, H, MLA_ROPE_DIM).transpose(1, 0, 2, 3, 4)
    t_chunks = jnp.arange(S, dtype=jnp.int32).reshape(nqb, Q_BLOCK)
    key_idx = jnp.arange(S, dtype=jnp.int32)

    def mla_block(args):
        qn, qr, tc = args
        s = (jnp.einsum('bqhd,bkhd->bhqk', qn, k_nope)
             + jnp.einsum('bqhd,bkd->bhqk', qr, k_rot)).astype(jnp.float32) * scale
        p = masked_softmax(s, key_idx[None, :] <= tc[:, None])
        return jnp.einsum('bhqk,bkhd->bqhd', p.astype(v.dtype), v)

    o = lax.map(mla_block, (qn_c, qr_c, t_chunks))
    return o.transpose(1, 0, 2, 3, 4).reshape(B, S, MLA_WIDTH)

def second_inputs(seed: int = 0) -> dict:
    key = jax.random.key(seed)
    ks = jax.random.split(key, 20)
    f32 = jnp.float32
    L, D = DEPTH, D_MODEL

    def nrm(k, shape, fan_in, gain=1.0):
        return jax.random.normal(k, shape, f32) * (gain * fan_in ** -0.5)

    def gain(k, shape):
        return 1.0 + 0.02 * jax.random.normal(k, shape, f32)

    x = jax.random.normal(ks[0], (BATCH, SEQ, D), f32)
    c = jax.random.normal(ks[1], (BATCH, D), f32)
    offset = jax.random.randint(ks[2], (BATCH, 1), 0, 1024, dtype=jnp.int32)
    positions = offset + jnp.arange(SEQ, dtype=jnp.int32)[None, :]
    return {
        "x": x,
        "c": c,
        "positions": positions,
        "ada_w": nrm(ks[3], (L, D, 3 * D), D, 0.5),
        "ada_b": 0.01 * jax.random.normal(ks[4], (L, 3 * D), f32),
        "norm_g": gain(ks[5], (L, D)),
        "w_in": nrm(ks[6], (L, D, IN_WIDTH), D),
        "cmp_pos": 0.02 * jax.random.normal(ks[7], (L, CMP_BLOCK, NSA_HEAD_DIM), f32),
        "cmp_k_w1": nrm(ks[8], (L, CMP_BLOCK * NSA_HEAD_DIM, CMP_HIDDEN), CMP_BLOCK * NSA_HEAD_DIM),
        "cmp_k_w2": nrm(ks[9], (L, CMP_HIDDEN, NSA_HEAD_DIM), CMP_HIDDEN),
        "cmp_v_w1": nrm(ks[10], (L, CMP_BLOCK * NSA_HEAD_DIM, CMP_HIDDEN), CMP_BLOCK * NSA_HEAD_DIM),
        "cmp_v_w2": nrm(ks[11], (L, CMP_HIDDEN, NSA_HEAD_DIM), CMP_HIDDEN),
        "q_norm_g": gain(ks[12], (L, MLA_Q_RANK)),
        "w_q_up": nrm(ks[13], (L, MLA_Q_RANK, MLA_HEADS * (MLA_NOPE_DIM + MLA_ROPE_DIM)), MLA_Q_RANK),
        "kv_norm_g": gain(ks[14], (L, MLA_KV_RANK)),
        "w_kv_up": nrm(ks[15], (L, MLA_KV_RANK, MLA_HEADS * (MLA_NOPE_DIM + MLA_V_DIM)), MLA_KV_RANK),
        "w_out": nrm(ks[16], (L, MIX_WIDTH, D), MIX_WIDTH),
        "final_norm_g": gain(ks[17], (D,)),
    }

def second_block(x, c, positions, ada_w, ada_b, norm_g, w_in, cmp_pos, cmp_k_w1, cmp_k_w2,
              cmp_v_w1, cmp_v_w2, q_norm_g, w_q_up, kv_norm_g, w_kv_up, w_out, final_norm_g):
    for l in range(DEPTH):
        mod = jax.nn.silu(c) @ ada_w[l] + ada_b[l]
        shift, scl, gate = jnp.split(mod, 3, axis=-1)
        h = rms_norm_2(x, norm_g[l]) * (1.0 + scl[:, None, :]) + shift[:, None, :]

        proj = h @ w_in[l]
        (q_n, kc_n, vc_n, ks_n, vs_n, kw_n, vw_n, gl_n, z_nsa,
         cq_m, ckv_m, kr_m, z_mla) = jnp.split(proj, IN_OFFSETS, axis=-1)

        o_nsa = nsa_attention(q_n, kc_n, vc_n, ks_n, vs_n, kw_n, vw_n, gl_n, positions,
                              cmp_pos[l], cmp_k_w1[l], cmp_k_w2[l], cmp_v_w1[l], cmp_v_w2[l])
        o_mla = mla_attention(cq_m, ckv_m, kr_m, positions,
                              q_norm_g[l], w_q_up[l], kv_norm_g[l], w_kv_up[l])

        mixed = jnp.concatenate([o_nsa * jax.nn.silu(z_nsa), o_mla * jax.nn.silu(z_mla)], axis=-1)
        x = x + gate[:, None, :] * (mixed @ w_out[l])
    return rms_norm_2(x, final_norm_g)


def setup_inputs(seed=0):
    out = dict(first_inputs(seed))
    for name, value in second_inputs(seed + 1).items():
        if name != "x":
            out[name + "_2"] = value
    return out


def reference(
    x, norm_mix, norm_mlp, norm_final, dn_w_in, dn_conv_w, dn_a_log, dn_dt_bias, dn_norm_w,
    dn_w_out, swa_w_qkv, swa_b_qkv, swa_sinks, swa_w_out, swa_b_out, rel_bias, mlp_w_up,
    mlp_w_down, c_2, positions_2, ada_w_2, ada_b_2, norm_g_2, w_in_2, cmp_pos_2, cmp_k_w1_2,
    cmp_k_w2_2, cmp_v_w1_2, cmp_v_w2_2, q_norm_g_2, w_q_up_2, kv_norm_g_2, w_kv_up_2, w_out_2,
    final_norm_g_2,
):
    x = first_block(
        x, norm_mix, norm_mlp, norm_final, dn_w_in, dn_conv_w, dn_a_log, dn_dt_bias, dn_norm_w,
        dn_w_out, swa_w_qkv, swa_b_qkv, swa_sinks, swa_w_out, swa_b_out, rel_bias, mlp_w_up,
        mlp_w_down,
    )
    return second_block(
        x, c_2, positions_2, ada_w_2, ada_b_2, norm_g_2, w_in_2, cmp_pos_2, cmp_k_w1_2,
        cmp_k_w2_2, cmp_v_w1_2, cmp_v_w2_2, q_norm_g_2, w_q_up_2, kv_norm_g_2, w_kv_up_2,
        w_out_2, final_norm_g_2,
    )


_drawn_inputs = setup_inputs


def setup_inputs(seed=0):
    import zlib

    import numpy as np

    out = dict(_drawn_inputs(seed))
    spreads = {}
    factors = {'norm_mix': 2.87,
     'norm_mlp': 3.322,
     'norm_final': 3.005,
     'dn_norm_w': 4.762,
     'ada_b_2': 8.0,
     'norm_g_2': 8.0,
     'cmp_pos_2': 8.0,
     'cmp_k_w1_2': 7.184,
     'cmp_k_w2_2': 6.742,
     'q_norm_g_2': 8.0,
     'w_q_up_2': 3.256,
     'kv_norm_g_2': 8.0,
     'final_norm_g_2': 2.818}
    for name, (base, spread) in spreads.items():
        noise = np.random.default_rng([zlib.crc32(name.encode()), seed]).standard_normal(out[name].shape)
        drawn = base * np.exp(spread * noise) if base else spread * noise
        out[name] = __import__('jax').numpy.asarray(drawn.astype(out[name].dtype))
    for name, factor in factors.items():
        out[name] = (out[name] * factor).astype(out[name].dtype)
    return out
```

```python
from contextlib import ExitStack

import numpy as np

import concourse.bass as bass
from concourse import mybir

P = 128
D = 1024
T = 512
KT = D // P
CH = T // P
H = 8
FF = 4 * D
QUARTERS = FF // D
EPS = 1e-6
RING = 4
NEG = -1e30

BA_LEAD = 96
DN_UNITS = 1 + 4 * H
U_OUT = DN_UNITS
U_MLP = U_OUT + KT
U_TWO = U_MLP + 2 * KT * QUARTERS

QH, DK = 8, 64
MN, MR = 64, 32
MD = MN + MR
CMP_BLOCK, CMP_STRIDE, CMP_HID = 32, 16, 128
NC = T // CMP_STRIDE - CMP_BLOCK // CMP_STRIDE + 1
NCP = 32
QW = QH * DK
AT_KC, AT_VC, AT_KS, AT_VS, AT_KW, AT_VW = (QW + P * n for n in range(6))
AT_GATE = QW + 6 * P
AT_Z = AT_GATE + 3 * QH
AT_CQ = AT_Z + QW
AT_CKV = AT_CQ + 256
AT_KR = AT_CKV + P
AT_ZM = AT_KR + MR
TWO = ["kc", "vc", "gate", "vs", "vw", "cq0", "cq1", "ckv", "kr", "ks", "kw", "q0", "q1", "q2", "q3"]
U_Z = U_TWO + len(TWO)
U_OUT2 = U_Z + KT
UNITS = U_OUT2 + KT
AUX = ["gate", "vs", "vw", "kr", "ks", "kw", "q0", "q1", "q2", "q3"]
ROPE = ["kr", "ks", "kw", "q0", "q1", "q2", "q3"]
TWO_PI = 6.28125, 0.0019350051879882812, 3.0199159819567e-07
MAGIC = 1.5 * 2.0 ** 23

LEVELS = [1, 2, 4, 8, 16, 32, 64]
NL = len(LEVELS)


def side_by_side(parts):
    cols, at, blocks = {}, 0, []
    for name, block in parts.items():
        cols[name] = (at, at + block.shape[1])
        at += block.shape[1]
        blocks.append(block)
    return np.ascontiguousarray(np.concatenate(blocks, axis=1).astype(np.float32)), cols


def shape_constants():
    i = np.arange(P)
    parts = {}
    parts["ident"] = np.eye(P)
    parts["mean"] = np.full((P, P), 1.0 / D)
    parts["ones"] = np.ones((P, P))
    parts["upto"] = (i[:, None] <= i[None, :]) * 1.0
    parts["after"] = (i[:, None] > i[None, :]) * 1.0
    for s in LEVELS:
        a, b = i[:, None] // s, i[None, :] // s
        parts[f"level{s}"] = ((a == b + 1) & (b % 2 == 0)) * 1.0
    parts["eps"] = np.tile(np.array([[EPS, 4 * EPS]]), (P, 1))
    return side_by_side(parts)


def shape_constants_2():
    i = np.arange(P)
    parts = {}
    parts["causal"] = np.where(i[None, :] <= i[:, None], 0.0, NEG)
    blk, t = np.arange(NCP)[None, None, :], (np.arange(CH) * P)[None, :, None] + i[:, None, None]
    seen = (blk * CMP_STRIDE + CMP_BLOCK - 1 <= t) & (blk < NC)
    parts["cmp_neg"] = np.where(seen, 0.0, NEG).reshape(P, -1)
    parts["cmp_one"] = (seen * 1.0).reshape(P, -1)
    for name, rows, first, width in (("rot", P, 0, 64), ("rot_m", P, 64, 32)):
        m = np.zeros((P, P))
        for h0 in range(first, P if first == 0 else 96, width):
            for d in range(width // 2):
                m[h0 + d + width // 2, h0 + d] = -1.0
                m[h0 + d, h0 + d + width // 2] = 1.0
        parts[name] = m
    for name, first, width in (("freq", 0, 64), ("freq_m", 64, 32)):
        half = width // 2
        inv = np.float32(10000.0) ** (-np.arange(half, dtype=np.float32) / np.float32(half))
        f = np.array([inv[(p - first) % width % half] if first <= p < (P if first == 0 else 96) else 0.0 for p in range(P)])
        parts[name] = f[:, None]
    return side_by_side(parts)


VEC_ROWS = {"norm_mix": KT, "norm_mlp": KT, "norm_final": KT, "norm_g_2": KT, "final_norm_g_2": KT,
            "ada_b_2": 3 * KT, "q_norm_g_2": 2, "kv_norm_g_2": 1, "dn_norm_w": 1, "c_2": KT}
VEC_AT, NVEC = {}, 0
for _name, _rows in VEC_ROWS.items():
    VEC_AT[_name] = NVEC
    NVEC += _rows


def build(nc, A, out, const_cols, const2_cols):
    F32, F32R = mybir.dt.float32, mybir.dt.float32r
    ALU, ACT, AX = mybir.AluOpType, mybir.ActivationFunctionType, mybir.AxisListType
    ctx = ExitStack()
    with ctx:
        place = [((nc.sbuf_base + 31) // 32) * 32]

        def at(name, shape, dt, offset):
            return nc.alloc_sbuf_tensor_at(name, shape, dt, offset=offset)

        def sb(name, shape, dt=F32):
            o = place[0]
            place[0] += ((int(np.prod(shape[1:])) * 4 + 31) // 32) * 32
            return at(name, shape, dt, o)

        def sem(name):
            return ctx.enter_context(nc.semaphore(name))

        xT = sb("xT", [P, KT, T])
        hhi = sb("hhi", [P, KT, T], F32R)
        hlo = sb("hlo", [P, KT, T], F32R)
        stage = sb("stage", [P, RING, KT, P])
        whi = sb("whi", [P, RING, KT, P], F32R)
        wlo = sb("wlo", [P, RING, KT, P], F32R)
        nconst = max(b for _, b in const_cols.values())
        const_at = place[0]
        const = sb("const", [P, nconst])
        K = {n: const[:, a:b] for n, (a, b) in const_cols.items()}
        vec = sb("vec", [P, NVEC])
        mod = sb("mod", [P, 4 * KT])
        cact = sb("cact", [P, KT])
        V = {n: vec[:, VEC_AT[n]:VEC_AT[n] + r] for n, r in VEC_ROWS.items()}
        act_at = place[0]
        ahi = [sb("ahi0", [P, KT, T], F32R), None]
        alo = [sb("alo0", [P, KT, T], F32R), None]
        scratch = place[0]
        ahi[1] = sb("ahi1", [P, KT, T], F32R)
        alo[1] = sb("alo1", [P, KT, T], F32R)
        mlp_end = place[0]

        place[0] = scratch
        convw = sb("convw", [P, 12, H])
        gates = sb("gates", [P, H, 4, CH])
        glog = sb("glog", [P, CH, H])
        qT = [sb(f"qT{b}", [P, T]) for b in range(2)]
        kT = [sb(f"kT{b}", [P, T]) for b in range(2)]
        vT = sb("vT", [P, T])
        zs = sb("zs", [P, T])
        acc = sb("acc", [P, T])
        th = sb("th", [P, T])
        sq = sb("sq", [P, 2, T])
        gd = sb("gd", [P, CH, P])
        gcol = sb("gcol", [P, CH])
        dec = sb("dec", [P, CH, P])
        decT = sb("decT", [P, CH, P])
        cols = [sb(f"cols{b}", [P, 12, CH]) for b in range(2)]
        low = sb("low", [P, CH, P])
        attnT = sb("attnT", [P, CH, P])
        kbeta = sb("kbeta", [P, CH, P])
        kdec = sb("kdec", [P, CH, P])
        vbeta = sb("vbeta", [P, CH, P])
        NB = 3
        lev = sb("lev", [P, NB, CH, P])
        inv = sb("inv", [P, CH, P])
        invTs = [sb(f"invT{b}", [P, CH, P]) for b in range(2)]
        qlev = {s: sb(f"qlev{s}", [P, CH, P]) for s in LEVELS[1:]}
        wT = sb("wT", [P, CH, P])
        vnew = sb("vnew", [P, CH, P])
        state = sb("state", [P, 2, P])
        o1 = sb("o1", [P, P])
        onat = sb("onat", [P, CH, P])
        osq = sb("osq", [P, CH, P])
        gf = sb("gf", [P, T])
        dn_end = place[0]
        place[0] = mlp_end
        nsq = sb("nsq", [P, 2, T])
        rs1, rr1 = sb("rs1", [P, T]), sb("rr1", [P, T])
        hf1 = sb("hf1", [P, 2, T])
        relu = sb("relu", [P, 2, T])
        af = hf1
        mod_w = sb("mod_w", [P, 3 * D])
        mod_acc = sb("mod_acc", [P, 3 * D])
        I32, BF16 = mybir.dt.int32, mybir.dt.bfloat16
        place[0] = act_at
        const2 = sb("const2", [P, max(b for _, b in const2_cols.values())])
        K2 = {n: const2[:, a:b] for n, (a, b) in const2_cols.items()}
        q2T_at = place[0]
        q2T = sb("q2T", [P, 4, T])
        kT2_at = place[0]
        kT2 = [sb(f"kT2_{b}", [P, T]) for b in range(2)]
        v2 = [sb(f"v2_{b}", [P, CH, P]) for b in range(2)]
        table = sb("table", [P, 4, T])
        cn = sb("cn", [P, 3, T])
        krT_at = place[0]
        krT = sb("krT", [P, T])
        identb, negb = sb("identb", [P, P], BF16), sb("negb", [P, P], BF16)
        gate2 = sb("gate2", [P, CH, 3 * QH])
        cposT = sb("cposT", [P, CMP_BLOCK])
        cpos = sb("cpos", [P, P])
        kcr = sb("kcr", [P, 2, NCP])
        ktmp = sb("ktmp", [P, 3, 2, NCP])
        hid = sb("hid", [P, 2, 2, 2, NCP])
        hid4 = sb("hid4", [P, 2, 4, NCP])
        vbd = sb("vbd", [P, 2, 4, DK])
        csm = sb("csm", [P, 4, 32])
        amax = sb("amax", [P, 8])
        aneg = sb("aneg", [P, 8])
        asum = sb("asum", [P, 8])
        ainv = sb("ainv", [P, 8])
        acoef = sb("acoef", [P, 8])
        w2c = sb("w2c", [P, 3, DK])
        small = place[0]
        raw = sb("raw", [P, 3, T])
        rcos = sb("rcos", [P, 2, T])
        rsin = sb("rsin", [P, T])
        csq = sb("csq", [P, 2, T])
        place[0] = small
        zs2 = sb("zs2", [P, KT, T])
        over = place[0]
        w1 = [sb(f"w1_{b}", [P, CMP_BLOCK, CMP_HID]) for b in range(2)]
        xb = sb("xb", [P, CMP_BLOCK, 2, NCP])
        kcT, vcT = (at(n, [P, T], F32, const_at + (const_cols["upto"][0] + b * T) * 4)
                    for b, n in enumerate(("kcT", "vcT")))
        turn = at("turn", [P, 4, T], F32, q2T_at)
        ang = at("ang", [P, 2, T], F32, kT2_at)
        pos_i = at("pos_i", [P, T], I32, krT_at)
        place[0] = over
        o_nsa = sb("o_nsa", [P, CH, QW])
        qm = sb("qm", [P, 2, T])
        km = sb("km", [P, 2, T])
        csc = at("csc", [P, 2, T], F32, place[0] - 4 * T * 4)
        cpT = at("cpT", [P, 2, T], F32, place[0] - 2 * T * 4)
        qh = sb("qh", [P, T])
        prob = sb("prob", [P, 2, T])
        probT = sb("probT", [P, 2, T])
        v_mla = sb("v_mla", [P, CH, QW])
        wq = sb("wq", [P, 2, 2, MD])
        wk = sb("wk", [P, 2, MN])
        wv = sb("wv", [P, QH, DK])
        gated = sb("gated", [P, 2, T])
        o_mla = at("o_mla", [P, CH, QW], F32, kT2_at)
        qraw = at("qraw", [P, 2, T], F32, q2T_at)
        qcos, qsin = (at(n, [P, T], F32, q2T_at + (2 + b) * T * 4) for b, n in enumerate(("qcos", "qsin")))
        place[0] = act_at
        onorm = sb("onorm", [P, 2, T])
        osqr = sb("osqr", [P, 2, T])
        ors, orr = sb("ors", [P, T]), sb("orr", [P, T])
        y = sb("y", [P, CH, D])
        assert place[0] <= small
        place[0] = act_at
        xn = sb("xn", [P, CH, D])
        rows = sb("rows", [P, 2, P])
        sqn = sb("sqn", [P, 2, T])
        rs = sb("rs", [P, T])
        rr = sb("rr", [P, T])
        hf = sb("hf", [P, 2, T])
        ba = sb("ba", [P, T])
        batok = sb("batok", [P, CH, 16])
        gtmp = sb("gtmp", [P, 4, CH, H])
        dtb = sb("dtb", [P, 2, H])
        assert place[0] <= scratch
        ps = ctx.enter_context(nc.psum_tensor("ps", [P, 8, T], F32))
        U = [ps[:, 0, :], ps[:, 1, :]]

        s = {}
        for name in """const_in x_in vec_in vec_tr vec_col xtr xev out_done
            w_hi w_lo w_used u_free
            n_sq n_stat n_sqrt n_rstd n_h n_hi n_lo
            ba_ev ba_tr ba_col gate_in gate_act gate_dve gate_ps gate_ready half_ready
            conv0 conv1 tanh seq_ready ztanh z_ready dz_in g_col dps dexp dmask sqs ss_ps norm_dve norm_act
            kk_ps kn_ps low_ready attn_ready kside lev_ready inv_ps inv_ready q_zero q_ps q_ev r_ps vn_ps vb_ready
            mod_c mod_in mod_done c2_in pos_in cpos_in w2_in wv_in
            act_steps dve_steps pool_steps pe_steps
            q_staged at_s at_max at_neg at_exp at_t at_tev at_o at_inv at_coef at_done
            p_ps p_ev p_rot p_cos p_sin p_q
            w_ps w_ev mlp_relu mlp_f mlp_hi mlp_lo v_ps v_ev st_ps st_ready o_ps o1_ps o1_ev o_ready o_stat o_act o_scaled o_tr g_f g_hi g_lo res""".split():
            s[name] = sem(name)
        w_in = [sem(f"w_in{r}") for r in range(RING)]
        w1_in = [sem(f"w1_in{b}") for b in range(2)]
        wq_in = [sem(f"wq_in{b}") for b in range(2)]

        tiles = range(KT)
        STEPS = {
            "pe": ["modulation"] + [f"square sums {k}" for k in tiles] + ["positions turned"]
                  + ["aux gate", "aux vs", "aux vw", "sum cq", "hidden k", "aux kr", "sum ckv", "aux ks", "aux kw", "aux q0",
                     "hidden v", "aux q1", "aux q2", "aux q3", "second layer", "rotate kc", "block scores", "block turned",
                     "block values", "latent values"] + [f"turned {k}" for k in tiles]
                  + [f"out sums {k}" for k in tiles] + [f"back {k}" for k in tiles],
            "act": [f"squares {k}" for k in tiles] + ["root 2", "root 1"] + [f"h high {k}" for k in tiles]
                   + ["ev kc", "ev vc", "ev gate", "ev vs", "ev vw", "gate tanh", "ev cq0", "tables", "ev cq1", "square cq0",
                      "square cq1", "ev ckv", "ev kr", "square ckv", "ev ks", "root cq", "ev kw", "root ckv", "tanh k",
                      "ev q0", "ev q1", "ev q2", "tanh v", "ev q3", "z tanh 0", "z tanh 1", "z tanh 2", "z tanh 3",
                      "z tanh 4", "z tanh 5", "block exp", "z tanh 6", "z tanh 7", "block turned", "latent values"]
                   + [f"mix high {k}" for k in tiles] + [f"out squares {k}" for k in tiles] + ["out root"]
                   + [f"out rows {k}" for k in tiles],
            "pool": ["window zero", "block zero"]
                    + [f"cos {n}" for n in ROPE] + [f"mix low {k}" for k in tiles],
            "dve": ["mod", "mod gain 1", "mod gain 2", "var 1", "var 2", "inv 2"]
                   + ["h 0"] + [f"{what} {k - d}" for k in range(1, KT) for what, d in (("h", 0), ("norm low", 1))]
                   + [f"norm low {KT - 1}", "inv 1"] + [f"x normed {k}" for k in tiles]
                   + ["bf16"] + [f"table {n}" for n in range(9)] + ["positions", "post gate", "post vs", "post vw", "window k",
                      "gates", "inv cq", "cq 0", "cq 1", "sin kr", "post kr", "window v", "inv ckv", "ckv",
                      "sin ks", "post ks", "sin kw", "post kw", "hidden k", "sin q0", "post q0", "sin q1", "post q1",
                      "sin q2", "post q2", "hidden v", "hidden v 4", "sin q3", "post q3", "z 0", "kc", "block values", "z 1",
                      "kc cos", "kc sin", "kc rotated", "z 2", "z 3", "scaled", "max", "less max", "z 4", "z 5", "sum",
                      "seen", "sum inv", "coef", "probs", "z 6", "z 7", "block out", "rotated keys"]
                   + [f"mixed {k}" for k in tiles] + [f"x {k}" for k in tiles] + ["out inv"] + [f"y {k}" for k in tiles],
        }
        assert all(len(set(v)) == len(v) for v in STEPS.values())

        def step_count(who, name):
            return STEPS[who].index(name) + 1

        def lane(who):
            count = [0]

            def done(ins, name):
                assert STEPS[who][count[0]] == name, (who, STEPS[who][count[0]], name)
                count[0] += 1
                ins.then_inc(s[who + "_steps"], 1)
            return done

        def after(eng, who, name):
            eng.wait_ge(s[who + "_steps"], step_count(who, name))

        def bc(col_ap, n):
            return col_ap.unsqueeze(2).broadcast_to([P, col_ap.shape[1], n])

        def bc_mid(block, n):
            return block.unsqueeze(1).broadcast_to([P, n, block.shape[1]])

        def known(x, v):
            return isinstance(x, int) and x == v

        w_in_T = A["dn_w_in"][0].rearrange("(k p) c -> p k c", p=P)
        w_out_T = A["dn_w_out"][0].rearrange("(k p) c -> p k c", p=P)
        w_up_T = A["mlp_w_up"][0].rearrange("(k p) c -> p k c", p=P)
        w_down_T = A["mlp_w_down"][0].rearrange("(q k p) c -> q p k c", p=P, k=KT)
        FN = 4 * D
        BA_N = BA_LEAD + 16
        Q, KK_, VV, ZZ = range(4)
        w_in2_T = A["w_in_2"][0].rearrange("(k p) c -> p k c", p=P)
        w_out2_T = A["w_out_2"][0].rearrange("(k p) c -> p k c", p=P)
        SCALE, SCALE_M = DK ** -0.5, MD ** -0.5

        def seen_by(name):
            return K2[name].rearrange("p (q n) -> p q n", n=NCP).unsqueeze(2).broadcast_to([P, CH, 4, NCP])

        def by_head(t):
            return t.rearrange("p (q h n) -> p q h n", q=CH, n=NCP)

        def windows(t, w):
            v = t.rearrange("p (n l) -> p n l", l=CMP_STRIDE)
            return v[:, w:w + NC, :].rearrange("p n l -> p l n")

        def level_halves(block, lv, odd):
            return block.rearrange("p (b o l) -> p b o l", o=2, l=lv)[:, :, odd, :]

        block = ctx.enter_context(nc.Block())

        @block.sync
        def _(sp):
            for c in range(CH):
                sp.dma_start(xn[:, c, :], A["x"][0, c * P:(c + 1) * P, :]).then_inc(s["x_in"], 16)
                if c == 0:
                    sp.dma_start(const[:, :], A["consts"]).then_inc(s["const_in"], 16)
            for name, r in VEC_ROWS.items():
                src = A[name]
                if len(src.shape) == 2:
                    src = src.rearrange("a c -> (a c)")
                sp.dma_start(rows[VEC_AT[name]:VEC_AT[name] + r, 0, :],
                             src.rearrange("(r p) -> r p", p=P)).then_inc(s["vec_in"], 16)
            for tap in range(4):
                sp.dma_start(rows[tap * 24:(tap + 1) * 24, 1, :],
                             A["dn_conv_w"][0, tap].rearrange("(r p) -> r p", p=P)).then_inc(s["vec_in"], 16)
            sp.dma_start(dtb[:, 0, :], A["dn_dt_bias"].broadcast_to([P, H])).then_inc(s["gate_in"], 16)
            sp.dma_start(dtb[:, 1, :], A["dn_a_log"].broadcast_to([P, H])).then_inc(s["gate_in"], 16)

            def load(n, slot, src, cols=P):
                if not isinstance(n, int) or n >= RING:
                    sp.wait_ge(s["w_lo"], n - RING + 1)
                sp.dma_start(stage[:, slot, :, 0:cols], src).then_inc(w_in[slot], 16)

            load(0, 0, w_in_T[:, :, 0:P])
            load(1, 1, w_in_T[:, :, D:D + P])
            load(2, 2, w_in_T[:, :, FN - BA_LEAD:FN + 16], BA_N)
            load(3, 3, w_in_T[:, :, 2 * D:2 * D + P])
            with sp.Fori(0, H - 1) as h:
                for j, (sec, ahead) in enumerate(((Q, 1), (KK_, 1), (ZZ, 0), (VV, 1))):
                    load(h * 4 + 4 + j, j, w_in_T[:, :, bass.ds((h + ahead) * P + sec * D, P)])
            load(DN_UNITS - 1, (DN_UNITS - 1) % RING, w_in_T[:, :, 3 * D + 7 * P:4 * D])
            for m in range(KT):
                load(U_OUT + m, (U_OUT + m) % RING, w_out_T[:, :, m * P:(m + 1) * P])
            sp.wait_ge(s["w_used"], U_OUT + 1)
            ada_T = A["ada_w_2"][0].rearrange("(k p) c -> p k c", p=P)

            def mod_rows(kk):
                sp.wait_ge(s["mod_done"], kk * 3 + 3)
                sp.dma_start(mod_w[:, :], ada_T[:, bass.ds(kk, 1), :].rearrange("p a c -> p (a c)"))\
                    .then_inc(s["mod_in"], 16)

            with sp.Fori(0, QUARTERS) as q:
                mod_rows(q * 2)
                for m in range(KT):
                    load(U_MLP + q * 16 + m, (U_MLP + m) % RING, w_up_T[:, :, bass.ds(q * D + m * P, P)])
                for m in range(KT):
                    load(U_MLP + q * 16 + KT + m, (U_MLP + m) % RING,
                         w_down_T[bass.ds(q, 1), :, :, m * P:(m + 1) * P].rearrange("a p k c -> p (a k) c"))
                    if m == 1:
                        mod_rows(q * 2 + 1)
            sp.wait_ge(s["w_used"], U_TWO)
            sp.dma_start(const2[:, :], A["consts2"]).then_inc(s["c2_in"], 16)
            sp.dma_start(pos_i[:, :], A["positions_2"].broadcast_to([P, T])).then_inc(s["pos_in"], 16)
            for half in range(2):
                sp.dma_start(cpos[0:CMP_BLOCK, half * DK:(half + 1) * DK], A["cmp_pos_2"][0]).then_inc(s["cpos_in"], 16)
            for n, name in enumerate(("k", "k", "v")):
                sp.dma_start(w2c[:, n], A[f"cmp_{name}_w2_2"][0]).then_inc(s["w2_in"], 16)
            first_col = {"kc": AT_KC, "vc": AT_VC, "gate": AT_GATE, "vs": AT_VS, "vw": AT_VW, "cq0": AT_CQ, "cq1": AT_CQ + P,
                         "ckv": AT_CKV, "kr": AT_KR - MN, "ks": AT_KS, "kw": AT_KW}
            for a, name in enumerate(TWO):
                n = U_TWO + a
                if name[0] == "q":
                    m = int(name[1])
                    sp.wait_ge(s["w_lo"], n - RING + 1)
                    for half in range(2):
                        c = m * DK + half * 4 * DK
                        sp.dma_start(stage[:, n % RING, :, half * DK:(half + 1) * DK], w_in2_T[:, :, c:c + DK])\
                            .then_inc(w_in[n % RING], 16)
                else:
                    c = first_col[name]
                    load(n, n % RING, w_in2_T[:, :, c:c + P])
                if a == 4:
                    after(sp, "dve", f"x normed {KT - 1}")
                    for w, name1 in enumerate(("k", "v")):
                        for half in range(2):
                            sp.dma_start(w1[w][half * DK:(half + 1) * DK],
                                         A[f"cmp_{name1}_w1_2"][0].rearrange("(l d) h -> d l h", d=DK)).then_inc(w1_in[w], 16)
            for m in range(KT):
                c = AT_Z + m * P if m < 4 else AT_ZM + (m - 4) * P
                load(U_Z + m, (U_Z + m) % RING, w_in2_T[:, :, c:c + P])
            for m in range(RING):
                load(U_OUT2 + m, (U_OUT2 + m) % RING, w_out2_T[:, :, m * P:(m + 1) * P])
            after(sp, "dve", "block out")
            kv_up = A["w_kv_up_2"][0].rearrange("r (h c) -> r h c", c=MN + DK)
            q_up = A["w_q_up_2"][0].rearrange("(k p) (h c) -> h p k c", p=P, c=MD)
            k_up = A["w_kv_up_2"][0].rearrange("r (h c) -> h r c", c=MN + DK)
            sp.dma_start(wv[:, :, :], kv_up[:, :, MN:]).then_inc(s["wv_in"], 16)

            def latent_weights(h, par, wait=True):
                if wait:
                    sp.wait_ge(s["p_ps"], h - 1)
                sp.dma_start(wq[:, par], q_up[bass.ds(h, 1)].rearrange("h p k c -> p (h k) c")).then_inc(wq_in[par], 16)
                sp.dma_start(wk[:, par], k_up[bass.ds(h, 1), :, 0:MN].rearrange("h r c -> r (h c)")).then_inc(wq_in[par], 16)

            latent_weights(0, 0, False)
            latent_weights(1, 1, False)
            with sp.Fori(1, QH // 2) as j:
                latent_weights(j * 2, 0)
                latent_weights(j * 2 + 1, 1)
            for m in range(RING, KT):
                load(U_OUT2 + m, (U_OUT2 + m) % RING, w_out2_T[:, :, m * P:(m + 1) * P])
            for half in range(2):
                after(sp, "act", f"out rows {half * 4 + 3}")
                for c in range(CH):
                    sp.dma_start(out[c * P:(c + 1) * P, half * 512:(half + 1) * 512],
                                 y[:, c, half * 512:(half + 1) * 512]).then_inc(s["out_done"], 16)
            sp.wait_ge(s["out_done"], 16 * 2 * CH)

        @block.scalar
        def _(act):
            def split_hi(n, slot, cols=P):
                halves = 16 if isinstance(n, int) and n >= U_TWO + TWO.index("q0") else 0
                act.wait_ge(w_in[slot], (n - slot) * (16 // RING) + 16 + halves)
                if not isinstance(n, int) or n >= RING:
                    act.wait_ge(s["w_used"], n - RING + 1)
                act.activation(whi[:, slot, :, 0:cols], stage[:, slot, :, 0:cols], ACT.Copy).then_inc(s["w_hi"], 1)

            def norm_squares(m, k):
                if m * KT + k >= 2:
                    act.wait_ge(s["n_stat"], m * KT + k - 1)
                act.activation(sqn[:, k % 2], xT[:, k], ACT.Square).then_inc(s["n_sq"], 1)

            def norm_rest(m):
                act.wait_ge(s["n_stat"], (m + 1) * KT)
                act.activation(rs[:, :], ps[:, 2, :], ACT.Sqrt, bias=K["eps"][:, 0:1]).then_inc(s["n_sqrt"], 1)

            def norm_hi(m):
                for k in range(KT):
                    act.wait_ge(s["n_h"], m * KT + k + 1)
                    act.activation(hhi[:, k], hf[:, k % 2], ACT.Copy).then_inc(s["n_hi"], 1)

            act.wait_ge(s["const_in"], 16)
            for k in range(KT):
                act.wait_ge(s["xtr"], k + 1)
                act.activation(xT[:, k], ps[:, 3 + k % 4, :], ACT.Copy).then_inc(s["xev"], 1)
                act.wait_ge(s["xev"], k + 1)
                norm_squares(0, k)
            norm_rest(0)
            split_hi(0, 0)
            split_hi(1, 1)
            split_hi(2, 2, BA_N)
            norm_hi(0)
            split_hi(3, 3)

            def tap0(h, seq):
                u = h * 3 + seq
                act.wait_ge(s["w_used"], h * 4 + (0, 1, 3)[seq] + 1)
                if not known(u, 0):
                    act.wait_ge(s["seq_ready"], u)
                act.activation(acc[:, :], ps[:, (0, 1, 1)[seq], :], ACT.Copy,
                               scale=convw[:, 9 + seq, bass.ds(h, 1)]).then_inc(s["conv0"], 1)

            def seq_tanh(h, seq):
                act.wait_ge(s["conv1"], (h * 3 + seq) * 3 + 3)
                act.activation(th[:, :], acc[:, :], ACT.Tanh, scale=0.5).then_inc(s["tanh"], 1)

            def squares(h, w, src):
                act.wait_ge(s["seq_ready"], h * 3 + w + 1)
                if not known(h, 0):
                    act.wait_ge(s["ss_ps"], h)
                act.activation(sq[:, w], src[:, :], ACT.Square).then_inc(s["sqs"], 1)

            act.wait_ge(s["vec_col"], 2)
            tap0(0, 0)
            seq_tanh(0, 0)
            squares(0, 0, qT[0])
            split_hi(4, 0)
            tap0(0, 1)
            seq_tanh(0, 1)
            squares(0, 1, kT[0])
            split_hi(5, 1)
            act.wait_ge(s["gate_in"], 32)
            act.activation(dtb[:, 1, :], dtb[:, 1, :], ACT.Exp).then_inc(s["gate_act"], 1)
            act.wait_ge(s["ba_col"], 1)
            act.activation(gtmp[:, 0], batok[:, :, 0:H], ACT.Tanh, scale=0.5).then_inc(s["gate_act"], 1)
            act.wait_ge(s["gate_dve"], 2)
            act.activation(gtmp[:, 2], gtmp[:, 2], ACT.Exp, scale=-1.0).then_inc(s["gate_act"], 1)
            act.wait_ge(s["gate_act"], 3)
            act.activation(gtmp[:, 2], gtmp[:, 2], ACT.Ln, bias=1.0).then_inc(s["gate_act"], 1)
            act.wait_ge(s["gate_ps"], 1)
            for n in range(3):
                act.activation(gates[:, :, 1 + n, :].rearrange("p h c -> p c h"),
                               ps[:, 4, 32 * n:32 * n + 32].rearrange("p (c h) -> p c h", h=H),
                               ACT.Exp).then_inc(s["gate_ready"], 1)
            act.activation(cact[:, :], V["c_2"], ACT.Tanh, scale=0.5).then_inc(s["mod_c"], 1)
            split_hi(6, 2)

            def decays(h, w):
                act.wait_ge(s["dps"], h * 2 + w + 1)
                if not known(h, 0):
                    act.wait_ge(s["attn_ready"], h) if w else act.wait_ge(s["low_ready"], h * 4)
                act.activation((dec, decT)[w][:, :, :], ps[:, 4 + w, :].rearrange("p (c i) -> p c i", c=CH), ACT.Exp)\
                    .then_inc(s["dexp"], 1)

            def norm_roots(h, col):
                act.wait_ge(s["norm_dve"], h * 5 + 2)
                act.activation(col[:, 2:4, :], col[:, 0:2, :], ACT.Sqrt).then_inc(s["norm_act"], 1)

            def out_root(h, col):
                act.wait_ge(s["o_stat"], h * 5 + 3)
                act.activation(col[:, 9, :], col[:, 8, :], ACT.Sqrt, scale=float(P) ** -2, bias=K["eps"][:, 0:1])\
                    .then_inc(s["o_act"], 1)

            def out_hi(h):
                act.wait_ge(s["g_f"], h + 1)
                act.activation(ahi[0][:, bass.ds(h, 1), :], gf[:, :].unsqueeze(1), ACT.Copy).then_inc(s["g_hi"], 1)

            def level(h, li):
                if known(h, 0):
                    act.wait_ge(s["q_zero"], NL - 1)
                act.wait_ge(s["q_ps"], h * 6 + li)
                lv = LEVELS[li]
                act.activation(qlev[lv][:, :, :].rearrange("p c (b o l) -> p (c b) o l", o=2, l=lv)[:, :, 1, :],
                               ps[:, 4, 0:CH * 64].rearrange("p (b l) -> p b l", l=lv), ACT.Copy)\
                    .then_inc(s["q_ev"], 1)

            def head(h, par, last):
                first = known(h, 0)
                level(h, 1)
                if not first:
                    out_root(h - 1, cols[1 - par])
                norm_roots(h, cols[par])
                level(h, 2)
                if not first:
                    out_hi(h - 1)
                level(h, 3)
                tap0(h, 2)
                level(h, 4)
                seq_tanh(h, 2)
                split_hi(h * 4 + 7, 3)
                level(h, 5)
                if not last:
                    tap0(h + 1, 0)
                level(h, 6)
                if not last:
                    seq_tanh(h + 1, 0)
                act.wait_ge(s["w_ps"], h + 1)
                act.activation(wT[:, :, :], ps[:, 5, :].rearrange("p (c i) -> p c i", c=CH), ACT.Copy, scale=-1.0)\
                    .then_inc(s["w_ev"], 1)
                for c in range(CH):
                    act.wait_ge(s["v_ps"], h * 4 + c + 1)
                    act.activation(vnew[:, c, :], ps[:, 3, 0:P], ACT.Copy).then_inc(s["v_ev"], 1)
                    if c:
                        act.wait_ge(s["o1_ps"], h * 3 + c)
                        if c > 1:
                            act.wait_ge(s["o_ready"], h * 4 + c)
                        act.activation(o1[:, :], ps[:, 3, P:2 * P], ACT.Copy,
                                       scale=gates[:, bass.ds(h, 1), 1, c]).then_inc(s["o1_ev"], 1)
                    if last:
                        continue
                    if c == 0:
                        tap0(h + 1, 1)
                        split_hi(h * 4 + 8, 0)
                        squares(h + 1, 0, qT[1 - par])
                    if c == 1:
                        decays(h + 1, 0)
                        seq_tanh(h + 1, 1)
                        decays(h + 1, 1)
                    if c == 2:
                        squares(h + 1, 1, kT[1 - par])
                        split_hi(h * 4 + 9, 1)
                zn = DN_UNITS - 1 if last else h * 4 + 6
                act.wait_ge(s["w_used"], zn + 1)
                act.activation(th[:, :], ps[:, 0, :], ACT.Tanh, scale=0.5).then_inc(s["ztanh"], 1)
                if last:
                    split_hi(DN_UNITS + 3, (DN_UNITS + 3) % RING)
                else:
                    split_hi(h * 4 + 10, 2)

            decays(0, 0)
            decays(0, 1)
            head(0, 0, False)
            with act.Fori(0, H // 2 - 1) as j:
                head(j * 2 + 1, 1, False)
                head(j * 2 + 2, 0, False)
            head(H - 1, 1, True)
            out_root(H - 1, cols[1])
            out_hi(H - 1)

            def next_hi(n, slot):
                split_hi(n + RING, slot)

            def squares1(m, k):
                act.wait_ge(s["res"], k + 1)
                if k >= 2:
                    act.wait_ge(s["n_stat"], m * KT + k - 1)
                act.activation(nsq[:, k % 2], xT[:, k], ACT.Square).then_inc(s["n_sq"], 1)

            for m in range(KT):
                next_hi(U_OUT + m, (U_OUT + m) % RING)
                squares1(1, m)
            act.wait_ge(s["n_stat"], 2 * KT)
            act.activation(rs1[:, :], ps[:, 2, :], ACT.Sqrt, bias=K["eps"][:, 0:1]).then_inc(s["n_sqrt"], 1)
            for k in range(KT):
                act.wait_ge(s["n_h"], KT + k + 1)
                act.activation(hhi[:, k], hf1[:, k % 2], ACT.Copy).then_inc(s["n_hi"], 1)

            def quarter(q, par):
                n0 = U_MLP + q * 16

                def hidden_hi(m):
                    act.wait_ge(s["mlp_f"], q * KT + m + 1)
                    act.activation(ahi[par][:, m], af[:, m % 2], ACT.Copy).then_inc(s["mlp_hi"], 1)

                for m in range(KT):
                    act.wait_ge(s["w_used"], n0 + m + 1)
                    if m >= 2:
                        act.wait_ge(s["mlp_f"], q * KT + m - 1)
                    act.activation(relu[:, m % 2], ps[:, (U_MLP + m) % 2, :], ACT.Relu).then_inc(s["mlp_relu"], 1)
                    next_hi(n0 + m, (U_MLP + m) % RING)
                    hidden_hi(m)
                for m in range(KT):
                    next_hi(n0 + KT + m, (U_MLP + m) % RING)

            with act.Fori(0, QUARTERS // 2) as j:
                quarter(j * 2, 0)
                quarter(j * 2 + 1, 1)

            done = lane("act")
            for k in range(KT):
                act.wait_ge(s["res"], QUARTERS * KT + k + 1)
                if k >= 2:
                    after(act, "pe", f"square sums {k - 2}")
                if k == 0:
                    act.wait_ge(s["mlp_f"], QUARTERS * KT)
                act.activation(nsq[:, k % 2], xT[:, k], ACT.Square)
                done(act.activation(relu[:, k % 2], xT[:, k], ACT.Square, scale=V["norm_final"][:, k:k + 1]), f"squares {k}")
            after(act, "dve", "var 2")
            done(act.activation(hf1[:, 1], hf1[:, 0], ACT.Sqrt), "root 2")
            done(act.activation(rs1[:, :], ps[:, 2, :], ACT.Sqrt, bias=K["eps"][:, 0:1]), "root 1")
            for k in range(KT):
                after(act, "dve", f"h {k}")
                done(act.activation(hhi[:, k], relu[:, k % 2], ACT.Identity, bias=mod[:, k:k + 1]), f"h high {k}")
            raw_of = {n: x % 3 for x, n in enumerate(AUX)}
            for a, name in enumerate(TWO):
                act.wait_ge(s["w_used"], U_TWO + a + 1)
                src = ps[:, (U_TWO + a) % 2, :]
                if name in ("kc", "vc"):
                    dst = (kcT, vcT)[a][:, :]
                elif name[0] == "c":
                    dst = cn[:, a - TWO.index("cq0")]
                else:
                    x = AUX.index(name)
                    if x >= 3:
                        after(act, "dve", f"post {AUX[x - 3]}")
                    dst = raw[:, x % 3]
                done(act.activation(dst, src, ACT.Copy), f"ev {name}")
                split_hi(U_TWO + a + RING, (U_TWO + a) % RING)
                if name == "vw":
                    after(act, "dve", "post gate")
                    done(act.activation(gate2[:, :, :], gate2[:, :, :], ACT.Tanh, scale=0.5), "gate tanh")
                if name == "cq0":
                    after(act, "dve", "table 8")
                    done(act.activation(table[:, :, :], table[:, :, :], ACT.Sin), "tables")
                if name == "cq1":
                    after(act, "act", "ev cq1")
                    for w in range(2):
                        done(act.activation(csq[:, w], cn[:, w], ACT.Square), f"square cq{w}")
                if name == "kr":
                    after(act, "pe", "sum cq")
                    after(act, "act", "ev ckv")
                    done(act.activation(csq[:, 0], cn[:, 2], ACT.Square), "square ckv")
                if name == "ks":
                    done(act.activation(rcos[:, 0], ps[:, 6, :], ACT.Sqrt, scale=4.0, bias=K["eps"][:, 0:1]), "root cq")
                if name == "kw":
                    after(act, "pe", "sum ckv")
                    done(act.activation(csq[:, 1], ps[:, 7, :], ACT.Sqrt, scale=8.0, bias=K["eps"][:, 0:1]), "root ckv")
                    after(act, "pe", "hidden k")
                    done(act.activation(hid[:, 0, 0], ps[:, 4, 0:2 * NCP].rearrange("p (g n) -> p g n", g=2),
                                        ACT.Tanh, scale=0.5), "tanh k")
                if name == "q2":
                    after(act, "pe", "hidden v")
                    done(act.activation(hid[:, 1, 0], ps[:, 5, 0:2 * NCP].rearrange("p (g n) -> p g n", g=2),
                                        ACT.Tanh, scale=0.5), "tanh v")

            def z_tanh(m):
                act.wait_ge(s["w_used"], U_Z + m + 1)
                if m >= 2:
                    after(act, "dve", f"z {m - 2}")
                else:
                    after(act, "pe", "hidden v")
                done(act.activation(prob[:, m % 2], ps[:, m % 2, :], ACT.Tanh, scale=0.5), f"z tanh {m}")
                if m < RING:
                    split_hi(U_Z + m + RING, (U_Z + m) % RING)
                else:
                    split_hi(U_Z + m + RING, (U_Z + m) % RING)

            for m in range(6):
                z_tanh(m)
            after(act, "dve", "less max")
            done(act.activation(csc[:, :, :], csc[:, :, :], ACT.Exp), "block exp")
            z_tanh(6)
            z_tanh(7)
            after(act, "pe", "block turned")
            done(act.activation(cpT[:, :, :], ps[:, 6:8, :], ACT.Copy), "block turned")

            def soft(i, n, exp_scale, keys):
                act.wait_ge(s["at_neg"], n + 1)
                if i >= 2:
                    act.wait_ge(s["at_t"], n - 1)
                    act.wait_ge(s["at_inv"], n - 1)
                act.activation(prob[:, i % 2, 0:keys], ps[:, i % 4, 0:keys], ACT.Exp, scale=exp_scale,
                               bias=aneg[:, i % 2:i % 2 + 1], accum_out=asum[:, i % 2:i % 2 + 1]).then_inc(s["at_exp"], 1)

            def turned(i, n, keys):
                act.wait_ge(s["at_t"], n + 1)
                if i >= 2:
                    act.wait_ge(s["at_o"], n - 1)
                act.activation(probT[:, i % 2, 0:keys], ps[:, 4 + i % 2, 0:keys], ACT.Copy).then_inc(s["at_tev"], 1)

            def attend(first, count, exp_scale):
                for i in range(count + 2):
                    if i < count:
                        soft(i, first + i, exp_scale, (i % 4 + 1) * P)
                    if i >= 2:
                        turned(i - 2, first + i - 2, ((i - 2) % 4 + 1) * P)

            with act.Fori(0, 4) as j:
                act.wait_ge(s["at_done"], j * 16 + 1)
                act.activation(qh[:, :].unsqueeze(1), q2T[:, bass.ds(j, 1), :], ACT.Copy).then_inc(s["q_staged"], 1)
                attend(j * 16, 16, SCALE)
            after(act, "pe", "latent values")
            done(act.activation(v_mla[:, :, :], ps[:, 0:4, :], ACT.Copy), "latent values")
            with act.Fori(0, QH // 2) as j:
                for par in range(2):
                    act.wait_ge(s["p_ps"], j * 2 + par + 1)
                    act.activation(qraw[0:MD, par], ps[0:MD, par, :], ACT.Copy)
                    act.activation(km[0:MN, par], ps[0:MN, 2 + par, :], ACT.Copy).then_inc(s["p_ev"], 1)
                attend(j * 8 + 64, 8, SCALE_M)
            for k in range(KT):
                after(act, "dve", f"mixed {k}")
                done(act.activation(hhi[:, k], gated[:, k % 2], ACT.Copy), f"mix high {k}")
            for m in range(KT):
                if m < KT - RING:
                    split_hi(U_OUT2 + m + RING, (U_OUT2 + m) % RING)
                after(act, "dve", f"x {m}")
                if m >= 2:
                    after(act, "pe", f"out sums {m - 2}")
                done(act.activation(osqr[:, m % 2], xT[:, m], ACT.Square), f"out squares {m}")
            after(act, "pe", f"out sums {KT - 1}")
            done(act.activation(ors[:, :], ps[:, 2, :], ACT.Sqrt, bias=K["eps"][:, 0:1]), "out root")
            for k in range(KT):
                after(act, "pe", f"back {k}")
                done(act.activation(y[:, :, k * P:(k + 1) * P], ps[:, 4 + k % 2, :].rearrange("p (c i) -> p c i", c=CH),
                                    ACT.Copy), f"out rows {k}")

        @block.gpsimd
        def _(pool):
            def split_lo(n, slot, cols=P):
                pool.wait_ge(s["w_hi"], n + 1)
                pool.tensor_tensor(wlo[:, slot, :, 0:cols], stage[:, slot, :, 0:cols], whi[:, slot, :, 0:cols],
                                   ALU.subtract).then_inc(s["w_lo"], 1)

            split_lo(0, 0)
            split_lo(1, 1)
            split_lo(2, 2, BA_N)
            for k in range(KT):
                pool.wait_ge(s["n_hi"], k + 1)
                pool.tensor_tensor(hlo[:, k], hf[:, k % 2], hhi[:, k], ALU.subtract).then_inc(s["n_lo"], 1)
            for lv in LEVELS[1:]:
                if lv == 2:
                    pool.wait_ge(s["n_stat"], KT)
                pool.memset(qlev[lv][:, :, :], 0.0).then_inc(s["q_zero"], 1)
            split_lo(3, 3)
            for n in range(4, 7):
                split_lo(n, n % RING)

            def decay_sums(h, w):
                if w == 0:
                    pool.wait_ge(s["g_col"], h + 1)
                else:
                    pool.wait_ge(s["dps"], h * 2 + w)
                pool.tensor_tensor(gd[:, :, :], bc_mid(K[("after", "upto")[w]], CH), bc(gcol[:, :], P), ALU.mult)\
                    .then_inc(s["dz_in"], 1)

            def decay_mask(h):
                pool.wait_ge(s["dexp"], h * 2 + 2)
                pool.tensor_tensor(decT[:, :, :], decT[:, :, :], bc_mid(K["upto"], CH), ALU.mult)\
                    .then_inc(s["dmask"], 1)

            def level(h, li):
                if li == 0:
                    pool.wait_ge(s["low_ready"], h * 4 + 4)
                if li == NB:
                    pool.wait_ge(s["inv_ready"], h * 13 + 2)
                elif li > NB:
                    pool.wait_ge(s["q_ps"], h * 6 + li - NB)
                elif not known(h, 0):
                    pool.wait_ge(s["q_ps"], h * 6)
                pool.tensor_tensor(lev[:, li % NB], low[:, :, :], bc_mid(K[f"level{LEVELS[li]}"], CH), ALU.mult)\
                    .then_inc(s["lev_ready"], 1)

            def head(h, par, last):
                for li in range(6):
                    level(h, li)
                split_lo(h * 4 + 7, 3)
                level(h, 6)
                if not last:
                    decay_sums(h + 1, 0)
                    split_lo(h * 4 + 8, 0)
                    decay_sums(h + 1, 1)
                    decay_mask(h + 1)
                    split_lo(h * 4 + 9, 1)
                    split_lo(h * 4 + 10, 2)
                else:
                    split_lo(DN_UNITS + 3, (DN_UNITS + 3) % RING)

            decay_sums(0, 0)
            decay_sums(0, 1)
            decay_mask(0)
            head(0, 0, False)
            with pool.Fori(0, H // 2 - 1) as j:
                head(j * 2 + 1, 1, False)
                head(j * 2 + 2, 0, False)
            head(H - 1, 1, True)
            for m in range(KT):
                split_lo(U_OUT + RING + m, (U_OUT + m) % RING)
            for k in range(KT):
                pool.wait_ge(s["n_hi"], KT + k + 1)
                pool.tensor_tensor(hlo[:, k], hf1[:, k % 2], hhi[:, k], ALU.subtract).then_inc(s["n_lo"], 1)

            def quarter(q, par):
                n0 = U_MLP + q * 16
                for m in range(KT):
                    split_lo(n0 + RING + m, (U_MLP + m) % RING)
                    pool.wait_ge(s["mlp_hi"], q * KT + m + 1)
                    pool.tensor_tensor(alo[par][:, m], af[:, m % 2], ahi[par][:, m], ALU.subtract)\
                        .then_inc(s["mlp_lo"], 1)
                for m in range(KT):
                    split_lo(n0 + KT + RING + m, (U_MLP + m) % RING)

            with pool.Fori(0, QUARTERS // 2) as j:
                quarter(j * 2, 0)
                quarter(j * 2 + 1, 1)

            done = lane("pool")
            for a, name in enumerate(TWO):
                split_lo(U_TWO + a + RING, (U_TWO + a) % RING)
                if a == 0:
                    after(pool, "dve", f"x normed {KT - 1}")
                    done(pool.memset(xb[:, :, :, :], 0.0), "window zero")
                    pool.memset(kcr[:, :, :], 0.0)
                    done(pool.memset(vbd[:, :, :, :], 0.0), "block zero")
                if name in ROPE:
                    r = ROPE.index(name)
                    after(pool, "act", f"ev {name}")
                    if r == 0:
                        after(pool, "act", "tables")
                    if r >= 2:
                        after(pool, "dve", f"post {ROPE[r - 2]}")
                    if r == 0:
                        after(pool, "dve", "cq 1")
                    done(pool.tensor_tensor(rcos[:, r % 2], raw[:, AUX.index(name) % 3],
                                            table[:, 3 if name == "kr" else 1], ALU.mult), f"cos {name}")
            for m in range(KT):
                split_lo(U_Z + m + RING, (U_Z + m) % RING)
            with pool.Fori(0, QH // 2) as j:
                for par in range(2):
                    pool.wait_ge(s["p_ev"], j * 2 + par + 1)
                    if par:
                        pool.wait_ge(s["p_q"], j * 2 + 1)
                    pool.tensor_tensor(qcos[0:MD, :], qraw[0:MD, par], table[0:MD, 3], ALU.mult).then_inc(s["p_cos"], 1)
                    pool.wait_ge(s["p_cos"], j * 2 + par + 1)
            for k in range(KT):
                after(pool, "act", f"mix high {k}")
                done(pool.tensor_tensor(hlo[:, k], gated[:, k % 2], hhi[:, k], ALU.subtract), f"mix low {k}")
            for m in range(KT - RING):
                split_lo(U_OUT2 + m + RING, (U_OUT2 + m) % RING)

        @block.vector
        def _(dve):
            dve.wait_ge(s["vec_tr"], 1)
            dve.tensor_copy(vec[:, :], ps[:, 7, 0:NVEC]).then_inc(s["vec_col"], 1)
            dve.tensor_copy(convw[:, :, :], ps[:, 7, P:P + 96].rearrange("p (a h) -> p a h", h=H))\
                .then_inc(s["vec_col"], 1)
            dve.wait_ge(s["vec_col"], 2)
            dve.tensor_scalar(V["dn_norm_w"], V["dn_norm_w"], 0.5, None, ALU.mult).then_inc(s["half_ready"], 1)

            def norm(m, gain):
                dve.wait_ge(s["n_sqrt"], m + 1)
                dve.reciprocal(rr[:, :], rs[:, :]).then_inc(s["n_rstd"], 1)
                dve.wait_ge(s["n_rstd"], m + 1)
                for k in range(KT):
                    if m * KT + k >= 2:
                        dve.wait_ge(s["n_lo"], m * KT + k - 1)
                    dve.scalar_tensor_tensor(out=hf[:, k % 2], in0=xT[:, k], scalar=gain[:, k:k + 1], in1=rr[:, :],
                                             op0=ALU.mult, op1=ALU.mult).then_inc(s["n_h"], 1)

            norm(0, V["norm_mix"])

            def tap(h, seq, t):
                u = h * 3 + seq
                dve.wait_ge(s["conv0"], u + 1) if t == 1 else dve.wait_ge(s["conv1"], u * 3 + t - 1)
                dve.scalar_tensor_tensor(out=acc[:, t:T], in0=ps[:, (0, 1, 1)[seq], 0:T - t],
                                         scalar=convw[:, (3 - t) * 3 + seq, bass.ds(h, 1)], in1=acc[:, t:T],
                                         op0=ALU.mult, op1=ALU.add).then_inc(s["conv1"], 1)

            def silu2(h, seq, dst):
                dve.wait_ge(s["tanh"], h * 3 + seq + 1)
                dve.scalar_tensor_tensor(out=dst[:, :], in0=th[:, :], scalar=1.0, in1=acc[:, :],
                                         op0=ALU.add, op1=ALU.mult).then_inc(s["seq_ready"], 1)

            for seq, dst in ((0, qT[0]), (1, kT[0])):
                for t in range(1, 4):
                    tap(0, seq, t)
                silu2(0, seq, dst)
            dve.wait_ge(s["w_used"], 3)
            dve.tensor_copy(ba[BA_LEAD:BA_N, :], ps[BA_LEAD:BA_N, 0, :]).then_inc(s["ba_ev"], 1)
            dve.wait_ge(s["ba_tr"], 1)
            dve.tensor_copy(batok[:, :, :], ps[:, 5, 0:CH * 16].rearrange("p (c n) -> p c n", c=CH))\
                .then_inc(s["ba_col"], 1)
            dve.wait_ge(s["ba_col"], 1)
            dve.wait_ge(s["gate_in"], 32)
            dve.tensor_tensor(gtmp[:, 1], batok[:, :, H:2 * H], bc_mid(dtb[:, 0, :], CH), ALU.add)\
                .then_inc(s["gate_dve"], 1)
            dve.wait_ge(s["gate_dve"], 1)
            dve.scalar_tensor_tensor(out=gtmp[:, 2], in0=gtmp[:, 1], scalar=-1.0, in1=gtmp[:, 1],
                                     op0=ALU.mult, op1=ALU.max).then_inc(s["gate_dve"], 1)
            dve.wait_ge(s["gate_act"], 4)
            dve.scalar_tensor_tensor(out=gtmp[:, 3], in0=gtmp[:, 1], scalar=0.0, in1=gtmp[:, 2],
                                     op0=ALU.max, op1=ALU.add).then_inc(s["gate_dve"], 1)
            dve.wait_ge(s["gate_dve"], 3)
            dve.scalar_tensor_tensor(out=glog[:, :, :], in0=gtmp[:, 3], scalar=-1.0, in1=bc_mid(dtb[:, 1, :], CH),
                                     op0=ALU.mult, op1=ALU.mult).then_inc(s["gate_dve"], 1)
            dve.tensor_scalar(gates[:, :, 0, :].rearrange("p h c -> p c h"), gtmp[:, 0], 0.5, 0.5,
                              ALU.mult, ALU.add).then_inc(s["gate_ready"], 1)
            dve.wait_ge(s["gate_ready"], 4)

            def gate(h, n):
                return gates[:, bass.ds(h, 1), n, :].rearrange("p a c -> p (a c)")

            def norms(h, col):
                dve.wait_ge(s["ss_ps"], h + 1)
                dve.tensor_scalar(col[:, 0:2, :], ps[:, 4, 0:8].rearrange("p (w c) -> p w c", w=2), 4 * EPS, None,
                                  ALU.add).then_inc(s["norm_dve"], 1)
                dve.wait_ge(s["norm_dve"], h * 5 + 1)
                dve.reciprocal(col[:, 0:2, :], col[:, 0:2, :]).then_inc(s["norm_dve"], 1)
                dve.wait_ge(s["norm_dve"], h * 5 + 2)
                dve.tensor_tensor(col[:, 4, :], gate(h, 0), col[:, 1, :], ALU.mult).then_inc(s["norm_dve"], 1)
                dve.wait_ge(s["norm_dve"], h * 5 + 3)
                dve.tensor_tensor(col[:, 5, :], col[:, 4, :], gate(h, 1), ALU.mult).then_inc(s["norm_dve"], 1)

            def lower(h, col):
                dve.wait_ge(s["kk_ps"], h * 2 + 1)
                dve.wait_ge(s["dexp"], h * 2 + 1)
                if not known(h, 0):
                    dve.wait_ge(s["lev_ready"], h * 7)
                for c in range(CH):
                    dve.scalar_tensor_tensor(out=low[:, c, :], in0=ps[:, 6, c * P:(c + 1) * P],
                                             scalar=col[:, 4, c:c + 1], in1=dec[:, c, :],
                                             op0=ALU.mult, op1=ALU.mult).then_inc(s["low_ready"], 1)

            def level(h, li, invT):
                lv = LEVELS[li]
                dve.wait_ge(s["r_ps"], h * 6 + li)
                r = ps[:, 6, :].rearrange("p (w b l) -> p w b l", w=2, l=lv)
                odd = invT[:, :, :].rearrange("p c (b o l) -> p (c b) o l", o=2, l=lv)[:, :, 1, :]
                even = inv[:, :, :].rearrange("p c (b o l) -> p (c b) o l", o=2, l=lv)[:, :, 0, :]
                dve.tensor_tensor(odd, odd, r[:, 0], ALU.subtract).then_inc(s["inv_ready"], 1)
                if li < NL - 1:
                    dve.tensor_tensor(even, even, r[:, 1], ALU.subtract).then_inc(s["inv_ready"], 1)

            def out_stats(h, col):
                dve.wait_ge(s["o_ready"], h * 4 + 4)
                if not known(h, 0):
                    dve.wait_ge(s["o_tr"], h)
                dve.tensor_tensor(osq[:, :, :], onat[:, :, :], onat[:, :, :], ALU.mult).then_inc(s["o_stat"], 1)
                dve.wait_ge(s["o_stat"], h * 5 + 1)
                dve.tensor_reduce(col[:, 7, :], osq[:, :, :], AX.X, ALU.add).then_inc(s["o_stat"], 1)
                dve.wait_ge(s["o_stat"], h * 5 + 2)
                dve.tensor_tensor(col[:, 8, :], col[:, 7, :], col[:, 0, :], ALU.mult).then_inc(s["o_stat"], 1)

            def out_scale(h, col):
                dve.wait_ge(s["o_act"], h + 1)
                dve.reciprocal(col[:, 10, :], col[:, 9, :]).then_inc(s["o_stat"], 1)
                dve.wait_ge(s["o_stat"], h * 5 + 4)
                dve.scalar_tensor_tensor(out=col[:, 11, :], in0=col[:, 10, :], scalar=float(P) ** -0.5, in1=col[:, 2, :],
                                         op0=ALU.mult, op1=ALU.mult).then_inc(s["o_stat"], 1)
                dve.wait_ge(s["o_stat"], h * 5 + 5)
                dve.tensor_tensor(osq[:, :, :], onat[:, :, :], bc(col[:, 11, :], P), ALU.mult).then_inc(s["o_scaled"], 1)

            def out_gate(h):
                dve.wait_ge(s["o_tr"], h + 1)
                dve.wait_ge(s["z_ready"], h + 1)
                if not known(h, 0):
                    dve.wait_ge(s["g_hi"], h)
                dve.scalar_tensor_tensor(out=gf[:, :], in0=ps[:, 3, :], scalar=V["dn_norm_w"], in1=zs[:, :],
                                         op0=ALU.mult, op1=ALU.mult).then_inc(s["g_f"], 1)

            def out_lo(h):
                dve.wait_ge(s["g_hi"], h + 1)
                dve.tensor_tensor(alo[0][:, bass.ds(h, 1), :], gf[:, :].unsqueeze(1), ahi[0][:, bass.ds(h, 1), :],
                                  ALU.subtract).then_inc(s["g_lo"], 1)

            def decay_col(h):
                if not known(h, 0):
                    dve.wait_ge(s["dz_in"], h * 2)
                dve.tensor_copy(gcol[:, :], glog[:, :, bass.ds(h, 1)].rearrange("p c a -> p (c a)"))\
                    .then_inc(s["g_col"], 1)

            def head(h, par, last):
                first = known(h, 0)
                col, invT = cols[par], invTs[par]
                dve.wait_ge(s["lev_ready"], h * 7 + 1)
                dve.tensor_tensor(inv[:, :, :], bc_mid(K["ident"], CH), lev[:, 0], ALU.subtract)\
                    .then_inc(s["inv_ready"], 1)
                dve.wait_ge(s["inv_ps"], h + 1)
                dve.tensor_tensor(invT[:, :, :], bc_mid(K["ident"], CH),
                                  ps[:, 4, :].rearrange("p (c i) -> p c i", c=CH), ALU.subtract)\
                    .then_inc(s["inv_ready"], 1)
                if not first:
                    out_stats(h - 1, cols[1 - par])
                dve.wait_ge(s["kk_ps"], h * 2 + 2)
                dve.wait_ge(s["dmask"], h + 1)
                dve.tensor_tensor(attnT[:, :, :], ps[:, 5, :].rearrange("p (c i) -> p c i", c=CH), decT[:, :, :],
                                  ALU.mult).then_inc(s["attn_ready"], 1)
                level(h, 1, invT)
                dve.wait_ge(s["kn_ps"], h + 1)
                kn = ps[:, 2, :].rearrange("p (c i) -> p c i", c=CH)
                dve.tensor_tensor(kbeta[:, :, :], kn, bc(col[:, 5, :], P), ALU.mult).then_inc(s["kside"], 1)
                dve.tensor_tensor(kdec[:, :, :], kn, bc(gate(h, 2), P), ALU.mult).then_inc(s["kside"], 1)
                if not first:
                    out_scale(h - 1, cols[1 - par])
                level(h, 2, invT)
                if not first:
                    out_gate(h - 1)
                level(h, 3, invT)
                if not last:
                    decay_col(h + 1)
                tap(h, 2, 1)
                tap(h, 2, 2)
                level(h, 4, invT)
                if not first:
                    out_lo(h - 1)
                tap(h, 2, 3)
                silu2(h, 2, vT)
                dve.wait_ge(s["norm_act"], h + 1)
                dve.scalar_tensor_tensor(out=col[:, 6, :], in0=col[:, 3, :], scalar=0.5, in1=gate(h, 0),
                                         op0=ALU.mult, op1=ALU.mult).then_inc(s["norm_dve"], 1)
                level(h, 5, invT)
                if not last:
                    tap(h + 1, 0, 1)
                    tap(h + 1, 0, 2)
                level(h, 6, invT)
                if not last:
                    tap(h + 1, 0, 3)
                dve.wait_ge(s["vn_ps"], h + 1)
                dve.wait_ge(s["norm_dve"], h * 5 + 5)
                dve.tensor_tensor(vbeta[:, :, :], ps[:, 2, :].rearrange("p (c i) -> p c i", c=CH), bc(col[:, 6, :], P),
                                  ALU.mult).then_inc(s["vb_ready"], 1)
                if not last:
                    silu2(h + 1, 0, qT[1 - par])
                for c in range(CH):
                    if c < CH - 1:
                        dve.wait_ge(s["st_ps"], h * 3 + c + 1)
                        if c == 0:
                            dve.tensor_copy(state[:, 0], ps[:, 7, 0:P]).then_inc(s["st_ready"], 1)
                        else:
                            dve.scalar_tensor_tensor(out=state[:, c % 2], in0=state[:, 1 - c % 2],
                                                     scalar=gates[:, bass.ds(h, 1), 3, c], in1=ps[:, 7, 0:P],
                                                     op0=ALU.mult, op1=ALU.add).then_inc(s["st_ready"], 1)
                    if c == 0 and not last:
                        tap(h + 1, 1, 1)
                    dve.wait_ge(s["o_ps"], h * 4 + c + 1)
                    if c == 0:
                        dve.tensor_copy(onat[:, 0], ps[:, 7, P:2 * P]).then_inc(s["o_ready"], 1)
                    else:
                        dve.wait_ge(s["o1_ev"], h * 3 + c)
                        dve.tensor_tensor(onat[:, c], ps[:, 7, P:2 * P], o1[:, :], ALU.add)\
                            .then_inc(s["o_ready"], 1)
                    if c == 0 and not last:
                        tap(h + 1, 1, 2)
                        tap(h + 1, 1, 3)
                    if c == 1 and not last:
                        silu2(h + 1, 1, kT[1 - par])
                if not last:
                    norms(h + 1, cols[1 - par])
                    lower(h + 1, cols[1 - par])
                dve.wait_ge(s["ztanh"], h + 1)
                if not first:
                    dve.wait_ge(s["g_f"], h)
                dve.scalar_tensor_tensor(out=zs[:, :], in0=th[:, :], scalar=1.0, in1=ps[:, 0, :],
                                         op0=ALU.add, op1=ALU.mult).then_inc(s["z_ready"], 1)

            dve.wait_ge(s["gate_dve"], 4)
            decay_col(0)
            norms(0, cols[0])
            lower(0, cols[0])
            head(0, 0, False)
            with dve.Fori(0, H // 2 - 1) as j:
                head(j * 2 + 1, 1, False)
                head(j * 2 + 2, 0, False)
            head(H - 1, 1, True)
            out_stats(H - 1, cols[1])
            out_scale(H - 1, cols[1])
            out_gate(H - 1)
            out_lo(H - 1)
            for m in range(KT):
                dve.wait_ge(s["w_used"], U_OUT + m + 1)
                dve.tensor_tensor(xT[:, m], xT[:, m], ps[:, (U_OUT + m) % 2, :], ALU.add).then_inc(s["res"], 1)
                if m == 0:
                    dve.wait_ge(s["mod_c"], 1)
                    dve.scalar_tensor_tensor(out=cact[:, :], in0=cact[:, :], scalar=1.0, in1=V["c_2"],
                                             op0=ALU.add, op1=ALU.mult).then_inc(s["mod_c"], 1)
                    for j in range(3):
                        dve.memset(mod_acc[:, j * D:(j + 1) * D], 0.0).then_inc(s["mod_done"], 1)
            dve.wait_ge(s["n_sqrt"], 2)
            dve.reciprocal(rr1[:, :], rs1[:, :]).then_inc(s["n_rstd"], 1)
            dve.wait_ge(s["n_rstd"], 2)
            for k in range(KT):
                if k >= 2:
                    dve.wait_ge(s["n_lo"], KT + k - 1)
                dve.scalar_tensor_tensor(out=hf1[:, k % 2], in0=xT[:, k], scalar=V["norm_mlp"][:, k:k + 1],
                                         in1=rr1[:, :], op0=ALU.mult, op1=ALU.mult).then_inc(s["n_h"], 1)

            def modulate(kk, j):
                if j == 0:
                    dve.wait_ge(s["mod_c"], 2)
                    dve.wait_ge(s["mod_in"], kk * 16 + 16)
                dve.wait_ge(s["mod_done"], kk * 3 + j + 1)
                cut = slice(j * D, (j + 1) * D)
                dve.scalar_tensor_tensor(out=mod_acc[:, cut], in0=mod_w[:, cut], scalar=cact[:, bass.ds(kk, 1)],
                                         in1=mod_acc[:, cut], op0=ALU.mult, op1=ALU.add).then_inc(s["mod_done"], 1)

            def quarter(q, par):
                n0 = U_MLP + q * 16
                for m in range(KT):
                    dve.wait_ge(s["mlp_relu"], q * KT + m + 1)
                    if m >= 2:
                        dve.wait_ge(s["mlp_lo"], q * KT + m - 1)
                    dve.tensor_tensor(af[:, m % 2], relu[:, m % 2], relu[:, m % 2], ALU.mult).then_inc(s["mlp_f"], 1)
                    if 2 <= m < 5:
                        modulate(q * 2, m - 2)
                for m in range(KT):
                    dve.wait_ge(s["w_used"], n0 + KT + m + 1)
                    dve.tensor_tensor(xT[:, m], xT[:, m], ps[:, (U_MLP + m) % 2, :], ALU.add).then_inc(s["res"], 1)
                    if 1 <= m < 4:
                        modulate(q * 2 + 1, m - 1)

            with dve.Fori(0, QUARTERS // 2) as j:
                quarter(j * 2, 0)
                quarter(j * 2 + 1, 1)

            done = lane("dve")
            after(dve, "pe", "modulation")
            done(dve.scalar_tensor_tensor(out=mod[:, 0:3 * KT], in0=ps[:, 7, 0:3 * KT], scalar=0.5, in1=V["ada_b_2"],
                                          op0=ALU.mult, op1=ALU.add), "mod")
            after(dve, "dve", "mod")
            done(dve.scalar_tensor_tensor(out=mod[:, 3 * KT:4 * KT], in0=mod[:, KT:2 * KT], scalar=1.0, in1=V["norm_g_2"],
                                          op0=ALU.add, op1=ALU.mult), "mod gain 1")
            after(dve, "dve", "mod gain 1")
            done(dve.tensor_tensor(mod[:, 3 * KT:4 * KT], mod[:, 3 * KT:4 * KT], V["norm_final"], ALU.mult), "mod gain 2")
            after(dve, "pe", f"square sums {KT - 1}")
            done(dve.tensor_scalar(hf1[:, 0], ps[:, 2, :], EPS, EPS * EPS, ALU.mult, ALU.add), "var 1")
            after(dve, "dve", "var 1")
            done(dve.tensor_tensor(hf1[:, 0], hf1[:, 0], ps[:, 3, :], ALU.add), "var 2")

            def norm_low(k):
                after(dve, "act", f"h high {k}")
                done(dve.scalar_tensor_tensor(out=hlo[:, k], in0=relu[:, k % 2], scalar=mod[:, k:k + 1], in1=hhi[:, k],
                                              op0=ALU.add, op1=ALU.subtract), f"norm low {k}")

            after(dve, "act", "root 2")
            done(dve.reciprocal(hf1[:, 0], hf1[:, 1]), "inv 2")
            after(dve, "dve", "inv 2")
            for k in range(KT):
                if k >= 2:
                    after(dve, "dve", f"norm low {k - 2}")
                done(dve.scalar_tensor_tensor(out=relu[:, k % 2], in0=xT[:, k], scalar=mod[:, 3 * KT + k:3 * KT + k + 1],
                                              in1=hf1[:, 0], op0=ALU.mult, op1=ALU.mult), f"h {k}")
                if k:
                    norm_low(k - 1)
            norm_low(KT - 1)
            after(dve, "act", "root 1")
            done(dve.reciprocal(rr1[:, :], rs1[:, :]), "inv 1")
            after(dve, "dve", "inv 1")
            for k in range(KT):
                done(dve.scalar_tensor_tensor(out=xT[:, k], in0=xT[:, k], scalar=V["norm_final"][:, k:k + 1],
                                              in1=rr1[:, :], op0=ALU.mult, op1=ALU.mult), f"x normed {k}")
            dve.wait_ge(s["c2_in"], 16)
            dve.tensor_copy(identb[:, :], K["ident"])
            done(dve.tensor_copy(negb[:, :], K2["causal"]), "bf16")
            dve.wait_ge(s["pos_in"], 16)
            table_step = [0]

            def tab(ins):
                done(ins, f"table {table_step[0]}")
                after(dve, "dve", f"table {table_step[0]}")
                table_step[0] += 1

            even, odd = turn[:, 0::2, :], turn[:, 1::2, :]

            tab(dve.tensor_copy(turn[:, 0], pos_i[:, :]))
            dve.tensor_scalar(ang[:, 0], turn[:, 0], K2["freq"], None, ALU.mult)
            tab(dve.tensor_scalar(ang[:, 1], turn[:, 0], K2["freq_m"], None, ALU.mult))
            dve.tensor_scalar(even, ang[:, :, :], 0.5 / np.pi, None, ALU.mult)
            tab(dve.tensor_scalar(odd, ang[:, :, :], 0.5 / np.pi, 0.25, ALU.mult, ALU.add))
            tab(dve.tensor_scalar(turn[:, :, :], turn[:, :, :], MAGIC, MAGIC, ALU.add, ALU.subtract))
            for m in range(2):
                ins = dve.scalar_tensor_tensor(out=table[:, 2 * m:2 * m + 2], in0=turn[:, 2 * m:2 * m + 2],
                                               scalar=-TWO_PI[0], in1=bc_mid(ang[:, m], 2), op0=ALU.mult, op1=ALU.add)
            tab(ins)
            for part in TWO_PI[1:]:
                tab(dve.scalar_tensor_tensor(out=table[:, :, :], in0=turn[:, :, :], scalar=-part, in1=table[:, :, :],
                                             op0=ALU.mult, op1=ALU.add))
            tab(dve.tensor_scalar(table[:, 1::2, :], table[:, 1::2, :], np.pi / 2, None, ALU.add))
            tab(dve.tensor_scalar(table[:, :, :], table[:, :, :], 3.1415925, -3.1415925, ALU.min, ALU.max))
            after(dve, "pe", "positions turned")
            done(dve.tensor_copy(cposT[:, :], ps[:, 7, P:P + CMP_BLOCK]), "positions")

            def window(w, src):
                after(dve, "act", ("ev kc", "ev vc")[w])
                after(dve, "dve", "positions")
                after(dve, "pool", "window zero") if w == 0 else after(dve, "pe", "hidden k")
                for g in range(2):
                    for half in range(2):
                        r, cut = slice(g * DK, (g + 1) * DK), slice(half * CMP_STRIDE, (half + 1) * CMP_STRIDE)
                        ins = dve.tensor_tensor(xb[r, cut, g, 0:NC], windows(src[r, :], half),
                                                cposT[r, cut].unsqueeze(2).broadcast_to([DK, CMP_STRIDE, NC]), ALU.add)
                done(ins, ("window k", "window v")[w])

            def aux_bank(name):
                return ps[:, 2 + AUX.index(name) % 2, :]

            after(dve, "pe", "aux gate")
            done(dve.tensor_copy(gate2[:, :, :], aux_bank("gate")[:, 0:CH * 3 * QH].rearrange("p (c n) -> p c n", c=CH)),
                 "post gate")
            for b, name in enumerate(("vs", "vw")):
                after(dve, "pe", f"aux {name}")
                done(dve.tensor_copy(v2[b][:, :, :], aux_bank(name).rearrange("p (c n) -> p c n", c=CH)), f"post {name}")
            window(0, kcT)
            after(dve, "act", "gate tanh")
            done(dve.tensor_scalar(gate2[:, :, :], gate2[:, :, :], 0.5, 0.5, ALU.mult, ALU.add), "gates")
            after(dve, "act", "root cq")
            done(dve.reciprocal(rcos[:, 1], rcos[:, 0]), "inv cq")
            after(dve, "dve", "inv cq")
            for w in range(2):
                done(dve.scalar_tensor_tensor(out=cn[:, w], in0=cn[:, w], scalar=V["q_norm_g_2"][:, w:w + 1], in1=rcos[:, 1],
                                              op0=ALU.mult, op1=ALU.mult), f"cq {w}")

            def rotated(name, dst, last):
                r = ROPE.index(name)
                rows_ = slice(MN, MD) if name == "kr" else slice(0, P)
                if last:
                    after(dve, "dve", last)
                after(dve, "pe", f"aux {name}")
                after(dve, "act", "tables")
                done(dve.tensor_tensor(rsin[rows_, :], aux_bank(name)[rows_], table[rows_, 2 if name == "kr" else 0], ALU.mult),
                     f"sin {name}")
                after(dve, "dve", f"sin {name}")
                after(dve, "pool", f"cos {name}")
                done(dve.tensor_tensor(dst[rows_], rcos[rows_, r % 2], rsin[rows_, :], ALU.add), f"post {name}")

            def hidden(w):
                after(dve, "act", f"tanh {'kv'[w]}")
                done(dve.scalar_tensor_tensor(out=hid[:, w, 1], in0=hid[:, w, 0], scalar=1.0,
                                              in1=ps[:, 4 + w, 0:2 * NCP].rearrange("p (g n) -> p g n", g=2),
                                              op0=ALU.add, op1=ALU.mult), f"hidden {'kv'[w]}")

            rotated("kr", krT[:, :], None)
            window(1, vcT)
            after(dve, "act", "root ckv")
            done(dve.reciprocal(csq[:, 0], csq[:, 1]), "inv ckv")
            after(dve, "dve", "inv ckv")
            done(dve.scalar_tensor_tensor(out=cn[:, 2], in0=cn[:, 2], scalar=V["kv_norm_g_2"], in1=csq[:, 0],
                                          op0=ALU.mult, op1=ALU.mult), "ckv")
            rotated("ks", kT2[0][:, :], "post kr")
            rotated("kw", kT2[1][:, :], "post ks")
            hidden(0)
            rotated("q0", q2T[:, 0], "post kw")
            rotated("q1", q2T[:, 1], "post q0")
            rotated("q2", q2T[:, 2], "post q1")
            hidden(1)
            after(dve, "dve", "hidden v")
            done(dve.tensor_copy(hid4[:, :, :, :], hid[:, 1, 1].unsqueeze(2).broadcast_to([P, 2, 4, NCP])), "hidden v 4")
            rotated("q3", q2T[:, 3], "post q2")

            def z_gate(m):
                after(dve, "act", f"z tanh {m}")
                if m == 0:
                    after(dve, "pe", "aux q3")
                done(dve.scalar_tensor_tensor(out=zs2[:, m], in0=prob[:, m % 2], scalar=1.0, in1=ps[:, m % 2, :],
                                              op0=ALU.add, op1=ALU.mult), f"z {m}")

            z_gate(0)
            after(dve, "pe", "second layer")
            done(dve.tensor_scalar(ktmp[:, 0], ps[:, 6, 0:2 * NCP].rearrange("p (g n) -> p g n", g=2), 0.5, None, ALU.mult),
                 "kc")
            after(dve, "pool", "block zero")
            for g in range(2):
                for h in range(4):
                    r = slice(h * NCP, (h + 1) * NCP)
                    ins = dve.tensor_scalar(vbd[r, g, h], ps[r, 6, 2 * NCP + g * DK:2 * NCP + (g + 1) * DK], 0.5, None,
                                            ALU.mult)
            done(ins, "block values")
            z_gate(1)

            def at_blocks(n):
                return table[:, n, CMP_BLOCK - 1::CMP_STRIDE].unsqueeze(1).broadcast_to([P, 2, NC])

            after(dve, "dve", "kc")
            done(dve.tensor_tensor(ktmp[:, 1, :, 0:NC], ktmp[:, 0, :, 0:NC], at_blocks(1), ALU.mult), "kc cos")
            after(dve, "pe", "rotate kc")
            done(dve.tensor_tensor(ktmp[:, 2, :, 0:NC], ps[:, 7, 0:2 * NCP].rearrange("p (g n) -> p g n", g=2)[:, :, 0:NC],
                                   at_blocks(0), ALU.mult), "kc sin")
            after(dve, "dve", "kc sin")
            done(dve.tensor_tensor(kcr[:, :, 0:NC], ktmp[:, 1, :, 0:NC], ktmp[:, 2, :, 0:NC], ALU.add), "kc rotated")
            z_gate(2)
            z_gate(3)
            after(dve, "pe", "block scores")
            for g in range(2):
                for c in range(CH):
                    ins = dve.scalar_tensor_tensor(out=by_head(csc[:, g])[:, c], in0=by_head(ps[:, 4 + g, :])[:, c],
                                                   scalar=SCALE, in1=seen_by("cmp_neg")[:, c], op0=ALU.mult, op1=ALU.add)
            done(ins, "scaled")
            scores = csc[:, :, :].rearrange("p g (r n) -> p (g r) n", n=NCP)
            after(dve, "dve", "scaled")
            done(dve.tensor_reduce(csm[:, 0], scores, AX.X, ALU.max), "max")
            after(dve, "dve", "max")
            done(dve.tensor_tensor(scores, scores, bc(csm[:, 0], NCP), ALU.subtract), "less max")
            z_gate(4)
            z_gate(5)
            after(dve, "act", "block exp")
            done(dve.tensor_reduce(csm[:, 1], scores, AX.X, ALU.add), "sum")
            after(dve, "dve", "sum")
            for g in range(2):
                ins = dve.tensor_tensor(by_head(csc[:, g]), by_head(csc[:, g]), seen_by("cmp_one"), ALU.mult)
            done(ins, "seen")
            done(dve.reciprocal(csm[:, 2], csm[:, 1]), "sum inv")
            after(dve, "dve", "sum inv")
            after(dve, "dve", "gates")
            done(dve.tensor_tensor(csm[:, 3].rearrange("p (g q h) -> p g q h", g=2, q=CH),
                                   csm[:, 2].rearrange("p (g q h) -> p g q h", g=2, q=CH),
                                   gate2[:, :, :].rearrange("p q (g h b) -> p g q h b", g=2, b=3)[:, :, :, :, 0], ALU.mult),
                 "coef")
            after(dve, "dve", "coef")
            done(dve.tensor_tensor(scores, scores, bc(csm[:, 3], NCP), ALU.mult), "probs")
            z_gate(6)
            z_gate(7)
            after(dve, "pe", "block values")
            done(dve.tensor_copy(o_nsa[:, :, :], ps[:, 2:6, :]), "block out")

            def most(i, n, exp_scale, keys):
                dve.wait_ge(s["at_s"], n + 1)
                if i >= 2:
                    dve.wait_ge(s["at_exp"], n - 1)
                c = slice(i % 2, i % 2 + 1)
                dve.tensor_reduce(amax[:, c], ps[:, i % 4, 0:keys], AX.X, ALU.max).then_inc(s["at_max"], 1)
                dve.wait_ge(s["at_max"], n + 1)
                dve.tensor_scalar(aneg[:, c], amax[:, c], -exp_scale, None, ALU.mult).then_inc(s["at_neg"], 1)

            def attend(first, count, exp_scale, weigh, combine):
                for i in range(count + 3):
                    if i < count:
                        most(i, first + i, exp_scale, (i % 4 + 1) * P)
                    if 1 <= i <= count:
                        k, n = i - 1, first + i - 1
                        dve.wait_ge(s["at_exp"], n + 1)
                        dve.reciprocal(ainv[:, k % 4:k % 4 + 1], asum[:, k % 2:k % 2 + 1]).then_inc(s["at_inv"], 1)
                        dve.wait_ge(s["at_inv"], n + 1)
                        weigh(k)
                    if i >= 3:
                        k, n = i - 3, first + i - 3
                        dve.wait_ge(s["at_o"], n + 1)
                        dve.wait_ge(s["at_done"], n + 1)
                        combine(k, n)

            dve.memset(acoef[:, :], 0.0).then_inc(s["at_done"], 1)
            with dve.Fori(0, 4) as j:
                def weigh(k):
                    g, b, c = k // 8, k // 4 % 2, slice(k % 4, k % 4 + 1)
                    dve.tensor_tensor(acoef[:, c], ainv[:, c], gate2[:, k % 4, bass.ds(j * 3 + (g * 12 + 1 + b), 1)],
                                      ALU.mult).then_inc(s["at_coef"], 1)

                def combine(k, n):
                    dve.wait_ge(s["at_coef"], n + 1)
                    o = o_nsa[:, k % 4, bass.ds(j * DK + k // 8 * 256, DK)]
                    dve.scalar_tensor_tensor(out=o, in0=ps[:, 6 + k % 2, 0:DK], scalar=acoef[:, k % 4:k % 4 + 1], in1=o,
                                             op0=ALU.mult, op1=ALU.add).then_inc(s["at_done"], 1)

                attend(j * 16, 16, SCALE, weigh, combine)
            for par in range(2):
                ins = dve.tensor_copy(km[MN:MD, par], krT[MN:MD, :])
            done(ins, "rotated keys")
            with dve.Fori(0, QH // 2) as j:
                for par in range(2):
                    if par:
                        dve.wait_ge(s["p_q"], j * 2 + 1)
                    dve.wait_ge(s["p_rot"], j * 2 + par + 1)
                    dve.tensor_tensor(qsin[0:MD, :], ps[0:MD, 4 + par, :], table[0:MD, 2], ALU.mult).then_inc(s["p_sin"], 1)
                    dve.wait_ge(s["p_sin"], j * 2 + par + 1)
                    dve.wait_ge(s["p_cos"], j * 2 + par + 1)
                    dve.tensor_tensor(qm[0:MD, par], qcos[0:MD, :], qsin[0:MD, :], ALU.add).then_inc(s["p_q"], 1)

                def combine_m(k, n):
                    dve.tensor_scalar(o_mla[:, k % 4, bass.ds(j * 2 * DK + k // 4 * DK, DK)], ps[:, 6 + k % 2, 0:DK],
                                      ainv[:, k % 4:k % 4 + 1], None, ALU.mult).then_inc(s["at_done"], 1)

                attend(j * 8 + 64, 8, SCALE_M, lambda k: None, combine_m)
            for k in range(KT):
                after(dve, "pe", f"turned {k}")
                if k >= 2:
                    after(dve, "pool", f"mix low {k - 2}")
                done(dve.scalar_tensor_tensor(out=gated[:, k % 2], in0=ps[:, 2 + k % 4, :], scalar=0.5, in1=zs2[:, k],
                                              op0=ALU.mult, op1=ALU.mult), f"mixed {k}")
            for m in range(KT):
                dve.wait_ge(s["w_used"], U_OUT2 + m + 1)
                done(dve.scalar_tensor_tensor(out=xT[:, m], in0=ps[:, m % 2, :], scalar=mod[:, 2 * KT + m:2 * KT + m + 1],
                                              in1=xT[:, m], op0=ALU.mult, op1=ALU.add), f"x {m}")
            after(dve, "act", "out root")
            done(dve.reciprocal(orr[:, :], ors[:, :]), "out inv")
            after(dve, "dve", "out inv")
            for k in range(KT):
                if k >= 2:
                    after(dve, "pe", f"back {k - 2}")
                done(dve.scalar_tensor_tensor(out=onorm[:, k % 2], in0=xT[:, k], scalar=V["final_norm_g_2"][:, k:k + 1],
                                              in1=orr[:, :], op0=ALU.mult, op1=ALU.mult), f"y {k}")

        @block.tensor
        def _(pe):
            def unit_parts(n, slot, hi, lo, width=P, ready=None):
                pe.wait_ge(s["w_lo"], n + 1)
                bank = ps[0:width, slot % 2, :]
                todo = [(k, w, x) for k in range(KT) for w, x in ((whi, hi), (whi, lo), (wlo, hi))]
                for i, (k, w, x) in enumerate(todo):
                    if ready is not None and i % 3 == 0:
                        ready(k)
                    mm = pe.matmul(bank, w[:, slot, k, 0:width], x[:, k], start=(i == 0), stop=(i == len(todo) - 1))
                    if i == len(todo) - 1:
                        mm.then_inc(s["w_used"], 1)
                    yield

            def unit(*a, **kw):
                for _ in unit_parts(*a, **kw):
                    pass

            pe.wait_ge(s["const_in"], 16)
            ident = K["ident"]
            pe.wait_ge(s["x_in"], 16 * CH)
            for k in range(KT):
                if k >= 4:
                    pe.wait_ge(s["xev"], k - 3)
                for c in range(CH):
                    mm = pe.transpose(ps[:, 3 + k % 4, c * P:(c + 1) * P], xn[:, c, k * P:(k + 1) * P], ident)
                mm.then_inc(s["xtr"], 1)

                def stat(k):
                    pe.wait_ge(s["n_sq"], k + 1)
                    pe.matmul(ps[:, 2, :], K["mean"], sqn[:, k % 2], start=(k == 0), stop=(k == KT - 1))\
                        .then_inc(s["n_stat"], 1)
                if k >= 1:
                    stat(k - 1)
            stat(KT - 1)
            pe.wait_ge(s["vec_in"], 16 * (len(VEC_ROWS) + 4))
            pe.transpose(ps[:, 7, 0:NVEC], rows[0:NVEC, 0, :], ident[0:NVEC, 0:NVEC])
            pe.transpose(ps[:, 7, P:P + 96], rows[0:96, 1, :], ident[0:96, 0:96]).then_inc(s["vec_tr"], 1)
            unit(0, 0, hhi, hlo, ready=lambda k: pe.wait_ge(s["n_lo"], k + 1))
            unit(1, 1, hhi, hlo)
            pe.wait_ge(s["conv1"], 3)
            unit(2, 2, hhi, hlo, BA_N)
            pe.wait_ge(s["ba_ev"], 1)
            for c in range(CH):
                mm = pe.transpose(ps[:, 5, c * 16:(c + 1) * 16], ba[BA_LEAD:BA_N, c * P:(c + 1) * P],
                                  ident[BA_LEAD:BA_N, BA_LEAD:BA_N])
            mm.then_inc(s["ba_tr"], 1)
            pe.wait_ge(s["gate_dve"], 4)
            g2 = glog[:, :, :].rearrange("p c h -> p (c h)")
            for n, m in enumerate(("upto", "after", "ones")):
                mm = pe.matmul(ps[:, 4, 32 * n:32 * n + 32], K[m], g2, start=True, stop=True)
            mm.then_inc(s["gate_ps"], 1)

            def chunk(t, c):
                return t[:, c * P:(c + 1) * P]

            def decay_sums(h, w):
                pe.wait_ge(s["dz_in"], h * 2 + w + 1)
                if w == 0:
                    pe.wait_ge(s["gate_ready"], 4) if known(h, 0) else pe.wait_ge(s["inv_ready"], h * 13)
                elif not known(h, 0):
                    pe.wait_ge(s["w_ev"], h)
                pe.matmul(ps[:, 4 + w, :], K[("upto", "after")[w]], gd[:, :, :].rearrange("p c i -> p (c i)"),
                          start=True, stop=True).then_inc(s["dps"], 1)

            def pair_products(h, q, k):
                pe.wait_ge(s["seq_ready"], h * 3 + 2)
                for c in range(CH):
                    mm = pe.matmul(ps[:, 6, c * P:(c + 1) * P], chunk(k, c), chunk(k, c), start=True, stop=True)
                mm.then_inc(s["kk_ps"], 1)
                pe.wait_ge(s["sqs"], h * 2 + 2)
                pe.wait_ge(s["dexp"], h * 2 + 1)
                for w in range(2):
                    for c in range(CH):
                        mm = pe.matmul(ps[:, 4, w * 4 + c:w * 4 + c + 1], chunk(sq[:, w], c), K["ones"][:, 0:1],
                                       start=True, stop=True)
                mm.then_inc(s["ss_ps"], 1)
                pe.wait_ge(s["dexp"], h * 2 + 2)
                for c in range(CH):
                    mm = pe.matmul(ps[:, 5, c * P:(c + 1) * P], chunk(k, c), chunk(q, c), start=True, stop=True)
                mm.then_inc(s["kk_ps"], 1)
                if not known(h, 0):
                    pe.wait_ge(s["vb_ready"], h)
                for c in range(CH):
                    mm = pe.transpose(ps[:, 2, c * P:(c + 1) * P], chunk(k, c), ident)
                mm.then_inc(s["kn_ps"], 1)

            def out_turn(h):
                pe.wait_ge(s["o_scaled"], h + 1)
                for c in range(CH):
                    mm = pe.transpose(ps[:, 3, c * P:(c + 1) * P], osq[:, c], ident)
                mm.then_inc(s["o_tr"], 1)

            def head(h, par, last):
                def fillers():
                    pe.wait_ge(s["seq_ready"], h * 3 + 2)
                    yield from unit_parts(h * 4 + 3, 3, hhi, hlo)
                    if not last:
                        pe.wait_ge(s["ba_ev"], 1) if known(h, 0) else pe.wait_ge(s["z_ready"], h)
                        yield from unit_parts(h * 4 + 4, 0, hhi, hlo)
                        pe.wait_ge(s["seq_ready"], h * 3 + 3)
                        yield from unit_parts(h * 4 + 5, 1, hhi, hlo)
                        pe.wait_ge(s["seq_ready"], h * 3 + 4)
                        yield from unit_parts(h * 4 + 6, 2, hhi, hlo)
                    else:
                        pe.wait_ge(s["z_ready"], h)
                        yield from unit_parts(DN_UNITS - 1, 0, hhi, hlo)

                stream = fillers()

                def fill(n):
                    for _ in range(n):
                        next(stream, None)

                first = known(h, 0)
                q, invT = qT[par], invTs[par]
                pe.wait_ge(s["lev_ready"], h * 7 + 1)
                pe.wait_ge(s["norm_dve"], h * 5 + 1)
                for c in range(CH):
                    mm = pe.transpose(ps[:, 4, c * P:(c + 1) * P], lev[:, 0, c], ident)
                mm.then_inc(s["inv_ps"], 1)
                fill(8)
                for li in range(1, NL):
                    lv = LEVELS[li]
                    pe.wait_ge(s["lev_ready"], h * 7 + li + 1)
                    pe.wait_ge(s["inv_ready"], h * 13 + 2 * li)

                    def half(t, odd):
                        return t.rearrange("p (b o l) -> p b o l", o=2, l=lv)[:, :, odd, :]

                    def to(bank, n):
                        return ps[:, bank, n * 64:(n + 1) * 64].rearrange("p (b l) -> p b l", l=lv)

                    for c in range(CH):
                        mm = pe.matmul(to(4, c), lev[:, li % NB, c], half(invT[:, c], 1), start=True, stop=True)
                    mm.then_inc(s["q_ps"], 1)
                    fill(6 if li > 2 else 5)
                    pe.wait_ge(s["q_ev"], h * 6 + li)
                    if li == 1:
                        pe.wait_ge(s["low_ready"], h * 4 + 4)
                    for c in range(CH):
                        mm = pe.matmul(to(6, c), inv[:, c], half(qlev[lv][:, c], 1), start=True, stop=True)
                    if li < NL - 1:
                        for c in range(CH):
                            mm = pe.matmul(to(6, CH + c), qlev[lv][:, c], half(inv[:, c], 0), start=True, stop=True)
                    mm.then_inc(s["r_ps"], 1)
                    fill(6 if li > 2 else 5)
                    if li == 2 and not first:
                        out_turn(h - 1)
                    if li == NL - 2:
                        pe.wait_ge(s["kside"], h * 2 + 2)
                        pe.wait_ge(s["seq_ready"], h * 3 + 3)
                        for c in range(CH):
                            mm = pe.transpose(ps[:, 2, c * P:(c + 1) * P], chunk(vT, c), ident)
                        mm.then_inc(s["vn_ps"], 1)
                pe.wait_ge(s["inv_ready"], h * 13 + 13)
                pe.wait_ge(s["attn_ready"], h + 1)
                for c in range(CH):
                    mm = pe.matmul(ps[:, 5, c * P:(c + 1) * P], kbeta[:, c], invT[:, c], start=True, stop=True)
                mm.then_inc(s["w_ps"], 1)
                for c in range(CH):
                    if c == 0:
                        pe.wait_ge(s["vb_ready"], h + 1)
                        if not first:
                            pe.wait_ge(s["g_f"], h)
                    else:
                        pe.wait_ge(s["v_ev"], h * 4 + c)
                        if c > 1:
                            pe.wait_ge(s["o1_ev"], h * 3 + c - 1)
                    vb = ps[:, 3, 0:P]
                    mm = pe.matmul(vb, invT[:, c], vbeta[:, c], start=True, stop=(c == 0))
                    if c:
                        pe.wait_ge(s["w_ev"], h + 1)
                        pe.wait_ge(s["st_ready"], h * 3 + c)
                        mm = pe.matmul(vb, wT[:, c], state[:, (c - 1) % 2], start=False, stop=True)
                    mm.then_inc(s["v_ps"], 1)
                    fill(3)
                    pe.wait_ge(s["v_ev"], h * 4 + c + 1)
                    if c:
                        pe.matmul(ps[:, 3, P:2 * P], chunk(q, c), state[:, (c - 1) % 2], start=True, stop=True)\
                            .then_inc(s["o1_ps"], 1)
                        pe.wait_ge(s["o_ready"], h * 4 + c)
                    if c < CH - 1:
                        pe.matmul(ps[:, 7, 0:P], kdec[:, c], vnew[:, c], start=True, stop=True).then_inc(s["st_ps"], 1)
                        if c == 0 and not last:
                            decay_sums(h + 1, 0)
                        fill(3)
                        pe.wait_ge(s["st_ready"], h * 3 + c + 1)
                    pe.matmul(ps[:, 7, P:2 * P], attnT[:, c], vnew[:, c], start=True, stop=True)\
                        .then_inc(s["o_ps"], 1)
                    if c == 1 and not last:
                        decay_sums(h + 1, 1)
                    if c < 3:
                        fill(3)
                if not last:
                    pair_products(h + 1, qT[1 - par], kT[1 - par])
                fill(96)

            decay_sums(0, 0)
            decay_sums(0, 1)
            pair_products(0, qT[0], kT[0])
            head(0, 0, False)
            with pe.Fori(0, H // 2 - 1) as j:
                head(j * 2 + 1, 1, False)
                head(j * 2 + 2, 0, False)
            head(H - 1, 1, True)
            out_turn(H - 1)

            def stat1(m, k):
                pe.wait_ge(s["n_sq"], m * KT + k + 1)
                pe.matmul(ps[:, 2, :], K["mean"], nsq[:, k % 2], start=(k == 0), stop=(k == KT - 1))\
                    .then_inc(s["n_stat"], 1)

            pe.wait_ge(s["z_ready"], H)
            for m in range(KT):
                if m >= 2:
                    pe.wait_ge(s["res"], m - 1)
                unit(U_OUT + m, (U_OUT + m) % RING, ahi[0], alo[0],
                     ready=(lambda k: pe.wait_ge(s["g_lo"], k + 1)) if m == 0 else None)
                if m:
                    stat1(1, m - 1)
            stat1(1, KT - 1)

            def quarter(q, par):
                n0 = U_MLP + q * 16
                for m in range(KT):
                    pe.wait_ge(s["mlp_relu"], q * KT + m - 1) if m >= 2 else pe.wait_ge(s["res"], q * KT + KT - 1 + m)
                    unit(n0 + m, (U_MLP + m) % RING, hhi, hlo,
                         ready=(lambda k: pe.wait_ge(s["n_lo"], KT + k + 1)) if m == 0 else None)
                for m in range(KT):
                    pe.wait_ge(s["mlp_relu"], q * KT + KT - 1 + m) if m < 2 else \
                        pe.wait_ge(s["res"], KT + q * KT + m - 1)
                    unit(n0 + KT + m, (U_MLP + m) % RING, ahi[par], alo[par],
                         ready=(lambda k: pe.wait_ge(s["mlp_lo"], q * KT + k + 1)) if m == 0 else None)

            with pe.Fori(0, QUARTERS // 2) as j:
                quarter(j * 2, 0)
                quarter(j * 2 + 1, 1)

            done = lane("pe")
            pe.wait_ge(s["mod_done"], 3 * (KT + 1))
            for m in range(3 * KT):
                mm = pe.matmul(ps[:, 7, m:m + 1], mod_acc[:, m * P:(m + 1) * P], K["ones"][:, 0:1], start=True, stop=True)
            done(mm, "modulation")
            for k in range(KT):
                after(pe, "act", f"squares {k}")
                pe.matmul(ps[:, 2, :], K["mean"], nsq[:, k % 2], start=(k == 0), stop=(k == KT - 1))
                done(pe.matmul(ps[:, 3, :], K["mean"], relu[:, k % 2], start=(k == 0), stop=(k == KT - 1)),
                     f"square sums {k}")

            def aux(name):
                x = AUX.index(name)
                after(pe, "act", f"ev {name}")
                if x >= 2:
                    after(pe, "dve", f"post {AUX[x - 2]}")
                if x == 4:
                    after(pe, "dve", "var 2")
                bank, src = ps[:, 2 + x % 2, :], raw[:, x % 3]
                if name == "gate":
                    after(pe, "dve", "var 1")
                    for c in range(CH):
                        mm = pe.transpose(bank[:, c * 3 * QH:(c + 1) * 3 * QH], src[0:3 * QH, c * P:(c + 1) * P],
                                          ident[0:3 * QH, 0:3 * QH])
                elif name[0] == "v":
                    if name == "vs":
                        after(pe, "dve", "var 2")
                    for c in range(CH):
                        mm = pe.transpose(bank[:, c * P:(c + 1) * P], src[:, c * P:(c + 1) * P], ident)
                elif name == "kr":
                    mm = pe.matmul(bank[0:MD], K2["rot_m"][MN:MD, 0:MD], src[MN:MD], start=True, stop=True)
                else:
                    mm = pe.matmul(bank, K2["rot"], src, start=True, stop=True)
                done(mm, f"aux {name}")

            def hidden(w):
                pe.wait_ge(w1_in[w], 32)
                after(pe, "dve", ("window k", "window v")[w])
                for l in range(CMP_BLOCK):
                    mm = pe.matmul(ps[:, 4 + w, 0:2 * NCP], w1[w][:, l], xb[:, l].rearrange("p g n -> p (g n)"),
                                   start=(l == 0), stop=(l == CMP_BLOCK - 1))
                done(mm, ("hidden k", "hidden v")[w])

            pe.wait_ge(s["c2_in"], 16)
            for a, name in enumerate(TWO):
                if a >= 2:
                    after(pe, "act", f"ev {TWO[a - 2]}")
                n = U_TWO + a
                unit(n, n % RING, hhi, hlo, ready=(lambda k: after(pe, "dve", f"norm low {k}")) if a == 0 else None)
                if a == 1:
                    pe.wait_ge(s["cpos_in"], 32)
                    after(pe, "dve", "mod")
                    done(pe.transpose(ps[:, 7, P:P + CMP_BLOCK], cpos[0:CMP_BLOCK, :], ident[0:CMP_BLOCK, 0:CMP_BLOCK]),
                         "positions turned")
                if TWO[a - 1] in AUX and a:
                    aux(TWO[a - 1])
                if name == "kr":
                    for w in range(2):
                        after(pe, "act", f"square cq{w}")
                        mm = pe.matmul(ps[:, 6, :], K["mean"], csq[:, w], start=(w == 0), stop=(w == 1))
                    done(mm, "sum cq")
                    hidden(0)
                if name == "ks":
                    after(pe, "act", "square ckv")
                    after(pe, "dve", "positions")
                    done(pe.matmul(ps[:, 7, :], K["mean"], csq[:, 0], start=True, stop=True), "sum ckv")
                if name == "q1":
                    hidden(1)
            aux("q3")

            def z_unit(m):
                after(pe, "act", f"ev q{2 + m}") if m < 2 else after(pe, "dve", f"z {m - 2}")
                unit(U_Z + m, (U_Z + m) % RING, hhi, hlo)

            z_unit(0)
            pe.wait_ge(s["w2_in"], 48)
            after(pe, "act", "root cq")
            after(pe, "dve", "hidden v 4")
            pe.matmul(ps[:, 6, 0:2 * NCP], w2c[:, 0:2].rearrange("p a c -> p (a c)"),
                      hid[:, 0, 1].rearrange("p g n -> p (g n)"), start=True, stop=True)
            for g in range(2):
                mm = pe.matmul(ps[:, 6, 2 * NCP + g * DK:2 * NCP + (g + 1) * DK],
                               hid4[:, g].rearrange("p r n -> p (r n)"), w2c[:, 2], start=True, stop=True)
            done(mm, "second layer")
            z_unit(1)
            after(pe, "dve", "kc")
            after(pe, "act", "root ckv")
            done(pe.matmul(ps[:, 7, 0:2 * NCP], K2["rot"], ktmp[:, 0].rearrange("p g n -> p (g n)"), start=True, stop=True),
                 "rotate kc")
            z_unit(2)
            z_unit(3)
            after(pe, "dve", "kc rotated")
            for h in range(QH):
                g, r = h // 4, slice(h // 4 * DK, (h // 4 + 1) * DK)
                for c in range(CH):
                    mm = pe.matmul(ps[:, 4 + g, c * P + h % 4 * NCP:c * P + (h % 4 + 1) * NCP],
                                   q2T[r, h % 4, c * P:(c + 1) * P], kcr[r, g], start=True, stop=True)
            done(mm, "block scores")
            z_unit(4)
            z_unit(5)
            z_unit(6)
            after(pe, "dve", "probs")
            for g in range(2):
                for c in range(CH):
                    mm = pe.transpose(ps[:, 6 + g, c * P:(c + 1) * P], csc[:, g, c * P:(c + 1) * P], ident)
            done(mm, "block turned")
            z_unit(7)
            after(pe, "act", "block turned")
            for g in range(2):
                for c in range(CH):
                    mm = pe.matmul(ps[:, 2 + c, g * 256:(g + 1) * 256], cpT[:, g, c * P:(c + 1) * P],
                                   vbd[:, g].rearrange("p h d -> p (h d)"), start=True, stop=True)
            done(mm, "block values")

            def attend(first, count, q_of, k_of, v_of):
                for i in range(count + 3):
                    if i < count:
                        n, qt = first + i, i % 4
                        if i >= 4:
                            pe.wait_ge(s["at_exp"], n - 3)
                        pe.matmul(ps[:, i % 4, 0:(qt + 1) * P], q_of(i), k_of(i), start=True, stop=False)
                        pe.matmul(ps[:, i % 4, qt * P:(qt + 1) * P], identb[:, :], negb[:, :], start=False, stop=True)                            .then_inc(s["at_s"], 1)
                    if 2 <= i < count + 2:
                        k, n, qt = i - 2, first + i - 2, (i - 2) % 4
                        pe.wait_ge(s["at_exp"], n + 1)
                        if k >= 2:
                            pe.wait_ge(s["at_tev"], n - 1)
                        for c in range(qt + 1):
                            mm = pe.transpose(ps[:, 4 + k % 2, c * P:(c + 1) * P], prob[:, k % 2, c * P:(c + 1) * P], ident)
                        mm.then_inc(s["at_t"], 1)
                    if i >= 3:
                        k, n, qt = i - 3, first + i - 3, (i - 3) % 4
                        pe.wait_ge(s["at_tev"], n + 1)
                        pe.wait_ge(s["at_done"], n) if k >= 2 else pe.wait_ge(s["at_done"], first + 1)
                        for c in range(qt + 1):
                            mm = pe.matmul(ps[:, 6 + k % 2, 0:DK], probT[:, k % 2, c * P:(c + 1) * P], v_of(k, c),
                                           start=(c == 0), stop=(c == qt))
                        mm.then_inc(s["at_o"], 1)

            def group(i):
                return slice(i // 8 * DK, (i // 8 + 1) * DK)

            after(pe, "dve", "block out")
            with pe.Fori(0, 4) as j:
                pe.wait_ge(s["q_staged"], j + 1)
                attend(j * 16, 16, lambda i: qh[group(i), i % 4 * P:(i % 4 + 1) * P],
                       lambda i: kT2[i // 4 % 2][group(i), 0:(i % 4 + 1) * P],
                       lambda i, c: v2[i // 4 % 2][:, c, group(i)])
            pe.wait_ge(s["at_done"], 65)
            pe.wait_ge(s["wv_in"], 16)
            for c in range(CH):
                mm = pe.matmul(ps[:, c, :], cn[:, 2, c * P:(c + 1) * P], wv[:, :, :].rearrange("p h d -> p (h d)"),
                               start=True, stop=True)
            done(mm, "latent values")
            after(pe, "act", "latent values")
            after(pe, "dve", "rotated keys")
            with pe.Fori(0, QH // 2) as j:
                pe.wait_ge(s["at_done"], j * 8 + 65)
                for par in range(2):
                    pe.wait_ge(wq_in[par], j * 32 + 32)
                    for k in range(2):
                        pe.matmul(ps[0:MD, par, :], wq[:, par, k], cn[:, k], start=(k == 0), stop=(k == 1))
                    pe.matmul(ps[0:MN, 2 + par, :], wk[:, par], cn[:, 2], start=True, stop=True).then_inc(s["p_ps"], 1)
                for par in range(2):
                    pe.wait_ge(s["p_ev"], j * 2 + par + 1)
                    pe.matmul(ps[0:MD, 4 + par, :], K2["rot_m"][0:MD, 0:MD], qraw[0:MD, par], start=True, stop=True)                        .then_inc(s["p_rot"], 1)
                pe.wait_ge(s["p_q"], j * 2 + 2)
                attend(j * 8 + 64, 8, lambda i: qm[0:MD, i // 4, i % 4 * P:(i % 4 + 1) * P],
                       lambda i: km[0:MD, i // 4, 0:(i % 4 + 1) * P],
                       lambda i, c: v_mla[:, c, bass.ds(j * 2 * DK + i // 4 * DK, DK)])
            pe.wait_ge(s["at_done"], 97)
            for k in range(KT):
                if k >= 4:
                    after(pe, "dve", f"mixed {k - 4}")
                o = (o_nsa, o_mla)[k // 4]
                for c in range(CH):
                    mm = pe.transpose(ps[:, 2 + k % 4, c * P:(c + 1) * P], o[:, c, k % 4 * P:(k % 4 + 1) * P], ident)
                done(mm, f"turned {k}")
            for m in range(KT):
                if m >= 2:
                    after(pe, "dve", f"x {m - 2}")
                unit(U_OUT2 + m, (U_OUT2 + m) % RING, hhi, hlo,
                     ready=(lambda k: after(pe, "pool", f"mix low {k}")) if m == 0 else None)
                if m:
                    after(pe, "act", f"out squares {m - 1}")
                    done(pe.matmul(ps[:, 2, :], K["mean"], osqr[:, (m - 1) % 2], start=(m == 1), stop=False),
                         f"out sums {m - 1}")
            after(pe, "act", f"out squares {KT - 1}")
            done(pe.matmul(ps[:, 2, :], K["mean"], osqr[:, (KT - 1) % 2], start=False, stop=True), f"out sums {KT - 1}")
            for k in range(KT):
                after(pe, "dve", f"y {k}")
                if k >= 2:
                    after(pe, "act", f"out rows {k - 2}")
                for c in range(CH):
                    mm = pe.transpose(ps[:, 4 + k % 2, c * P:(c + 1) * P], onorm[:, k % 2, c * P:(c + 1) * P], ident)
                done(mm, f"back {k}")


_INS = ["x", "norm_mix", "norm_mlp", "norm_final", "dn_w_in", "dn_conv_w", "dn_a_log", "dn_dt_bias", "dn_norm_w",
        "dn_w_out", "mlp_w_up", "mlp_w_down", "c_2", "positions_2", "ada_w_2", "ada_b_2", "norm_g_2", "w_in_2",
        "cmp_pos_2", "cmp_k_w1_2", "cmp_k_w2_2", "cmp_v_w1_2", "cmp_v_w2_2", "q_norm_g_2", "w_q_up_2",
        "kv_norm_g_2", "w_kv_up_2", "w_out_2", "final_norm_g_2"]


def kernel(**inputs):
    import concourse.bacc as bacc
    from concourse.bass_utils import run_bass_kernel_spmd

    nc = bacc.Bacc("TRN2", target_bir_lowering=False, num_devices=1)
    arrays, A = {}, {}

    def give(name, a):
        arrays[name] = a
        A[name] = nc.dram_tensor(name, a.shape, mybir.dt.from_np(a.dtype), kind="ExternalInput").ap()

    for name in _INS:
        give(name, np.ascontiguousarray(inputs[name]))
    consts, cols = shape_constants()
    give("consts", consts)
    consts2, cols2 = shape_constants_2()
    give("consts2", consts2)
    out = nc.dram_tensor("out", (T, D), mybir.dt.float32, kind="ExternalOutput").ap()
    build(nc, A, out, cols, cols2)
    r = run_bass_kernel_spmd(nc, [arrays], core_ids=[0])
    return r.results[0]["out"].reshape(1, T, D)
```

```python
from contextlib import ExitStack

import numpy as np

import concourse.bass as bass
from concourse import mybir

P = 128
D = 1024
T = 512
KT = D // P
CH = T // P
H = 8
FF = 4 * D
QUARTERS = FF // D
EPS = 1e-6
F_INV, F_Q, F_R, F_W, F_C0, F_C = 7, 4, 4, 11, 6, 4
RING = 4
NEG = -1e30

BA_LEAD = 96
DN_UNITS = 1 + 4 * H
U_OUT = DN_UNITS
U_MLP = U_OUT + KT
U_TWO = U_MLP + 2 * KT * QUARTERS

QH, DK = 8, 64
MN, MR = 64, 32
MD = MN + MR
CMP_BLOCK, CMP_STRIDE, CMP_HID = 32, 16, 128
NC = T // CMP_STRIDE - CMP_BLOCK // CMP_STRIDE + 1
NCP = 32
QW = QH * DK
AT_KC, AT_VC, AT_KS, AT_VS, AT_KW, AT_VW = (QW + P * n for n in range(6))
AT_GATE = QW + 6 * P
AT_Z = AT_GATE + 3 * QH
AT_CQ = AT_Z + QW
AT_CKV = AT_CQ + 256
AT_KR = AT_CKV + P
AT_ZM = AT_KR + MR
TWO = ["kc", "vc", "gate", "vs", "vw", "q0", "q1", "q2", "q3", "ks", "kw", "cq0", "cq1", "ckv", "kr"]
U_Z = U_TWO + len(TWO)
U_OUT2 = U_Z + KT
KH = KT // 2
AUX = ["gate", "vs", "vw", "q0", "q1", "q2", "q3", "ks", "kw", "kr"]
ROPE = ["q0", "q1", "q2", "q3", "ks", "kw", "kr"]
TWO_PI = 6.28125, 0.0019350051879882812, 3.0199159819567e-07
MAGIC = 1.5 * 2.0 ** 23

LEVELS = [1, 2, 4, 8, 16, 32, 64]
NL = len(LEVELS)


def side_by_side(parts):
    cols, at, blocks = {}, 0, []
    for name, block in parts.items():
        cols[name] = (at, at + block.shape[1])
        at += block.shape[1]
        blocks.append(block)
    return np.ascontiguousarray(np.concatenate(blocks, axis=1).astype(np.float32)), cols


def shape_constants():
    i = np.arange(P)
    parts = {}
    parts["ident"] = np.eye(P)
    parts["mean"] = np.full((P, P), 1.0 / D)
    parts["ones"] = np.ones((P, P))
    parts["upto"] = (i[:, None] <= i[None, :]) * 1.0
    parts["after"] = (i[:, None] > i[None, :]) * 1.0
    for s in LEVELS:
        a, b = i[:, None] // s, i[None, :] // s
        parts[f"level{s}"] = ((a == b + 1) & (b % 2 == 0)) * 1.0
    parts["eps"] = np.tile(np.array([[EPS, 4 * EPS]]), (P, 1))
    return side_by_side(parts)


def shape_constants_2():
    i = np.arange(P)
    parts = {}
    parts["causal"] = np.where(i[None, :] <= i[:, None], 0.0, NEG)
    blk, t = np.arange(NCP)[None, None, :], (np.arange(CH) * P)[None, :, None] + i[:, None, None]
    seen = (blk * CMP_STRIDE + CMP_BLOCK - 1 <= t) & (blk < NC)
    parts["cmp_neg"] = np.where(seen, 0.0, NEG).reshape(P, -1)
    parts["cmp_one"] = (seen * 1.0).reshape(P, -1)
    for name, rows, first, width in (("rot", P, 0, 64), ("rot_m", P, 64, 32)):
        m = np.zeros((P, P))
        for h0 in range(first, P if first == 0 else 96, width):
            for d in range(width // 2):
                m[h0 + d + width // 2, h0 + d] = -1.0
                m[h0 + d, h0 + d + width // 2] = 1.0
        parts[name] = m
    for name, first, width in (("freq", 0, 64), ("freq_m", 64, 32)):
        half = width // 2
        inv = np.float32(10000.0) ** (-np.arange(half, dtype=np.float32) / np.float32(half))
        f = np.array([inv[(p - first) % width % half] if first <= p < (P if first == 0 else 96) else 0.0 for p in range(P)])
        parts[name] = f[:, None]
    return side_by_side(parts)


VEC_ROWS = {"norm_mix": KT, "norm_mlp": KT, "norm_final": KT, "norm_g_2": KT, "final_norm_g_2": KT,
            "ada_b_2": 3 * KT, "q_norm_g_2": 2, "kv_norm_g_2": 1, "dn_norm_w": 1, "c_2": KT}
VEC_AT, NVEC = {}, 0
for _name, _rows in VEC_ROWS.items():
    VEC_AT[_name] = NVEC
    NVEC += _rows


def build(nc, A, out, const_cols, const2_cols):
    F32, F32R = mybir.dt.float32, mybir.dt.float32r
    ALU, ACT, AX = mybir.AluOpType, mybir.ActivationFunctionType, mybir.AxisListType
    ctx = ExitStack()
    with ctx:
        place = [((nc.sbuf_base + 31) // 32) * 32]

        def at(name, shape, dt, offset):
            return nc.alloc_sbuf_tensor_at(name, shape, dt, offset=offset)

        def sb(name, shape, dt=F32):
            o = place[0]
            place[0] += ((int(np.prod(shape[1:])) * 4 + 31) // 32) * 32
            return at(name, shape, dt, o)

        def sem(name):
            return ctx.enter_context(nc.semaphore(name))

        xT = sb("xT", [P, KT, T])
        hhi = sb("hhi", [P, KT, T], F32R)
        hlo = sb("hlo", [P, KT, T], F32R)
        stage = sb("stage", [P, RING, KT, P])
        whi = sb("whi", [P, RING, KT, P], F32R)
        wlo = sb("wlo", [P, RING, KT, P], F32R)
        nconst = max(b for _, b in const_cols.values())
        const_at = place[0]
        const = sb("const", [P, nconst])
        K = {n: const[:, a:b] for n, (a, b) in const_cols.items()}
        vec = sb("vec", [P, NVEC])
        mod = sb("mod", [P, 4 * KT])
        cact = sb("cact", [P, KT])
        V = {n: vec[:, VEC_AT[n]:VEC_AT[n] + r] for n, r in VEC_ROWS.items()}
        act_at = place[0]
        ahi = [sb("ahi0", [P, KT, T], F32R), None]
        alo = [sb("alo0", [P, KT, T], F32R), None]
        scratch = place[0]
        ahi[1] = sb("ahi1", [P, KT, T], F32R)
        alo[1] = sb("alo1", [P, KT, T], F32R)
        mlp_end = place[0]

        place[0] = scratch
        convw = sb("convw", [P, 12, H])
        gates = sb("gates", [P, H, 4, CH])
        glog = sb("glog", [P, CH, H])
        qT = [sb(f"qT{b}", [P, T]) for b in range(2)]
        kT = [sb(f"kT{b}", [P, T]) for b in range(2)]
        vT = sb("vT", [P, T])
        zs = sb("zs", [P, T])
        acc = sb("acc", [P, T])
        th = sb("th", [P, T])
        sq = sb("sq", [P, 2, T])
        gd = sb("gd", [P, CH, P])
        gcol = sb("gcol", [P, CH])
        dec = sb("dec", [P, CH, P])
        decT = sb("decT", [P, CH, P])
        cols = [sb(f"cols{b}", [P, 12, CH]) for b in range(2)]
        low = sb("low", [P, CH, P])
        attnT = sb("attnT", [P, CH, P])
        kbeta = sb("kbeta", [P, CH, P])
        kdec = sb("kdec", [P, CH, P])
        vbeta = sb("vbeta", [P, CH, P])
        NB = 3
        lev = sb("lev", [P, NB, CH, P])
        inv = sb("inv", [P, CH, P])
        invTs = [sb(f"invT{b}", [P, CH, P]) for b in range(2)]
        qlev = {s: sb(f"qlev{s}", [P, CH, P]) for s in LEVELS[1:]}
        wT = sb("wT", [P, CH, P])
        vnew = sb("vnew", [P, CH, P])
        state = sb("state", [P, 2, P])
        o1 = sb("o1", [P, P])
        onat = sb("onat", [P, CH, P])
        osq = sb("osq", [P, CH, P])
        gf = sb("gf", [P, T])
        dn_end = place[0]
        place[0] = mlp_end
        nsq = sb("nsq", [P, 2, T])
        rs1, rr1 = sb("rs1", [P, T]), sb("rr1", [P, T])
        hf1 = sb("hf1", [P, 2, T])
        relu = sb("relu", [P, 2, T])
        af = hf1
        mod_w = sb("mod_w", [P, 3 * D])
        mod_acc = sb("mod_acc", [P, 3 * D])
        I32, BF16 = mybir.dt.int32, mybir.dt.bfloat16
        place[0] = act_at
        const2 = sb("const2", [P, max(b for _, b in const2_cols.values())])
        K2 = {n: const2[:, a:b] for n, (a, b) in const2_cols.items()}
        q2T_at = place[0]
        q2T = sb("q2T", [P, 4, T])
        kT2_at = place[0]
        kT2 = [sb(f"kT2_{b}", [P, T]) for b in range(2)]
        v2 = [sb(f"v2_{b}", [P, CH, P]) for b in range(2)]
        table = sb("table", [P, 4, T])
        cn = sb("cn", [P, 3, T])
        krT_at = place[0]
        krT = sb("krT", [P, T])
        identb, negb = sb("identb", [P, P], BF16), sb("negb", [P, P], BF16)
        gate2 = sb("gate2", [P, CH, 3 * QH])
        cposT = sb("cposT", [P, CMP_BLOCK])
        cpos = sb("cpos", [P, P])
        kcr = sb("kcr", [P, 2, NCP])
        ktmp = sb("ktmp", [P, 3, 2, NCP])
        hid = sb("hid", [P, 2, 2, 2, NCP])
        hid4 = sb("hid4", [P, 2, 4, NCP])
        vbd = sb("vbd", [P, 2, 4, DK])
        csm = sb("csm", [P, 4, 32])
        amax = sb("amax", [P, 8])
        aneg = sb("aneg", [P, 8])
        asum = sb("asum", [P, 8])
        ainv = sb("ainv", [P, 8])
        acoef = sb("acoef", [P, 8])
        w2c = sb("w2c", [P, 3, DK])
        small = place[0]
        raw = sb("raw", [P, 3, T])
        rcos = sb("rcos", [P, 2, T])
        rsin = sb("rsin", [P, T])
        csq = sb("csq", [P, 2, T])
        place[0] = small
        zs2 = sb("zs2", [P, KT, T])
        over = place[0]
        w1 = [sb(f"w1_{b}", [P, CMP_BLOCK, CMP_HID]) for b in range(2)]
        xb = sb("xb", [P, CMP_BLOCK, 2, NCP])
        kcT, vcT = (at(n, [P, T], F32, const_at + (const_cols["upto"][0] + b * T) * 4)
                    for b, n in enumerate(("kcT", "vcT")))
        turn = at("turn", [P, 4, T], F32, q2T_at)
        ang = at("ang", [P, 2, T], F32, kT2_at)
        pos_i = at("pos_i", [P, T], I32, krT_at)
        place[0] = over
        o_nsa = sb("o_nsa", [P, CH, QW])
        qm = sb("qm", [P, 2, T])
        km = sb("km", [P, 2, T])
        csc = at("csc", [P, 2, T], F32, place[0] - 4 * T * 4)
        cpT = at("cpT", [P, 2, T], F32, place[0] - 2 * T * 4)
        qh = sb("qh", [P, 2, T])
        zth = sb("zth", [P, T])
        prob = sb("prob", [P, 2, T])
        probT = sb("probT", [P, 2, T])
        v_mla = sb("v_mla", [P, CH, QW])
        wq = sb("wq", [P, 2, 2, MD])
        wk = sb("wk", [P, 2, MN])
        wv = sb("wv", [P, QH, DK])
        gated = sb("gated", [P, 2, T])
        o_mla = at("o_mla", [P, CH, QW], F32, kT2_at)
        qraw = at("qraw", [P, 2, T], F32, q2T_at)
        qcos, qsin = (at(n, [P, T], F32, q2T_at + (2 + b) * T * 4) for b, n in enumerate(("qcos", "qsin")))
        place[0] = act_at
        onorm = sb("onorm", [P, 2, T])
        osqr = sb("osqr", [P, 2, T])
        ors, orr = sb("ors", [P, T]), sb("orr", [P, T])
        y = sb("y", [P, CH, D])
        assert place[0] <= small
        place[0] = act_at
        xn = sb("xn", [P, CH, D])
        rows = sb("rows", [P, 2, P])
        sqn = sb("sqn", [P, 2, T])
        rs = sb("rs", [P, T])
        rr = sb("rr", [P, T])
        hf = sb("hf", [P, 2, T])
        ba = sb("ba", [P, T])
        batok = sb("batok", [P, CH, 16])
        gtmp = sb("gtmp", [P, 4, CH, H])
        dtb = sb("dtb", [P, 2, H])
        assert place[0] <= scratch
        ps = ctx.enter_context(nc.psum_tensor("ps", [P, 8, T], F32))
        U = [ps[:, 0, :], ps[:, 1, :]]

        s = {}
        for name in """const_in x_in vec_in vec_tr vec_col xtr xev out_done w_hi w_lo w_used n_sq n_stat n_sqrt n_rstd
            n_h n_hi n_lo ba_ev ba_tr ba_col gate_in gate_act gate_dve gate_ps gate_ready half_ready conv0
            conv1 tanh seq_ready ztanh z_ready dz_in g_col dps dexp dmask sqs ss_ps norm_dve norm_act kk_ps
            kn_ps low_ready attn_ready kside lev_ready inv_ps inv_ready q_zero q_ps q_ev r_ps vn_ps vb_ready
            mod_c mod_in mod_done c2_in pos_in cpos_in w2_in wv_in act_steps dve_steps pool_steps pe_steps
            e_sq e_add z_th z_done xa_done q_staged at_s at_max at_neg at_exp at_t at_tev at_o at_inv
            at_coef at_done p_ps p_ev p_rot p_cos p_sin p_q w_ps w_ev mlp_relu mlp_f mlp_hi mlp_lo v_ps v_ev
            st_ps st_ready o_ps o1_ps o1_ev o_ready o_stat o_act o_scaled o_tr g_f g_hi g_lo res""".split():
            s[name] = sem(name)
        w_in = [sem(f"w_in{r}") for r in range(RING)]
        w1_in = [sem(f"w1_in{b}") for b in range(2)]
        wq_in = [sem(f"wq_in{b}") for b in range(2)]

        tiles = range(KT)
        STEPS = {
            "pe": ["modulation", "square sums", "positions turned"]
                  + ["aux gate", "aux vs", "aux vw", "aux q0", "hidden k", "aux q1", "aux q2", "hidden v", "aux q3",
                     "aux ks", "second layer", "aux kw", "rotate kc", "block scores", "sum cq", "aux kr", "sum ckv",
                     "block turned", "block values"] + [f"turned {k}" for k in range(KH)] + ["latent values"]
                  + [f"turned {k}" for k in range(KH, KT)]
                  + [f"out sums {k}" for k in tiles] + [f"back {k}" for k in tiles],
            "act": ["root 2", "root 1"] + [f"h high {k}" for k in tiles]
                   + ["ev kc", "ev vc", "ev gate", "ev vs", "ev vw", "gate tanh", "ev q0", "tables", "ev q1", "ev q2",
                      "tanh k", "ev q3", "ev ks", "tanh v", "ev kw", "ev cq0", "ev cq1", "square cq0", "square cq1",
                      "ev ckv", "block exp", "ev kr", "root cq", "square ckv", "root ckv", "block turned"]
                   + [f"mix high {k}" for k in range(KH)] + ["latent values"]
                   + [f"mix high {k}" for k in range(KH, KT)] + [f"out squares {k}" for k in tiles] + ["out root"]
                   + [f"out rows {k}" for k in tiles],
            "pool": ["window zero", "block zero"]
                    + [f"cos {n}" for n in ROPE] + [f"mix low {k}" for k in tiles],
            "dve": ["mod", "mod gain 1", "mod gain 2", "var 1", "var 2", "inv 2"]
                   + ["h 0"] + [f"{what} {k - d}" for k in range(1, KT) for what, d in (("h", 0), ("norm low", 1))]
                   + [f"norm low {KT - 1}", "inv 1"] + [f"x normed {k}" for k in tiles]
                   + ["bf16"] + [f"table {n}" for n in range(9)] + ["positions", "post gate", "post vs", "post vw", "window k",
                      "gates", "sin q0", "post q0", "window v", "sin q1", "post q1", "hidden k", "sin q2", "post q2",
                      "sin q3", "post q3", "hidden v", "hidden v 4", "sin ks", "post ks", "kc", "block values", "kc cos",
                      "sin kw", "post kw", "kc sin", "kc rotated", "scaled", "max", "less max", "sum", "seen", "sum inv",
                      "coef", "probs", "sin kr", "post kr", "inv cq", "cq 0", "cq 1", "inv ckv", "ckv", "block out"]
                   + [f"mixed {k}" for k in range(KH)] + ["rotated keys"]
                   + [f"mixed {k}" for k in range(KH, KT)] + [f"x {k}" for k in tiles] + ["out inv"] + [f"y {k}" for k in tiles],
        }
        assert all(len(set(v)) == len(v) for v in STEPS.values())

        def step_count(who, name):
            return STEPS[who].index(name) + 1

        def lane(who):
            count = [0]

            def done(ins, name):
                assert STEPS[who][count[0]] == name, (who, STEPS[who][count[0]], name)
                count[0] += 1
                ins.then_inc(s[who + "_steps"], 1)
            return done

        def after(eng, who, name):
            eng.wait_ge(s[who + "_steps"], step_count(who, name))

        def bc(col_ap, n):
            return col_ap.unsqueeze(2).broadcast_to([P, col_ap.shape[1], n])

        def bc_mid(block, n):
            return block.unsqueeze(1).broadcast_to([P, n, block.shape[1]])

        def known(x, v):
            return isinstance(x, int) and x == v

        w_in_T = A["dn_w_in"][0].rearrange("(k p) c -> p k c", p=P)
        w_out_T = A["dn_w_out"][0].rearrange("(k p) c -> p k c", p=P)
        w_up_T = A["mlp_w_up"][0].rearrange("(k p) c -> p k c", p=P)
        w_down_T = A["mlp_w_down"][0].rearrange("(q k p) c -> q p k c", p=P, k=KT)
        FN = 4 * D
        BA_N = BA_LEAD + 16
        Q, KK_, VV, ZZ = range(4)
        w_in2_T = A["w_in_2"][0].rearrange("(k p) c -> p k c", p=P)
        w_out2_T = A["w_out_2"][0].rearrange("(k p) c -> p k c", p=P)
        SCALE, SCALE_M = DK ** -0.5, MD ** -0.5

        def seen_by(name):
            return K2[name].rearrange("p (q n) -> p q n", n=NCP).unsqueeze(2).broadcast_to([P, CH, 4, NCP])

        def by_head(t):
            return t.rearrange("p (q h n) -> p q h n", q=CH, n=NCP)

        def windows(t, w):
            v = t.rearrange("p (n l) -> p n l", l=CMP_STRIDE)
            return v[:, w:w + NC, :].rearrange("p n l -> p l n")

        def level_halves(block, lv, odd):
            return block.rearrange("p (b o l) -> p b o l", o=2, l=lv)[:, :, odd, :]

        TURNS = [("q", 0), ("k", 0), ("rot", 0)]
        for i in range(16):
            TURNS.append(("s", i))
            if i < 12 and i % 4 == 0:
                TURNS += [("q", i // 4 + 1), ("k", i // 4 + 1)]
            if i < 12 and i % 4 == 1:
                TURNS.append(("rot", i // 4 + 1))

        def turn_bank(what, i):
            return 2 + TURNS.index((what, i)) % 3

        def score_bank(i):
            return 2 + i % 3

        block = ctx.enter_context(nc.Block())

        @block.sync
        def _(sp):
            for c in range(CH):
                sp.dma_start(xn[:, c, :], A["x"][0, c * P:(c + 1) * P, :]).then_inc(s["x_in"], 16)
                if c == 0:
                    sp.dma_start(const[:, :], A["consts"]).then_inc(s["const_in"], 16)
            for name, r in VEC_ROWS.items():
                src = A[name]
                if len(src.shape) == 2:
                    src = src.rearrange("a c -> (a c)")
                sp.dma_start(rows[VEC_AT[name]:VEC_AT[name] + r, 0, :],
                             src.rearrange("(r p) -> r p", p=P)).then_inc(s["vec_in"], 16)
            for tap in range(4):
                sp.dma_start(rows[tap * 24:(tap + 1) * 24, 1, :],
                             A["dn_conv_w"][0, tap].rearrange("(r p) -> r p", p=P)).then_inc(s["vec_in"], 16)
            sp.dma_start(dtb[:, 0, :], A["dn_dt_bias"].broadcast_to([P, H])).then_inc(s["gate_in"], 16)
            sp.dma_start(dtb[:, 1, :], A["dn_a_log"].broadcast_to([P, H])).then_inc(s["gate_in"], 16)

            def load(n, slot, src, cols=P, ks=KT):
                if not isinstance(n, int) or n >= RING:
                    sp.wait_ge(s["w_lo"], n - RING + 1)
                sp.dma_start(stage[:, slot, 0:ks, 0:cols], src).then_inc(w_in[slot], 16)

            load(0, 0, w_in_T[:, :, 0:P])
            load(1, 1, w_in_T[:, :, D:D + P])
            load(2, 2, w_in_T[:, :, FN - BA_LEAD:FN + 16], BA_N)
            load(3, 3, w_in_T[:, :, 2 * D:2 * D + P])
            with sp.Fori(0, H - 1) as h:
                for j, (sec, ahead) in enumerate(((Q, 1), (KK_, 1), (ZZ, 0), (VV, 1))):
                    load(h * 4 + 4 + j, j, w_in_T[:, :, bass.ds((h + ahead) * P + sec * D, P)])
            load(DN_UNITS - 1, (DN_UNITS - 1) % RING, w_in_T[:, :, 3 * D + 7 * P:4 * D])
            for m in range(KT):
                load(U_OUT + m, (U_OUT + m) % RING, w_out_T[:, :, m * P:(m + 1) * P])
            sp.wait_ge(s["w_used"], U_OUT + 1)
            ada_T = A["ada_w_2"][0].rearrange("(k p) c -> p k c", p=P)

            def mod_rows(kk):
                sp.wait_ge(s["mod_done"], kk * 3 + 3)
                sp.dma_start(mod_w[:, :], ada_T[:, bass.ds(kk, 1), :].rearrange("p a c -> p (a c)"))\
                    .then_inc(s["mod_in"], 16)

            with sp.Fori(0, QUARTERS) as q:
                mod_rows(q * 2)
                for m in range(KT):
                    load(U_MLP + q * 16 + m, (U_MLP + m) % RING, w_up_T[:, :, bass.ds(q * D + m * P, P)])
                for m in range(KT):
                    load(U_MLP + q * 16 + KT + m, (U_MLP + m) % RING,
                         w_down_T[bass.ds(q, 1), :, :, m * P:(m + 1) * P].rearrange("a p k c -> p (a k) c"))
                    if m == 1:
                        mod_rows(q * 2 + 1)
            first_col = {"kc": AT_KC, "vc": AT_VC, "gate": AT_GATE, "vs": AT_VS, "vw": AT_VW, "cq0": AT_CQ, "cq1": AT_CQ + P,
                         "ckv": AT_CKV, "kr": AT_KR - MN, "ks": AT_KS, "kw": AT_KW}
            for a, name in enumerate(TWO):
                n = U_TWO + a
                if name[0] == "q":
                    m = int(name[1])
                    sp.wait_ge(s["w_lo"], n - RING + 1)
                    for half in range(2):
                        c = m * DK + half * 4 * DK
                        sp.dma_start(stage[:, n % RING, :, half * DK:(half + 1) * DK], w_in2_T[:, :, c:c + DK])\
                            .then_inc(w_in[n % RING], 16)
                else:
                    c = first_col[name]
                    load(n, n % RING, w_in2_T[:, :, c:c + P])
                if a == RING - 1:
                    sp.wait_ge(s["w_used"], U_TWO)
                    sp.dma_start(const2[:, :], A["consts2"]).then_inc(s["c2_in"], 16)
                    sp.dma_start(pos_i[:, :], A["positions_2"].broadcast_to([P, T])).then_inc(s["pos_in"], 16)
                    for half in range(2):
                        sp.dma_start(cpos[0:CMP_BLOCK, half * DK:(half + 1) * DK], A["cmp_pos_2"][0]).then_inc(s["cpos_in"], 16)
                    for n, name in enumerate(("k", "k", "v")):
                        sp.dma_start(w2c[:, n], A[f"cmp_{name}_w2_2"][0]).then_inc(s["w2_in"], 16)
                if a == 6:
                    after(sp, "dve", f"x normed {KT - 1}")
                    for w, name1 in enumerate(("k", "v")):
                        for half in range(2):
                            sp.dma_start(w1[w][half * DK:(half + 1) * DK],
                                         A[f"cmp_{name1}_w1_2"][0].rearrange("(l d) h -> d l h", d=DK)).then_inc(w1_in[w], 16)
            for m in range(4):
                load(U_Z + m, (U_Z + m) % RING, w_in2_T[:, :, AT_Z + m * P:AT_Z + (m + 1) * P])
            after(sp, "dve", "block out")
            kv_up = A["w_kv_up_2"][0].rearrange("r (h c) -> r h c", c=MN + DK)
            q_up = A["w_q_up_2"][0].rearrange("(k p) (h c) -> h p k c", p=P, c=MD)
            k_up = A["w_kv_up_2"][0].rearrange("r (h c) -> h r c", c=MN + DK)
            sp.dma_start(wv[:, :, :], kv_up[:, :, MN:]).then_inc(s["wv_in"], 16)

            def latent_weights(h, par, wait=True):
                if wait:
                    sp.wait_ge(s["p_ps"], h - 1)
                sp.dma_start(wq[:, par], q_up[bass.ds(h, 1)].rearrange("h p k c -> p (h k) c")).then_inc(wq_in[par], 16)
                sp.dma_start(wk[:, par], k_up[bass.ds(h, 1), :, 0:MN].rearrange("h r c -> r (h c)")).then_inc(wq_in[par], 16)

            latent_weights(0, 0, False)
            latent_weights(1, 1, False)
            for m in range(4):
                load(U_Z + 4 + m, (U_Z + m) % RING, w_in2_T[:, :, AT_ZM + m * P:AT_ZM + (m + 1) * P])

            def out_tile(u):
                m, k0 = u % KT, u // KT * KH
                load(U_OUT2 + u, u % RING, w_out2_T[:, k0:k0 + KH, m * P:(m + 1) * P], ks=KH)

            for u in range(2 * RING):
                out_tile(u)
            for h in range(2, QH):
                latent_weights(h, h % 2)
                out_tile(6 + h)
            out_tile(2 * KT - 2)
            out_tile(2 * KT - 1)
            for half in range(2):
                after(sp, "act", f"out rows {half * 4 + 3}")
                for c in range(CH):
                    sp.dma_start(out[c * P:(c + 1) * P, half * 512:(half + 1) * 512],
                                 y[:, c, half * 512:(half + 1) * 512]).then_inc(s["out_done"], 16)
            sp.wait_ge(s["out_done"], 16 * 2 * CH)

        @block.scalar
        def _(act):
            def split_hi(n, slot, cols=P, halves=0, ks=KT):
                if isinstance(n, int) and n >= U_TWO + TWO.index("q0"):
                    halves = 16
                act.wait_ge(w_in[slot], (n - slot) * (16 // RING) + 16 + halves)
                if not isinstance(n, int) or n >= RING:
                    act.wait_ge(s["w_used"], n - RING + 1)
                act.activation(whi[:, slot, 0:ks, 0:cols], stage[:, slot, 0:ks, 0:cols], ACT.Copy).then_inc(s["w_hi"], 1)

            def norm_squares(m, k):
                if m * KT + k >= 2:
                    act.wait_ge(s["n_stat"], m * KT + k - 1)
                act.activation(sqn[:, k % 2], xT[:, k], ACT.Square).then_inc(s["n_sq"], 1)

            def norm_rest(m):
                act.wait_ge(s["n_stat"], (m + 1) * KT)
                act.activation(rs[:, :], ps[:, 2, :], ACT.Sqrt, bias=K["eps"][:, 0:1]).then_inc(s["n_sqrt"], 1)

            def norm_hi(m):
                for k in range(KT):
                    act.wait_ge(s["n_h"], m * KT + k + 1)
                    act.activation(hhi[:, k], hf[:, k % 2], ACT.Copy).then_inc(s["n_hi"], 1)

            act.wait_ge(s["const_in"], 16)
            for k in range(KT):
                act.wait_ge(s["xtr"], k + 1)
                act.activation(xT[:, k], ps[:, 3 + k % 4, :], ACT.Copy).then_inc(s["xev"], 1)
                act.wait_ge(s["xev"], k + 1)
                norm_squares(0, k)
            norm_rest(0)
            split_hi(0, 0)
            split_hi(1, 1)
            split_hi(2, 2, BA_N)
            norm_hi(0)
            split_hi(3, 3)

            def tap0(h, seq):
                u = h * 3 + seq
                act.wait_ge(s["w_used"], h * 4 + (0, 1, 3)[seq] + 1)
                if not known(u, 0):
                    act.wait_ge(s["seq_ready"], u)
                act.activation(acc[:, :], ps[:, (0, 1, 1)[seq], :], ACT.Copy,
                               scale=convw[:, 9 + seq, bass.ds(h, 1)]).then_inc(s["conv0"], 1)

            def seq_tanh(h, seq):
                act.wait_ge(s["conv1"], (h * 3 + seq) * 3 + 3)
                act.activation(th[:, :], acc[:, :], ACT.Tanh, scale=0.5).then_inc(s["tanh"], 1)

            def squares(h, w, src):
                act.wait_ge(s["seq_ready"], h * 3 + w + 1)
                if not known(h, 0):
                    act.wait_ge(s["ss_ps"], h)
                act.activation(sq[:, w], src[:, :], ACT.Square).then_inc(s["sqs"], 1)

            act.wait_ge(s["vec_col"], 2)
            tap0(0, 0)
            seq_tanh(0, 0)
            squares(0, 0, qT[0])
            split_hi(4, 0)
            tap0(0, 1)
            seq_tanh(0, 1)
            squares(0, 1, kT[0])
            split_hi(5, 1)
            act.wait_ge(s["gate_in"], 32)
            act.activation(dtb[:, 1, :], dtb[:, 1, :], ACT.Exp).then_inc(s["gate_act"], 1)
            act.wait_ge(s["ba_col"], 1)
            act.activation(gtmp[:, 0], batok[:, :, 0:H], ACT.Tanh, scale=0.5).then_inc(s["gate_act"], 1)
            act.wait_ge(s["gate_dve"], 2)
            act.activation(gtmp[:, 2], gtmp[:, 2], ACT.Exp, scale=-1.0).then_inc(s["gate_act"], 1)
            act.wait_ge(s["gate_act"], 3)
            act.activation(gtmp[:, 2], gtmp[:, 2], ACT.Ln, bias=1.0).then_inc(s["gate_act"], 1)
            act.wait_ge(s["gate_ps"], 1)
            for n in range(3):
                act.activation(gates[:, :, 1 + n, :].rearrange("p h c -> p c h"),
                               ps[:, 4, 32 * n:32 * n + 32].rearrange("p (c h) -> p c h", h=H),
                               ACT.Exp).then_inc(s["gate_ready"], 1)
            act.activation(cact[:, :], V["c_2"], ACT.Tanh, scale=0.5).then_inc(s["mod_c"], 1)
            split_hi(6, 2)

            def decays(h, w):
                act.wait_ge(s["dps"], h * 2 + w + 1)
                if not known(h, 0):
                    act.wait_ge(s["attn_ready"], h) if w else act.wait_ge(s["low_ready"], h * 4)
                act.activation((dec, decT)[w][:, :, :], ps[:, 4 + w, :].rearrange("p (c i) -> p c i", c=CH), ACT.Exp)\
                    .then_inc(s["dexp"], 1)

            def norm_roots(h, col):
                act.wait_ge(s["norm_dve"], h * 5 + 2)
                act.activation(col[:, 2:4, :], col[:, 0:2, :], ACT.Sqrt).then_inc(s["norm_act"], 1)

            def out_root(h, col):
                act.wait_ge(s["o_stat"], h * 5 + 3)
                act.activation(col[:, 9, :], col[:, 8, :], ACT.Sqrt, scale=float(P) ** -2, bias=K["eps"][:, 0:1])\
                    .then_inc(s["o_act"], 1)

            def out_hi(h):
                act.wait_ge(s["g_f"], h + 1)
                act.activation(ahi[0][:, bass.ds(h, 1), :], gf[:, :].unsqueeze(1), ACT.Copy).then_inc(s["g_hi"], 1)

            def level(h, li):
                if known(h, 0):
                    act.wait_ge(s["q_zero"], NL - 1)
                act.wait_ge(s["q_ps"], h * 6 + li)
                lv = LEVELS[li]
                act.activation(qlev[lv][:, :, :].rearrange("p c (b o l) -> p (c b) o l", o=2, l=lv)[:, :, 1, :],
                               ps[:, 4, 0:CH * 64].rearrange("p (b l) -> p b l", l=lv), ACT.Copy)\
                    .then_inc(s["q_ev"], 1)

            def head(h, par, last):
                first = known(h, 0)
                level(h, 1)
                if not first:
                    out_root(h - 1, cols[1 - par])
                norm_roots(h, cols[par])
                level(h, 2)
                if not first:
                    out_hi(h - 1)
                level(h, 3)
                tap0(h, 2)
                level(h, 4)
                seq_tanh(h, 2)
                split_hi(h * 4 + 7, 3)
                level(h, 5)
                if not last:
                    tap0(h + 1, 0)
                level(h, 6)
                if not last:
                    seq_tanh(h + 1, 0)
                act.wait_ge(s["w_ps"], h + 1)
                act.activation(wT[:, :, :], ps[:, 5, :].rearrange("p (c i) -> p c i", c=CH), ACT.Copy, scale=-1.0)\
                    .then_inc(s["w_ev"], 1)
                for c in range(CH):
                    act.wait_ge(s["v_ps"], h * 4 + c + 1)
                    act.activation(vnew[:, c, :], ps[:, 3, 0:P], ACT.Copy).then_inc(s["v_ev"], 1)
                    if c:
                        act.wait_ge(s["o1_ps"], h * 3 + c)
                        if c > 1:
                            act.wait_ge(s["o_ready"], h * 4 + c)
                        act.activation(o1[:, :], ps[:, 3, P:2 * P], ACT.Copy,
                                       scale=gates[:, bass.ds(h, 1), 1, c]).then_inc(s["o1_ev"], 1)
                    if last:
                        continue
                    if c == 0:
                        tap0(h + 1, 1)
                        split_hi(h * 4 + 8, 0)
                        squares(h + 1, 0, qT[1 - par])
                    if c == 1:
                        decays(h + 1, 0)
                        seq_tanh(h + 1, 1)
                        decays(h + 1, 1)
                    if c == 2:
                        squares(h + 1, 1, kT[1 - par])
                        split_hi(h * 4 + 9, 1)
                zn = DN_UNITS - 1 if last else h * 4 + 6
                act.wait_ge(s["w_used"], zn + 1)
                act.activation(th[:, :], ps[:, 0, :], ACT.Tanh, scale=0.5).then_inc(s["ztanh"], 1)
                if last:
                    split_hi(DN_UNITS + 3, (DN_UNITS + 3) % RING)
                else:
                    split_hi(h * 4 + 10, 2)

            decays(0, 0)
            decays(0, 1)
            head(0, 0, False)
            with act.Fori(0, H // 2 - 1) as j:
                head(j * 2 + 1, 1, False)
                head(j * 2 + 2, 0, False)
            head(H - 1, 1, True)
            out_root(H - 1, cols[1])
            out_hi(H - 1)

            def next_hi(n, slot):
                split_hi(n + RING, slot)

            def squares1(m, k):
                act.wait_ge(s["res"], k + 1)
                if k >= 2:
                    act.wait_ge(s["n_stat"], m * KT + k - 1)
                act.activation(nsq[:, k % 2], xT[:, k], ACT.Square).then_inc(s["n_sq"], 1)

            for m in range(KT):
                next_hi(U_OUT + m, (U_OUT + m) % RING)
                squares1(1, m)
            act.wait_ge(s["n_stat"], 2 * KT)
            act.activation(rs1[:, :], ps[:, 2, :], ACT.Sqrt, bias=K["eps"][:, 0:1]).then_inc(s["n_sqrt"], 1)
            for k in range(KT):
                act.wait_ge(s["n_h"], KT + k + 1)
                act.activation(hhi[:, k], hf1[:, k % 2], ACT.Copy).then_inc(s["n_hi"], 1)

            def quarter(q, par):
                n0 = U_MLP + q * 16

                def hidden_hi(m):
                    act.wait_ge(s["mlp_f"], q * KT + m + 1)
                    act.activation(ahi[par][:, m], af[:, m % 2], ACT.Copy).then_inc(s["mlp_hi"], 1)

                for m in range(KT):
                    act.wait_ge(s["w_used"], n0 + m + 1)
                    if m >= 2:
                        act.wait_ge(s["mlp_f"], q * KT + m - 1)
                    act.activation(relu[:, m % 2], ps[:, (U_MLP + m) % 2, :], ACT.Relu).then_inc(s["mlp_relu"], 1)
                    next_hi(n0 + m, (U_MLP + m) % RING)
                    hidden_hi(m)
                for m in range(KT):
                    next_hi(n0 + KT + m, (U_MLP + m) % RING)
                    act.wait_ge(s["res"], q * KT + KT + m + 1)
                    if m:
                        act.wait_ge(s["e_add"], q * KT + m)
                    act.activation(nsq[:, 0], xT[:, m], ACT.Square)
                    act.activation(nsq[:, 1], xT[:, m], ACT.Square, scale=V["norm_final"][:, m:m + 1])\
                        .then_inc(s["e_sq"], 1)

            with act.Fori(0, QUARTERS // 2) as j:
                quarter(j * 2, 0)
                quarter(j * 2 + 1, 1)

            done = lane("act")
            after(act, "dve", "var 2")
            done(act.activation(hf1[:, 1], hf1[:, 0], ACT.Sqrt), "root 2")
            done(act.activation(rs1[:, :], ps[:, 2, :], ACT.Sqrt, bias=K["eps"][:, 0:1]), "root 1")
            for k in range(KT):
                after(act, "dve", f"h {k}")
                done(act.activation(hhi[:, k], relu[:, k % 2], ACT.Identity, bias=mod[:, k:k + 1]), f"h high {k}")
            raw_of = {n: x % 3 for x, n in enumerate(AUX)}
            for a, name in enumerate(TWO):
                act.wait_ge(s["w_used"], U_TWO + a + 1)
                src = ps[:, (U_TWO + a) % 2, :]
                if name in ("kc", "vc"):
                    dst = (kcT, vcT)[a][:, :]
                elif name[0] == "c":
                    dst = cn[:, a - TWO.index("cq0")]
                else:
                    x = AUX.index(name)
                    if x >= 3:
                        after(act, "dve", f"post {AUX[x - 3]}")
                    dst = raw[:, x % 3]
                done(act.activation(dst, src, ACT.Copy), f"ev {name}")
                split_hi(U_TWO + a + RING, (U_TWO + a) % RING)
                if name == "vw":
                    after(act, "dve", "post gate")
                    done(act.activation(gate2[:, :, :], gate2[:, :, :], ACT.Tanh, scale=0.5), "gate tanh")
                if name == "q0":
                    after(act, "dve", "table 8")
                    done(act.activation(table[:, :, :], table[:, :, :], ACT.Sin), "tables")
                if name in ("q2", "ks"):
                    w = ("q2", "ks").index(name)
                    after(act, "pe", f"hidden {'kv'[w]}")
                    done(act.activation(hid[:, w, 0], ps[:, 4 + w, 0:2 * NCP].rearrange("p (g n) -> p g n", g=2),
                                        ACT.Tanh, scale=0.5), f"tanh {'kv'[w]}")
                if name == "cq1":
                    after(act, "act", "ev cq1")
                    for w in range(2):
                        done(act.activation(csq[:, w], cn[:, w], ACT.Square), f"square cq{w}")
                if name == "ckv":
                    after(act, "dve", "less max")
                    done(act.activation(csc[:, :, :], csc[:, :, :], ACT.Exp), "block exp")
            after(act, "pe", "sum cq")
            done(act.activation(prob[:, 0], ps[:, 6, :], ACT.Sqrt, scale=4.0, bias=K["eps"][:, 0:1]), "root cq")
            after(act, "act", "ev ckv")
            done(act.activation(csq[:, 0], cn[:, 2], ACT.Square), "square ckv")
            after(act, "pe", "sum ckv")
            done(act.activation(probT[:, 0], ps[:, 7, :], ACT.Sqrt, scale=8.0, bias=K["eps"][:, 0:1]), "root ckv")
            after(act, "pe", "block turned")
            done(act.activation(cpT[:, :, :], ps[:, 6:8, :], ACT.Copy), "block turned")

            def soft(i, n, exp_scale, keys, bank):
                act.wait_ge(s["at_neg"], n + 1)
                if i >= 2:
                    act.wait_ge(s["at_t"], n - 1)
                    act.wait_ge(s["at_inv"], n - 1)
                act.activation(prob[:, i % 2, 0:keys], ps[:, bank, 0:keys], ACT.Exp, scale=exp_scale,
                               bias=aneg[:, i % 2:i % 2 + 1], accum_out=asum[:, i % 2:i % 2 + 1]).then_inc(s["at_exp"], 1)

            def turned(i, n, keys):
                act.wait_ge(s["at_t"], n + 1)
                if i >= 2:
                    act.wait_ge(s["at_o"], n - 1)
                act.activation(probT[:, i % 2, 0:keys], ps[:, 5 + i % 2, 0:keys], ACT.Copy).then_inc(s["at_tev"], 1)

            def attend(first, count, exp_scale, between, bank_of=score_bank):
                for i in range(count + 2):
                    between(i)
                    if i < count:
                        soft(i, first + i, exp_scale, (i % 4 + 1) * P, bank_of(i))
                    if i >= 2:
                        turned(i - 2, first + i - 2, ((i - 2) % 4 + 1) * P)

            with act.Fori(0, 2) as j:
                act.wait_ge(s["at_done"], j * 32 + 1)
                for par in range(2):
                    act.activation(qh[:, par:par + 1], q2T[:, bass.ds(j * 2 + par, 1), :], ACT.Copy)\
                        .then_inc(s["q_staged"], 1)

                def between(i):
                    if i % 8 == 1 and i > 1:
                        u = i // 8 - 1
                        act.wait_ge(s["w_used"], j * 4 + U_Z + u + 1)
                        if u:
                            act.wait_ge(s["z_done"], j * 4 + u)
                        act.activation(zth[:, :], ps[:, u % 2, :], ACT.Tanh, scale=0.5).then_inc(s["z_th"], 1)
                        split_hi(j * 4 + U_Z + RING + u, u, halves=16)

                attend(j * 32, 32, SCALE, between)

            def mix_high(k):
                after(act, "dve", f"mixed {k}")
                done(act.activation(hhi[:, k], gated[:, k % 2], ACT.Copy), f"mix high {k}")

            for k in range(KH):
                mix_high(k)
            after(act, "pe", "latent values")
            done(act.activation(v_mla[:, :, :], ps[:, 0:4, :], ACT.Copy), "latent values")
            with act.Fori(0, 2) as j:
                def projected(hh):
                    act.wait_ge(s["p_ps"], j * 4 + hh + 1)
                    if hh >= 2:
                        act.wait_ge(s["p_q"], j * 4 + hh - 1)
                    act.activation(qraw[0:MD, hh % 2], ps[0:MD, turn_bank("q", hh), :], ACT.Copy)
                    act.activation(km[0:MN, hh % 2], ps[0:MN, turn_bank("k", hh), :], ACT.Copy).then_inc(s["p_ev"], 1)

                def between(i):
                    if i % 4 == 1 and i < 12:
                        projected(i // 4 + 1)
                    if i % 4 == 1 and i < 16:
                        u = i // 4
                        split_hi(j * 4 + U_OUT2 + RING + u, u, halves=16, ks=KH)

                projected(0)
                attend(j * 16 + 64, 16, SCALE_M, between, lambda i: turn_bank("s", i))
            for k in range(KH, KT):
                mix_high(k)
            for m in range(KT):
                if m < KT - RING:
                    split_hi(U_OUT2 + KT + m + RING, m % RING, ks=KH)
                after(act, "dve", f"x {m}")
                if m >= 2:
                    after(act, "pe", f"out sums {m - 2}")
                done(act.activation(osqr[:, m % 2], xT[:, m], ACT.Square), f"out squares {m}")
            after(act, "pe", f"out sums {KT - 1}")
            done(act.activation(ors[:, :], ps[:, 2, :], ACT.Sqrt, bias=K["eps"][:, 0:1]), "out root")
            for k in range(KT):
                after(act, "pe", f"back {k}")
                done(act.activation(y[:, :, k * P:(k + 1) * P], ps[:, 4 + k % 2, :].rearrange("p (c i) -> p c i", c=CH),
                                    ACT.Copy), f"out rows {k}")

        @block.gpsimd
        def _(pool):
            def split_lo(n, slot, cols=P, ks=KT):
                pool.wait_ge(s["w_hi"], n + 1)
                pool.tensor_tensor(wlo[:, slot, 0:ks, 0:cols], stage[:, slot, 0:ks, 0:cols], whi[:, slot, 0:ks, 0:cols],
                                   ALU.subtract).then_inc(s["w_lo"], 1)

            split_lo(0, 0)
            for k in range(KT):
                pool.wait_ge(s["n_hi"], k + 1)
                pool.tensor_tensor(hlo[:, k], hf[:, k % 2], hhi[:, k], ALU.subtract).then_inc(s["n_lo"], 1)
            split_lo(1, 1)
            split_lo(2, 2, BA_N)
            for lv in LEVELS[1:]:
                if lv == 2:
                    pool.wait_ge(s["n_stat"], KT)
                pool.memset(qlev[lv][:, :, :], 0.0).then_inc(s["q_zero"], 1)
            split_lo(3, 3)
            for n in range(4, 7):
                split_lo(n, n % RING)

            def decay_sums(h, w):
                if w == 0:
                    pool.wait_ge(s["g_col"], h + 1)
                else:
                    pool.wait_ge(s["dps"], h * 2 + w)
                pool.tensor_tensor(gd[:, :, :], bc_mid(K[("after", "upto")[w]], CH), bc(gcol[:, :], P), ALU.mult)\
                    .then_inc(s["dz_in"], 1)

            def decay_mask(h):
                pool.wait_ge(s["dexp"], h * 2 + 2)
                pool.tensor_tensor(decT[:, :, :], decT[:, :, :], bc_mid(K["upto"], CH), ALU.mult)\
                    .then_inc(s["dmask"], 1)

            def level(h, li):
                if li == 0:
                    pool.wait_ge(s["low_ready"], h * 4 + 4)
                if li == NB:
                    pool.wait_ge(s["inv_ready"], h * 13 + 2)
                elif li > NB:
                    pool.wait_ge(s["q_ps"], h * 6 + li - NB)
                elif not known(h, 0):
                    pool.wait_ge(s["q_ps"], h * 6)
                pool.tensor_tensor(lev[:, li % NB], low[:, :, :], bc_mid(K[f"level{LEVELS[li]}"], CH), ALU.mult)\
                    .then_inc(s["lev_ready"], 1)

            def head(h, par, last):
                for li in range(6):
                    level(h, li)
                split_lo(h * 4 + 7, 3)
                level(h, 6)
                if not last:
                    decay_sums(h + 1, 0)
                    split_lo(h * 4 + 8, 0)
                    decay_sums(h + 1, 1)
                    decay_mask(h + 1)
                    split_lo(h * 4 + 9, 1)
                    split_lo(h * 4 + 10, 2)
                else:
                    split_lo(DN_UNITS + 3, (DN_UNITS + 3) % RING)

            decay_sums(0, 0)
            decay_sums(0, 1)
            decay_mask(0)
            head(0, 0, False)
            with pool.Fori(0, H // 2 - 1) as j:
                head(j * 2 + 1, 1, False)
                head(j * 2 + 2, 0, False)
            head(H - 1, 1, True)
            for m in range(KT):
                split_lo(U_OUT + RING + m, (U_OUT + m) % RING)
            for k in range(KT):
                pool.wait_ge(s["n_hi"], KT + k + 1)
                pool.tensor_tensor(hlo[:, k], hf1[:, k % 2], hhi[:, k], ALU.subtract).then_inc(s["n_lo"], 1)

            def quarter(q, par):
                n0 = U_MLP + q * 16
                for m in range(KT):
                    split_lo(n0 + RING + m, (U_MLP + m) % RING)
                    pool.wait_ge(s["mlp_hi"], q * KT + m + 1)
                    pool.tensor_tensor(alo[par][:, m], af[:, m % 2], ahi[par][:, m], ALU.subtract)\
                        .then_inc(s["mlp_lo"], 1)
                for m in range(KT):
                    split_lo(n0 + KT + RING + m, (U_MLP + m) % RING)

            with pool.Fori(0, QUARTERS // 2) as j:
                quarter(j * 2, 0)
                quarter(j * 2 + 1, 1)

            done = lane("pool")
            for a, name in enumerate(TWO):
                split_lo(U_TWO + a + RING, (U_TWO + a) % RING)
                if a == 0:
                    after(pool, "dve", f"x normed {KT - 1}")
                    done(pool.memset(xb[:, :, :, :], 0.0), "window zero")
                    pool.memset(kcr[:, :, :], 0.0)
                    done(pool.memset(vbd[:, :, :, :], 0.0), "block zero")
                if name in ROPE:
                    r = ROPE.index(name)
                    after(pool, "act", f"ev {name}")
                    if r == 0:
                        after(pool, "act", "tables")
                    if r >= 2:
                        after(pool, "dve", f"post {ROPE[r - 2]}")
                    done(pool.tensor_tensor(rcos[:, r % 2], raw[:, AUX.index(name) % 3],
                                            table[:, 3 if name == "kr" else 1], ALU.mult), f"cos {name}")
            with pool.Fori(0, 2) as j:
                for u in range(4):
                    split_lo(j * 4 + U_Z + RING + u, u)

            def mix_low(k):
                after(pool, "act", f"mix high {k}")
                done(pool.tensor_tensor(hlo[:, k], gated[:, k % 2], hhi[:, k], ALU.subtract), f"mix low {k}")

            for k in range(KH):
                mix_low(k)
            with pool.Fori(0, 2) as j:
                for hh in range(4):
                    pool.wait_ge(s["p_ev"], j * 4 + hh + 1)
                    if hh:
                        pool.wait_ge(s["p_q"], j * 4 + hh)
                    pool.tensor_tensor(qcos[0:MD, :], qraw[0:MD, hh % 2], table[0:MD, 3], ALU.mult).then_inc(s["p_cos"], 1)
                    pool.wait_ge(s["p_cos"], j * 4 + hh + 1)
                    if hh:
                        split_lo(j * 4 + U_OUT2 + RING + hh - 1, hh - 1, ks=KH)
                split_lo(j * 4 + U_OUT2 + RING + 3, 3, ks=KH)
            for k in range(KH, KT):
                mix_low(k)
            for m in range(KT - RING):
                split_lo(U_OUT2 + KT + m + RING, m % RING, ks=KH)

        @block.vector
        def _(dve):
            dve.wait_ge(s["vec_tr"], 1)
            dve.tensor_copy(vec[:, :], ps[:, 7, 0:NVEC]).then_inc(s["vec_col"], 1)
            dve.tensor_copy(convw[:, :, :], ps[:, 7, P:P + 96].rearrange("p (a h) -> p a h", h=H))\
                .then_inc(s["vec_col"], 1)
            dve.wait_ge(s["vec_col"], 2)
            dve.tensor_scalar(V["dn_norm_w"], V["dn_norm_w"], 0.5, None, ALU.mult).then_inc(s["half_ready"], 1)

            def norm(m, gain):
                dve.wait_ge(s["n_sqrt"], m + 1)
                dve.reciprocal(rr[:, :], rs[:, :]).then_inc(s["n_rstd"], 1)
                dve.wait_ge(s["n_rstd"], m + 1)
                for k in range(KT):
                    if m * KT + k >= 2:
                        dve.wait_ge(s["n_lo"], m * KT + k - 1)
                    dve.scalar_tensor_tensor(out=hf[:, k % 2], in0=xT[:, k], scalar=gain[:, k:k + 1], in1=rr[:, :],
                                             op0=ALU.mult, op1=ALU.mult).then_inc(s["n_h"], 1)

            norm(0, V["norm_mix"])

            def tap(h, seq, t):
                u = h * 3 + seq
                dve.wait_ge(s["conv0"], u + 1) if t == 1 else dve.wait_ge(s["conv1"], u * 3 + t - 1)
                dve.scalar_tensor_tensor(out=acc[:, t:T], in0=ps[:, (0, 1, 1)[seq], 0:T - t],
                                         scalar=convw[:, (3 - t) * 3 + seq, bass.ds(h, 1)], in1=acc[:, t:T],
                                         op0=ALU.mult, op1=ALU.add).then_inc(s["conv1"], 1)

            def silu2(h, seq, dst):
                dve.wait_ge(s["tanh"], h * 3 + seq + 1)
                dve.scalar_tensor_tensor(out=dst[:, :], in0=th[:, :], scalar=1.0, in1=acc[:, :],
                                         op0=ALU.add, op1=ALU.mult).then_inc(s["seq_ready"], 1)

            for seq, dst in ((0, qT[0]), (1, kT[0])):
                for t in range(1, 4):
                    tap(0, seq, t)
                silu2(0, seq, dst)
            dve.wait_ge(s["w_used"], 3)
            dve.tensor_copy(ba[BA_LEAD:BA_N, :], ps[BA_LEAD:BA_N, 0, :]).then_inc(s["ba_ev"], 1)
            dve.wait_ge(s["ba_tr"], 1)
            dve.tensor_copy(batok[:, :, :], ps[:, 5, 0:CH * 16].rearrange("p (c n) -> p c n", c=CH))\
                .then_inc(s["ba_col"], 1)
            dve.wait_ge(s["ba_col"], 1)
            dve.wait_ge(s["gate_in"], 32)
            dve.tensor_tensor(gtmp[:, 1], batok[:, :, H:2 * H], bc_mid(dtb[:, 0, :], CH), ALU.add)\
                .then_inc(s["gate_dve"], 1)
            dve.wait_ge(s["gate_dve"], 1)
            dve.scalar_tensor_tensor(out=gtmp[:, 2], in0=gtmp[:, 1], scalar=-1.0, in1=gtmp[:, 1],
                                     op0=ALU.mult, op1=ALU.max).then_inc(s["gate_dve"], 1)
            dve.wait_ge(s["gate_act"], 4)
            dve.scalar_tensor_tensor(out=gtmp[:, 3], in0=gtmp[:, 1], scalar=0.0, in1=gtmp[:, 2],
                                     op0=ALU.max, op1=ALU.add).then_inc(s["gate_dve"], 1)
            dve.wait_ge(s["gate_dve"], 3)
            dve.scalar_tensor_tensor(out=glog[:, :, :], in0=gtmp[:, 3], scalar=-1.0, in1=bc_mid(dtb[:, 1, :], CH),
                                     op0=ALU.mult, op1=ALU.mult).then_inc(s["gate_dve"], 1)
            dve.tensor_scalar(gates[:, :, 0, :].rearrange("p h c -> p c h"), gtmp[:, 0], 0.5, 0.5,
                              ALU.mult, ALU.add).then_inc(s["gate_ready"], 1)
            dve.wait_ge(s["gate_ready"], 4)

            def gate(h, n):
                return gates[:, bass.ds(h, 1), n, :].rearrange("p a c -> p (a c)")

            def norms(h, col):
                dve.wait_ge(s["ss_ps"], h + 1)
                dve.tensor_scalar(col[:, 0:2, :], ps[:, 4, 0:8].rearrange("p (w c) -> p w c", w=2), 4 * EPS, None,
                                  ALU.add).then_inc(s["norm_dve"], 1)
                dve.wait_ge(s["norm_dve"], h * 5 + 1)
                dve.reciprocal(col[:, 0:2, :], col[:, 0:2, :]).then_inc(s["norm_dve"], 1)
                dve.wait_ge(s["norm_dve"], h * 5 + 2)
                dve.tensor_tensor(col[:, 4, :], gate(h, 0), col[:, 1, :], ALU.mult).then_inc(s["norm_dve"], 1)
                dve.wait_ge(s["norm_dve"], h * 5 + 3)
                dve.tensor_tensor(col[:, 5, :], col[:, 4, :], gate(h, 1), ALU.mult).then_inc(s["norm_dve"], 1)

            def lower(h, col):
                dve.wait_ge(s["kk_ps"], h * 2 + 1)
                dve.wait_ge(s["dexp"], h * 2 + 1)
                if not known(h, 0):
                    dve.wait_ge(s["lev_ready"], h * 7)
                for c in range(CH):
                    dve.scalar_tensor_tensor(out=low[:, c, :], in0=ps[:, 6, c * P:(c + 1) * P],
                                             scalar=col[:, 4, c:c + 1], in1=dec[:, c, :],
                                             op0=ALU.mult, op1=ALU.mult).then_inc(s["low_ready"], 1)

            def level(h, li, invT):
                lv = LEVELS[li]
                dve.wait_ge(s["r_ps"], h * 6 + li)
                r = ps[:, 6, :].rearrange("p (w b l) -> p w b l", w=2, l=lv)
                odd = invT[:, :, :].rearrange("p c (b o l) -> p (c b) o l", o=2, l=lv)[:, :, 1, :]
                even = inv[:, :, :].rearrange("p c (b o l) -> p (c b) o l", o=2, l=lv)[:, :, 0, :]
                dve.tensor_tensor(odd, odd, r[:, 0], ALU.subtract).then_inc(s["inv_ready"], 1)
                if li < NL - 1:
                    dve.tensor_tensor(even, even, r[:, 1], ALU.subtract).then_inc(s["inv_ready"], 1)

            def out_stats(h, col):
                dve.wait_ge(s["o_ready"], h * 4 + 4)
                if not known(h, 0):
                    dve.wait_ge(s["o_tr"], h)
                dve.tensor_tensor(osq[:, :, :], onat[:, :, :], onat[:, :, :], ALU.mult).then_inc(s["o_stat"], 1)
                dve.wait_ge(s["o_stat"], h * 5 + 1)
                dve.tensor_reduce(col[:, 7, :], osq[:, :, :], AX.X, ALU.add).then_inc(s["o_stat"], 1)
                dve.wait_ge(s["o_stat"], h * 5 + 2)
                dve.tensor_tensor(col[:, 8, :], col[:, 7, :], col[:, 0, :], ALU.mult).then_inc(s["o_stat"], 1)

            def out_scale(h, col):
                dve.wait_ge(s["o_act"], h + 1)
                dve.reciprocal(col[:, 10, :], col[:, 9, :]).then_inc(s["o_stat"], 1)
                dve.wait_ge(s["o_stat"], h * 5 + 4)
                dve.scalar_tensor_tensor(out=col[:, 11, :], in0=col[:, 10, :], scalar=float(P) ** -0.5, in1=col[:, 2, :],
                                         op0=ALU.mult, op1=ALU.mult).then_inc(s["o_stat"], 1)
                dve.wait_ge(s["o_stat"], h * 5 + 5)
                dve.tensor_tensor(osq[:, :, :], onat[:, :, :], bc(col[:, 11, :], P), ALU.mult).then_inc(s["o_scaled"], 1)

            def out_gate(h):
                dve.wait_ge(s["o_tr"], h + 1)
                dve.wait_ge(s["z_ready"], h + 1)
                if not known(h, 0):
                    dve.wait_ge(s["g_hi"], h)
                dve.scalar_tensor_tensor(out=gf[:, :], in0=ps[:, 3, :], scalar=V["dn_norm_w"], in1=zs[:, :],
                                         op0=ALU.mult, op1=ALU.mult).then_inc(s["g_f"], 1)

            def out_lo(h):
                dve.wait_ge(s["g_hi"], h + 1)
                dve.tensor_tensor(alo[0][:, bass.ds(h, 1), :], gf[:, :].unsqueeze(1), ahi[0][:, bass.ds(h, 1), :],
                                  ALU.subtract).then_inc(s["g_lo"], 1)

            def decay_col(h):
                if not known(h, 0):
                    dve.wait_ge(s["dz_in"], h * 2)
                dve.tensor_copy(gcol[:, :], glog[:, :, bass.ds(h, 1)].rearrange("p c a -> p (c a)"))\
                    .then_inc(s["g_col"], 1)

            def head(h, par, last):
                first = known(h, 0)
                col, invT = cols[par], invTs[par]
                dve.wait_ge(s["lev_ready"], h * 7 + 1)
                dve.tensor_tensor(inv[:, :, :], bc_mid(K["ident"], CH), lev[:, 0], ALU.subtract)\
                    .then_inc(s["inv_ready"], 1)
                dve.wait_ge(s["inv_ps"], h + 1)
                dve.tensor_tensor(invT[:, :, :], bc_mid(K["ident"], CH),
                                  ps[:, 4, :].rearrange("p (c i) -> p c i", c=CH), ALU.subtract)\
                    .then_inc(s["inv_ready"], 1)
                if not first:
                    out_stats(h - 1, cols[1 - par])
                dve.wait_ge(s["kk_ps"], h * 2 + 2)
                dve.wait_ge(s["dmask"], h + 1)
                dve.tensor_tensor(attnT[:, :, :], ps[:, 5, :].rearrange("p (c i) -> p c i", c=CH), decT[:, :, :],
                                  ALU.mult).then_inc(s["attn_ready"], 1)
                level(h, 1, invT)
                dve.wait_ge(s["kn_ps"], h + 1)
                kn = ps[:, 2, :].rearrange("p (c i) -> p c i", c=CH)
                dve.tensor_tensor(kbeta[:, :, :], kn, bc(col[:, 5, :], P), ALU.mult).then_inc(s["kside"], 1)
                dve.tensor_tensor(kdec[:, :, :], kn, bc(gate(h, 2), P), ALU.mult).then_inc(s["kside"], 1)
                if not first:
                    out_scale(h - 1, cols[1 - par])
                level(h, 2, invT)
                if not first:
                    out_gate(h - 1)
                level(h, 3, invT)
                if not last:
                    decay_col(h + 1)
                tap(h, 2, 1)
                tap(h, 2, 2)
                level(h, 4, invT)
                if not first:
                    out_lo(h - 1)
                tap(h, 2, 3)
                silu2(h, 2, vT)
                dve.wait_ge(s["norm_act"], h + 1)
                dve.scalar_tensor_tensor(out=col[:, 6, :], in0=col[:, 3, :], scalar=0.5, in1=gate(h, 0),
                                         op0=ALU.mult, op1=ALU.mult).then_inc(s["norm_dve"], 1)
                level(h, 5, invT)
                if not last:
                    tap(h + 1, 0, 1)
                    tap(h + 1, 0, 2)
                level(h, 6, invT)
                dve.wait_ge(s["vn_ps"], h + 1)
                dve.wait_ge(s["norm_dve"], h * 5 + 5)
                dve.tensor_tensor(vbeta[:, :, :], ps[:, 2, :].rearrange("p (c i) -> p c i", c=CH), bc(col[:, 6, :], P),
                                  ALU.mult).then_inc(s["vb_ready"], 1)
                if not last:
                    tap(h + 1, 0, 3)
                if not last:
                    silu2(h + 1, 0, qT[1 - par])
                for c in range(CH):
                    if c < CH - 1:
                        dve.wait_ge(s["st_ps"], h * 3 + c + 1)
                        if c == 0:
                            dve.tensor_copy(state[:, 0], ps[:, 7, 0:P]).then_inc(s["st_ready"], 1)
                        else:
                            dve.scalar_tensor_tensor(out=state[:, c % 2], in0=state[:, 1 - c % 2],
                                                     scalar=gates[:, bass.ds(h, 1), 3, c], in1=ps[:, 7, 0:P],
                                                     op0=ALU.mult, op1=ALU.add).then_inc(s["st_ready"], 1)
                    if c == 0 and not last:
                        tap(h + 1, 1, 1)
                    dve.wait_ge(s["o_ps"], h * 4 + c + 1)
                    if c == 0:
                        dve.tensor_copy(onat[:, 0], ps[:, 7, P:2 * P]).then_inc(s["o_ready"], 1)
                    else:
                        dve.wait_ge(s["o1_ev"], h * 3 + c)
                        dve.tensor_tensor(onat[:, c], ps[:, 7, P:2 * P], o1[:, :], ALU.add)\
                            .then_inc(s["o_ready"], 1)
                    if c == 0 and not last:
                        tap(h + 1, 1, 2)
                        tap(h + 1, 1, 3)
                    if c == 1 and not last:
                        silu2(h + 1, 1, kT[1 - par])
                if not last:
                    norms(h + 1, cols[1 - par])
                    lower(h + 1, cols[1 - par])
                dve.wait_ge(s["ztanh"], h + 1)
                if not first:
                    dve.wait_ge(s["g_f"], h)
                dve.scalar_tensor_tensor(out=zs[:, :], in0=th[:, :], scalar=1.0, in1=ps[:, 0, :],
                                         op0=ALU.add, op1=ALU.mult).then_inc(s["z_ready"], 1)

            dve.wait_ge(s["gate_dve"], 4)
            decay_col(0)
            norms(0, cols[0])
            lower(0, cols[0])
            head(0, 0, False)
            with dve.Fori(0, H // 2 - 1) as j:
                head(j * 2 + 1, 1, False)
                head(j * 2 + 2, 0, False)
            head(H - 1, 1, True)
            out_stats(H - 1, cols[1])
            out_scale(H - 1, cols[1])
            out_gate(H - 1)
            out_lo(H - 1)
            for m in range(KT):
                dve.wait_ge(s["w_used"], U_OUT + m + 1)
                dve.tensor_tensor(xT[:, m], xT[:, m], ps[:, (U_OUT + m) % 2, :], ALU.add).then_inc(s["res"], 1)
                if m == 0:
                    dve.wait_ge(s["mod_c"], 1)
                    dve.scalar_tensor_tensor(out=cact[:, :], in0=cact[:, :], scalar=1.0, in1=V["c_2"],
                                             op0=ALU.add, op1=ALU.mult).then_inc(s["mod_c"], 1)
                    for j in range(3):
                        dve.memset(mod_acc[:, j * D:(j + 1) * D], 0.0).then_inc(s["mod_done"], 1)
            dve.wait_ge(s["n_sqrt"], 2)
            dve.reciprocal(rr1[:, :], rs1[:, :]).then_inc(s["n_rstd"], 1)
            dve.wait_ge(s["n_rstd"], 2)
            for k in range(KT):
                if k >= 2:
                    dve.wait_ge(s["n_lo"], KT + k - 1)
                dve.scalar_tensor_tensor(out=hf1[:, k % 2], in0=xT[:, k], scalar=V["norm_mlp"][:, k:k + 1],
                                         in1=rr1[:, :], op0=ALU.mult, op1=ALU.mult).then_inc(s["n_h"], 1)

            def modulate(kk, j):
                if j == 0:
                    dve.wait_ge(s["mod_c"], 2)
                    dve.wait_ge(s["mod_in"], kk * 16 + 16)
                dve.wait_ge(s["mod_done"], kk * 3 + j + 1)
                cut = slice(j * D, (j + 1) * D)
                dve.scalar_tensor_tensor(out=mod_acc[:, cut], in0=mod_w[:, cut], scalar=cact[:, bass.ds(kk, 1)],
                                         in1=mod_acc[:, cut], op0=ALU.mult, op1=ALU.add).then_inc(s["mod_done"], 1)

            def quarter(q, par):
                n0 = U_MLP + q * 16
                for m in range(KT):
                    dve.wait_ge(s["mlp_relu"], q * KT + m + 1)
                    if m >= 2:
                        dve.wait_ge(s["mlp_lo"], q * KT + m - 1)
                    dve.tensor_tensor(af[:, m % 2], relu[:, m % 2], relu[:, m % 2], ALU.mult).then_inc(s["mlp_f"], 1)
                    if 2 <= m < 5:
                        modulate(q * 2, m - 2)
                for m in range(KT):
                    dve.wait_ge(s["w_used"], n0 + KT + m + 1)
                    dve.tensor_tensor(xT[:, m], xT[:, m], ps[:, (U_MLP + m) % 2, :], ALU.add).then_inc(s["res"], 1)
                    if 1 <= m < 4:
                        modulate(q * 2 + 1, m - 1)
                    dve.wait_ge(s["e_sq"], q * KT + m + 1)
                    if m == 0:
                        dve.wait_ge(s["mlp_lo"], q * KT + KT)
                        dve.tensor_copy(hf1[:, :, :], nsq[:, :, :]).then_inc(s["e_add"], 1)
                    else:
                        dve.wait_ge(s["e_add"], q * KT + m)
                        dve.tensor_tensor(hf1[:, :, :], hf1[:, :, :], nsq[:, :, :], ALU.add).then_inc(s["e_add"], 1)
                dve.wait_ge(s["e_add"], q * KT + KT)

            with dve.Fori(0, QUARTERS // 2) as j:
                quarter(j * 2, 0)
                quarter(j * 2 + 1, 1)

            done = lane("dve")
            after(dve, "pe", "modulation")
            done(dve.scalar_tensor_tensor(out=mod[:, 0:3 * KT], in0=ps[:, 7, 0:3 * KT], scalar=0.5, in1=V["ada_b_2"],
                                          op0=ALU.mult, op1=ALU.add), "mod")
            after(dve, "dve", "mod")
            done(dve.scalar_tensor_tensor(out=mod[:, 3 * KT:4 * KT], in0=mod[:, KT:2 * KT], scalar=1.0, in1=V["norm_g_2"],
                                          op0=ALU.add, op1=ALU.mult), "mod gain 1")
            after(dve, "dve", "mod gain 1")
            done(dve.tensor_tensor(mod[:, 3 * KT:4 * KT], mod[:, 3 * KT:4 * KT], V["norm_final"], ALU.mult), "mod gain 2")
            after(dve, "pe", "square sums")
            done(dve.tensor_scalar(hf1[:, 0], ps[:, 2, :], EPS, EPS * EPS, ALU.mult, ALU.add), "var 1")
            after(dve, "dve", "var 1")
            done(dve.tensor_tensor(hf1[:, 0], hf1[:, 0], ps[:, 3, :], ALU.add), "var 2")

            def norm_low(k):
                after(dve, "act", f"h high {k}")
                done(dve.scalar_tensor_tensor(out=hlo[:, k], in0=relu[:, k % 2], scalar=mod[:, k:k + 1], in1=hhi[:, k],
                                              op0=ALU.add, op1=ALU.subtract), f"norm low {k}")

            after(dve, "act", "root 2")
            done(dve.reciprocal(hf1[:, 0], hf1[:, 1]), "inv 2")
            after(dve, "dve", "inv 2")
            for k in range(KT):
                if k >= 2:
                    after(dve, "dve", f"norm low {k - 2}")
                done(dve.scalar_tensor_tensor(out=relu[:, k % 2], in0=xT[:, k], scalar=mod[:, 3 * KT + k:3 * KT + k + 1],
                                              in1=hf1[:, 0], op0=ALU.mult, op1=ALU.mult), f"h {k}")
                if k:
                    norm_low(k - 1)
            norm_low(KT - 1)
            after(dve, "act", "root 1")
            done(dve.reciprocal(rr1[:, :], rs1[:, :]), "inv 1")
            after(dve, "dve", "inv 1")
            for k in range(KT):
                done(dve.scalar_tensor_tensor(out=xT[:, k], in0=xT[:, k], scalar=V["norm_final"][:, k:k + 1],
                                              in1=rr1[:, :], op0=ALU.mult, op1=ALU.mult), f"x normed {k}")
            dve.wait_ge(s["c2_in"], 16)
            dve.tensor_copy(identb[:, :], K["ident"])
            done(dve.tensor_copy(negb[:, :], K2["causal"]), "bf16")
            dve.wait_ge(s["pos_in"], 16)
            table_step = [0]

            def tab(ins):
                done(ins, f"table {table_step[0]}")
                after(dve, "dve", f"table {table_step[0]}")
                table_step[0] += 1

            even, odd = turn[:, 0::2, :], turn[:, 1::2, :]

            tab(dve.tensor_copy(turn[:, 0], pos_i[:, :]))
            dve.tensor_scalar(ang[:, 0], turn[:, 0], K2["freq"], None, ALU.mult)
            tab(dve.tensor_scalar(ang[:, 1], turn[:, 0], K2["freq_m"], None, ALU.mult))
            dve.tensor_scalar(even, ang[:, :, :], 0.5 / np.pi, None, ALU.mult)
            tab(dve.tensor_scalar(odd, ang[:, :, :], 0.5 / np.pi, 0.25, ALU.mult, ALU.add))
            tab(dve.tensor_scalar(turn[:, :, :], turn[:, :, :], MAGIC, MAGIC, ALU.add, ALU.subtract))
            for m in range(2):
                ins = dve.scalar_tensor_tensor(out=table[:, 2 * m:2 * m + 2], in0=turn[:, 2 * m:2 * m + 2],
                                               scalar=-TWO_PI[0], in1=bc_mid(ang[:, m], 2), op0=ALU.mult, op1=ALU.add)
            tab(ins)
            for part in TWO_PI[1:]:
                tab(dve.scalar_tensor_tensor(out=table[:, :, :], in0=turn[:, :, :], scalar=-part, in1=table[:, :, :],
                                             op0=ALU.mult, op1=ALU.add))
            tab(dve.tensor_scalar(table[:, 1::2, :], table[:, 1::2, :], np.pi / 2, None, ALU.add))
            tab(dve.tensor_scalar(table[:, :, :], table[:, :, :], 3.1415925, -3.1415925, ALU.min, ALU.max))
            after(dve, "pe", "positions turned")
            done(dve.tensor_copy(cposT[:, :], ps[:, 7, P:P + CMP_BLOCK]), "positions")

            def window(w, src):
                after(dve, "act", ("ev kc", "ev vc")[w])
                after(dve, "dve", "positions")
                after(dve, "pool", "window zero") if w == 0 else after(dve, "pe", "hidden k")
                for g in range(2):
                    for half in range(2):
                        r, cut = slice(g * DK, (g + 1) * DK), slice(half * CMP_STRIDE, (half + 1) * CMP_STRIDE)
                        ins = dve.tensor_tensor(xb[r, cut, g, 0:NC], windows(src[r, :], half),
                                                cposT[r, cut].unsqueeze(2).broadcast_to([DK, CMP_STRIDE, NC]), ALU.add)
                done(ins, ("window k", "window v")[w])

            def aux_bank(name):
                return ps[:, 2 + AUX.index(name) % 2, :]

            after(dve, "pe", "aux gate")
            done(dve.tensor_copy(gate2[:, :, :], aux_bank("gate")[:, 0:CH * 3 * QH].rearrange("p (c n) -> p c n", c=CH)),
                 "post gate")
            for b, name in enumerate(("vs", "vw")):
                after(dve, "pe", f"aux {name}")
                done(dve.tensor_copy(v2[b][:, :, :], aux_bank(name).rearrange("p (c n) -> p c n", c=CH)), f"post {name}")
            window(0, kcT)
            after(dve, "act", "gate tanh")
            done(dve.tensor_scalar(gate2[:, :, :], gate2[:, :, :], 0.5, 0.5, ALU.mult, ALU.add), "gates")

            def rotated(name, dst, last):
                r = ROPE.index(name)
                rows_ = slice(MN, MD) if name == "kr" else slice(0, P)
                if last:
                    after(dve, "dve", last)
                after(dve, "pe", f"aux {name}")
                after(dve, "act", "tables")
                done(dve.tensor_tensor(rsin[rows_, :], aux_bank(name)[rows_], table[rows_, 2 if name == "kr" else 0], ALU.mult),
                     f"sin {name}")
                after(dve, "dve", f"sin {name}")
                after(dve, "pool", f"cos {name}")
                done(dve.tensor_tensor(dst[rows_], rcos[rows_, r % 2], rsin[rows_, :], ALU.add), f"post {name}")

            def hidden(w):
                after(dve, "act", f"tanh {'kv'[w]}")
                done(dve.scalar_tensor_tensor(out=hid[:, w, 1], in0=hid[:, w, 0], scalar=1.0,
                                              in1=ps[:, 4 + w, 0:2 * NCP].rearrange("p (g n) -> p g n", g=2),
                                              op0=ALU.add, op1=ALU.mult), f"hidden {'kv'[w]}")

            rotated("q0", q2T[:, 0], None)
            window(1, vcT)
            rotated("q1", q2T[:, 1], "post q0")
            hidden(0)
            rotated("q2", q2T[:, 2], "post q1")
            rotated("q3", q2T[:, 3], "post q2")
            hidden(1)
            after(dve, "dve", "hidden v")
            done(dve.tensor_copy(hid4[:, :, :, :], hid[:, 1, 1].unsqueeze(2).broadcast_to([P, 2, 4, NCP])), "hidden v 4")
            rotated("ks", kT2[0][:, :], "post q3")
            after(dve, "pe", "second layer")
            done(dve.tensor_scalar(ktmp[:, 0], ps[:, 6, 0:2 * NCP].rearrange("p (g n) -> p g n", g=2), 0.5, None, ALU.mult),
                 "kc")
            after(dve, "pool", "block zero")
            for g in range(2):
                for h in range(4):
                    r = slice(h * NCP, (h + 1) * NCP)
                    ins = dve.tensor_scalar(vbd[r, g, h], ps[r, 6, 2 * NCP + g * DK:2 * NCP + (g + 1) * DK], 0.5, None,
                                            ALU.mult)
            done(ins, "block values")

            def at_blocks(n):
                return table[:, n, CMP_BLOCK - 1::CMP_STRIDE].unsqueeze(1).broadcast_to([P, 2, NC])

            after(dve, "dve", "kc")
            done(dve.tensor_tensor(ktmp[:, 1, :, 0:NC], ktmp[:, 0, :, 0:NC], at_blocks(1), ALU.mult), "kc cos")
            rotated("kw", kT2[1][:, :], "post ks")
            after(dve, "pe", "rotate kc")
            done(dve.tensor_tensor(ktmp[:, 2, :, 0:NC], ps[:, 7, 0:2 * NCP].rearrange("p (g n) -> p g n", g=2)[:, :, 0:NC],
                                   at_blocks(0), ALU.mult), "kc sin")
            after(dve, "dve", "kc sin")
            done(dve.tensor_tensor(kcr[:, :, 0:NC], ktmp[:, 1, :, 0:NC], ktmp[:, 2, :, 0:NC], ALU.add), "kc rotated")
            after(dve, "pe", "block scores")
            for g in range(2):
                for c in range(CH):
                    ins = dve.scalar_tensor_tensor(out=by_head(csc[:, g])[:, c], in0=by_head(ps[:, 4 + g, :])[:, c],
                                                   scalar=SCALE, in1=seen_by("cmp_neg")[:, c], op0=ALU.mult, op1=ALU.add)
            done(ins, "scaled")
            scores = csc[:, :, :].rearrange("p g (r n) -> p (g r) n", n=NCP)
            after(dve, "dve", "scaled")
            done(dve.tensor_reduce(csm[:, 0], scores, AX.X, ALU.max), "max")
            after(dve, "dve", "max")
            done(dve.tensor_tensor(scores, scores, bc(csm[:, 0], NCP), ALU.subtract), "less max")
            after(dve, "act", "block exp")
            done(dve.tensor_reduce(csm[:, 1], scores, AX.X, ALU.add), "sum")
            after(dve, "dve", "sum")
            for g in range(2):
                ins = dve.tensor_tensor(by_head(csc[:, g]), by_head(csc[:, g]), seen_by("cmp_one"), ALU.mult)
            done(ins, "seen")
            done(dve.reciprocal(csm[:, 2], csm[:, 1]), "sum inv")
            after(dve, "dve", "sum inv")
            after(dve, "dve", "gates")
            done(dve.tensor_tensor(csm[:, 3].rearrange("p (g q h) -> p g q h", g=2, q=CH),
                                   csm[:, 2].rearrange("p (g q h) -> p g q h", g=2, q=CH),
                                   gate2[:, :, :].rearrange("p q (g h b) -> p g q h b", g=2, b=3)[:, :, :, :, 0], ALU.mult),
                 "coef")
            after(dve, "dve", "coef")
            done(dve.tensor_tensor(scores, scores, bc(csm[:, 3], NCP), ALU.mult), "probs")
            rotated("kr", krT[:, :], "post kw")
            after(dve, "act", "root cq")
            done(dve.reciprocal(prob[:, 1], prob[:, 0]), "inv cq")
            after(dve, "dve", "inv cq")
            for w in range(2):
                done(dve.scalar_tensor_tensor(out=cn[:, w], in0=cn[:, w], scalar=V["q_norm_g_2"][:, w:w + 1], in1=prob[:, 1],
                                              op0=ALU.mult, op1=ALU.mult), f"cq {w}")
            after(dve, "act", "root ckv")
            done(dve.reciprocal(probT[:, 1], probT[:, 0]), "inv ckv")
            after(dve, "dve", "inv ckv")
            done(dve.scalar_tensor_tensor(out=cn[:, 2], in0=cn[:, 2], scalar=V["kv_norm_g_2"], in1=probT[:, 1],
                                          op0=ALU.mult, op1=ALU.mult), "ckv")
            after(dve, "pe", "block values")
            done(dve.tensor_copy(o_nsa[:, :, :], ps[:, 2:6, :]), "block out")

            def most(i, n, exp_scale, keys, bank):
                dve.wait_ge(s["at_s"], n + 1)
                if i >= 2:
                    dve.wait_ge(s["at_exp"], n - 1)
                c = slice(i % 2, i % 2 + 1)
                dve.tensor_reduce(amax[:, c], ps[:, bank, 0:keys], AX.X, ALU.max).then_inc(s["at_max"], 1)
                dve.wait_ge(s["at_max"], n + 1)
                dve.tensor_scalar(aneg[:, c], amax[:, c], -exp_scale, None, ALU.mult).then_inc(s["at_neg"], 1)

            def attend(first, count, exp_scale, weigh, combine, between, bank_of=score_bank):
                for i in range(count + 3):
                    between(i)
                    if i < count:
                        most(i, first + i, exp_scale, (i % 4 + 1) * P, bank_of(i))
                    if 1 <= i <= count:
                        k, n = i - 1, first + i - 1
                        dve.wait_ge(s["at_exp"], n + 1)
                        dve.reciprocal(ainv[:, k % 4:k % 4 + 1], asum[:, k % 2:k % 2 + 1]).then_inc(s["at_inv"], 1)
                        dve.wait_ge(s["at_inv"], n + 1)
                        weigh(k)
                    if i >= 3:
                        k, n = i - 3, first + i - 3
                        dve.wait_ge(s["at_o"], n + 1)
                        dve.wait_ge(s["at_done"], n + 1)
                        combine(k, n)

            dve.memset(acoef[:, :], 0.0).then_inc(s["at_done"], 1)
            with dve.Fori(0, 2) as j:
                def between(i):
                    if i % 8 == 2 and i > 2:
                        u = i // 8 - 1
                        dve.wait_ge(s["z_th"], j * 4 + u + 1)
                        dve.scalar_tensor_tensor(out=zs2[:, bass.ds(j * 4 + u, 1), :], in0=zth[:, :].unsqueeze(1),
                                                 scalar=1.0, in1=ps[:, u % 2:u % 2 + 1, :],
                                                 op0=ALU.add, op1=ALU.mult).then_inc(s["z_done"], 1)

                def weigh(k):
                    pair, g, b, c = k // 16, k // 8 % 2, k // 4 % 2, slice(k % 4, k % 4 + 1)
                    dve.tensor_tensor(acoef[:, c], ainv[:, c],
                                      gate2[:, k % 4, bass.ds(j * 6 + (pair * 3 + g * 12 + 1 + b), 1)],
                                      ALU.mult).then_inc(s["at_coef"], 1)

                def combine(k, n):
                    dve.wait_ge(s["at_coef"], n + 1)
                    o = o_nsa[:, k % 4, bass.ds(j * 2 * DK + (k // 16 * DK + k // 8 % 2 * 256), DK)]
                    dve.scalar_tensor_tensor(out=o, in0=ps[:, 7, 0:DK], scalar=acoef[:, k % 4:k % 4 + 1], in1=o,
                                             op0=ALU.mult, op1=ALU.add).then_inc(s["at_done"], 1)

                attend(j * 32, 32, SCALE, weigh, combine, between)

            def mix(k):
                after(dve, "pe", f"turned {k}")
                if k >= 2:
                    after(dve, "pool", f"mix low {k - 2}")
                done(dve.scalar_tensor_tensor(out=gated[:, k % 2], in0=ps[:, 2 + k % 4, :], scalar=0.5, in1=zs2[:, k],
                                              op0=ALU.mult, op1=ALU.mult), f"mixed {k}")

            for k in range(KH):
                mix(k)
            for par in range(2):
                ins = dve.tensor_copy(km[MN:MD, par], krT[MN:MD, :])
            done(ins, "rotated keys")
            with dve.Fori(0, 2) as j:
                def rotate(hh):
                    if hh:
                        dve.wait_ge(s["p_q"], j * 4 + hh)
                    dve.wait_ge(s["p_rot"], j * 4 + hh + 1)
                    dve.tensor_tensor(qsin[0:MD, :], ps[0:MD, turn_bank("rot", hh), :], table[0:MD, 2], ALU.mult)\
                        .then_inc(s["p_sin"], 1)
                    dve.wait_ge(s["p_sin"], j * 4 + hh + 1)
                    dve.wait_ge(s["p_cos"], j * 4 + hh + 1)
                    dve.tensor_tensor(qm[0:MD, hh % 2], qcos[0:MD, :], qsin[0:MD, :], ALU.add).then_inc(s["p_q"], 1)

                def between_m(i):
                    if i % 4 == 2 and i < 12:
                        rotate(i // 4 + 1)
                    if i % 4 == 1 and i < 16:
                        u = i // 4
                        dve.wait_ge(s["w_used"], j * 4 + U_OUT2 + u + 1)
                        x_u = xT[:, bass.ds(j * 4 + u, 1), :]
                        dve.scalar_tensor_tensor(out=x_u, in0=ps[:, u % 2:u % 2 + 1, :],
                                                 scalar=mod[:, bass.ds(j * 4 + (2 * KT + u), 1)],
                                                 in1=x_u, op0=ALU.mult, op1=ALU.add).then_inc(s["xa_done"], 1)

                def combine_m(k, n):
                    dve.tensor_scalar(o_mla[:, k % 4, bass.ds(j * 4 * DK + k // 4 * DK, DK)], ps[:, 7, 0:DK],
                                      ainv[:, k % 4:k % 4 + 1], None, ALU.mult).then_inc(s["at_done"], 1)

                rotate(0)
                attend(j * 16 + 64, 16, SCALE_M, lambda k: None, combine_m, between_m, lambda i: turn_bank("s", i))
            for k in range(KH, KT):
                mix(k)
            for m in range(KT):
                dve.wait_ge(s["w_used"], U_OUT2 + KT + m + 1)
                done(dve.scalar_tensor_tensor(out=xT[:, m], in0=ps[:, m % 2, :], scalar=mod[:, 2 * KT + m:2 * KT + m + 1],
                                              in1=xT[:, m], op0=ALU.mult, op1=ALU.add), f"x {m}")
            after(dve, "act", "out root")
            done(dve.reciprocal(orr[:, :], ors[:, :]), "out inv")
            after(dve, "dve", "out inv")
            for k in range(KT):
                if k >= 2:
                    after(dve, "pe", f"back {k - 2}")
                done(dve.scalar_tensor_tensor(out=onorm[:, k % 2], in0=xT[:, k], scalar=V["final_norm_g_2"][:, k:k + 1],
                                              in1=orr[:, :], op0=ALU.mult, op1=ALU.mult), f"y {k}")

        @block.tensor
        def _(pe):
            def unit_parts(n, slot, hi, lo, width=P, ready=None, ks=range(KT)):
                pe.wait_ge(s["w_lo"], n + 1)
                bank = ps[0:width, slot % 2, :]
                todo = [(k, w, x) for k in ks for w, x in ((whi, hi), (whi, lo), (wlo, hi))]
                for i, (k, w, x) in enumerate(todo):
                    if ready is not None and i % 3 == 0:
                        ready(k)
                    mm = pe.matmul(bank, w[:, slot, k - ks[0], 0:width], x[:, k], start=(i == 0), stop=(i == len(todo) - 1))
                    if i == len(todo) - 1:
                        mm.then_inc(s["w_used"], 1)
                    yield

            def unit(*a, **kw):
                for _ in unit_parts(*a, **kw):
                    pass

            pe.wait_ge(s["const_in"], 16)
            ident = K["ident"]
            pe.wait_ge(s["x_in"], 16 * CH)
            for k in range(KT):
                if k >= 4:
                    pe.wait_ge(s["xev"], k - 3)
                for c in range(CH):
                    mm = pe.transpose(ps[:, 3 + k % 4, c * P:(c + 1) * P], xn[:, c, k * P:(k + 1) * P], ident)
                mm.then_inc(s["xtr"], 1)

                def stat(k):
                    pe.wait_ge(s["n_sq"], k + 1)
                    pe.matmul(ps[:, 2, :], K["mean"], sqn[:, k % 2], start=(k == 0), stop=(k == KT - 1))\
                        .then_inc(s["n_stat"], 1)
                if k >= 1:
                    stat(k - 1)
            stat(KT - 1)
            pe.wait_ge(s["vec_in"], 16 * (len(VEC_ROWS) + 4))
            pe.transpose(ps[:, 7, 0:NVEC], rows[0:NVEC, 0, :], ident[0:NVEC, 0:NVEC])
            pe.transpose(ps[:, 7, P:P + 96], rows[0:96, 1, :], ident[0:96, 0:96]).then_inc(s["vec_tr"], 1)
            unit(0, 0, hhi, hlo, ready=lambda k: pe.wait_ge(s["n_lo"], k + 1))
            unit(1, 1, hhi, hlo)
            pe.wait_ge(s["conv1"], 3)
            unit(2, 2, hhi, hlo, BA_N)
            pe.wait_ge(s["ba_ev"], 1)
            for c in range(CH):
                mm = pe.transpose(ps[:, 5, c * 16:(c + 1) * 16], ba[BA_LEAD:BA_N, c * P:(c + 1) * P],
                                  ident[BA_LEAD:BA_N, BA_LEAD:BA_N])
            mm.then_inc(s["ba_tr"], 1)
            pe.wait_ge(s["gate_dve"], 4)
            g2 = glog[:, :, :].rearrange("p c h -> p (c h)")
            for n, m in enumerate(("upto", "after", "ones")):
                mm = pe.matmul(ps[:, 4, 32 * n:32 * n + 32], K[m], g2, start=True, stop=True)
            mm.then_inc(s["gate_ps"], 1)

            def chunk(t, c):
                return t[:, c * P:(c + 1) * P]

            def decay_sums(h, w):
                pe.wait_ge(s["dz_in"], h * 2 + w + 1)
                if w == 0:
                    pe.wait_ge(s["gate_ready"], 4) if known(h, 0) else pe.wait_ge(s["inv_ready"], h * 13)
                elif not known(h, 0):
                    pe.wait_ge(s["w_ev"], h)
                pe.matmul(ps[:, 4 + w, :], K[("upto", "after")[w]], gd[:, :, :].rearrange("p c i -> p (c i)"),
                          start=True, stop=True).then_inc(s["dps"], 1)

            def pair_products(h, q, k):
                pe.wait_ge(s["seq_ready"], h * 3 + 2)
                for c in range(CH):
                    mm = pe.matmul(ps[:, 6, c * P:(c + 1) * P], chunk(k, c), chunk(k, c), start=True, stop=True)
                mm.then_inc(s["kk_ps"], 1)
                pe.wait_ge(s["sqs"], h * 2 + 2)
                pe.wait_ge(s["dexp"], h * 2 + 1)
                for w in range(2):
                    for c in range(CH):
                        mm = pe.matmul(ps[:, 4, w * 4 + c:w * 4 + c + 1], chunk(sq[:, w], c), K["ones"][:, 0:1],
                                       start=True, stop=True)
                mm.then_inc(s["ss_ps"], 1)
                pe.wait_ge(s["dexp"], h * 2 + 2)
                for c in range(CH):
                    mm = pe.matmul(ps[:, 5, c * P:(c + 1) * P], chunk(k, c), chunk(q, c), start=True, stop=True)
                mm.then_inc(s["kk_ps"], 1)
                if not known(h, 0):
                    pe.wait_ge(s["vb_ready"], h)
                for c in range(CH):
                    mm = pe.transpose(ps[:, 2, c * P:(c + 1) * P], chunk(k, c), ident)
                mm.then_inc(s["kn_ps"], 1)

            def out_turn(h):
                pe.wait_ge(s["o_scaled"], h + 1)
                for c in range(CH):
                    mm = pe.transpose(ps[:, 3, c * P:(c + 1) * P], osq[:, c], ident)
                mm.then_inc(s["o_tr"], 1)

            def head(h, par, last):
                def fillers():
                    pe.wait_ge(s["seq_ready"], h * 3 + 2)
                    yield from unit_parts(h * 4 + 3, 3, hhi, hlo)
                    if not last:
                        pe.wait_ge(s["ba_ev"], 1) if known(h, 0) else pe.wait_ge(s["z_ready"], h)
                        yield from unit_parts(h * 4 + 4, 0, hhi, hlo)
                        pe.wait_ge(s["seq_ready"], h * 3 + 3)
                        yield from unit_parts(h * 4 + 5, 1, hhi, hlo)
                        pe.wait_ge(s["seq_ready"], h * 3 + 4)
                        yield from unit_parts(h * 4 + 6, 2, hhi, hlo)
                    else:
                        pe.wait_ge(s["z_ready"], h)
                        yield from unit_parts(DN_UNITS - 1, 0, hhi, hlo)

                stream = fillers()

                def fill(n):
                    for _ in range(n):
                        next(stream, None)

                first = known(h, 0)
                q, invT = qT[par], invTs[par]
                pe.wait_ge(s["lev_ready"], h * 7 + 1)
                pe.wait_ge(s["norm_dve"], h * 5 + 1)
                for c in range(CH):
                    mm = pe.transpose(ps[:, 4, c * P:(c + 1) * P], lev[:, 0, c], ident)
                mm.then_inc(s["inv_ps"], 1)
                fill(F_INV)
                for li in range(1, NL):
                    lv = LEVELS[li]
                    pe.wait_ge(s["lev_ready"], h * 7 + li + 1)
                    pe.wait_ge(s["inv_ready"], h * 13 + 2 * li)

                    def half(t, odd):
                        return t.rearrange("p (b o l) -> p b o l", o=2, l=lv)[:, :, odd, :]

                    def to(bank, n):
                        return ps[:, bank, n * 64:(n + 1) * 64].rearrange("p (b l) -> p b l", l=lv)

                    for c in range(CH):
                        mm = pe.matmul(to(4, c), lev[:, li % NB, c], half(invT[:, c], 1), start=True, stop=True)
                    mm.then_inc(s["q_ps"], 1)
                    fill(F_Q)
                    pe.wait_ge(s["q_ev"], h * 6 + li)
                    if li == 1:
                        pe.wait_ge(s["low_ready"], h * 4 + 4)
                    for c in range(CH):
                        mm = pe.matmul(to(6, c), inv[:, c], half(qlev[lv][:, c], 1), start=True, stop=True)
                    if li < NL - 1:
                        for c in range(CH):
                            mm = pe.matmul(to(6, CH + c), qlev[lv][:, c], half(inv[:, c], 0), start=True, stop=True)
                    mm.then_inc(s["r_ps"], 1)
                    fill(F_R)
                    if li == 2 and not first:
                        out_turn(h - 1)
                    if li == NL - 2:
                        pe.wait_ge(s["kside"], h * 2 + 2)
                        pe.wait_ge(s["seq_ready"], h * 3 + 3)
                        for c in range(CH):
                            mm = pe.transpose(ps[:, 2, c * P:(c + 1) * P], chunk(vT, c), ident)
                        mm.then_inc(s["vn_ps"], 1)
                fill(F_W)
                pe.wait_ge(s["inv_ready"], h * 13 + 13)
                pe.wait_ge(s["attn_ready"], h + 1)
                for c in range(CH):
                    mm = pe.matmul(ps[:, 5, c * P:(c + 1) * P], kbeta[:, c], invT[:, c], start=True, stop=True)
                mm.then_inc(s["w_ps"], 1)
                for c in range(CH):
                    if c == 0:
                        pe.wait_ge(s["vb_ready"], h + 1)
                        if not first:
                            pe.wait_ge(s["g_f"], h)
                    else:
                        pe.wait_ge(s["v_ev"], h * 4 + c)
                        if c > 1:
                            pe.wait_ge(s["o1_ev"], h * 3 + c - 1)
                    vb = ps[:, 3, 0:P]
                    mm = pe.matmul(vb, invT[:, c], vbeta[:, c], start=True, stop=(c == 0))
                    if c:
                        pe.wait_ge(s["w_ev"], h + 1)
                        pe.wait_ge(s["st_ready"], h * 3 + c)
                        mm = pe.matmul(vb, wT[:, c], state[:, (c - 1) % 2], start=False, stop=True)
                    mm.then_inc(s["v_ps"], 1)
                    fill(F_C0 if c == 0 else F_C)
                    pe.wait_ge(s["v_ev"], h * 4 + c + 1)
                    if c:
                        pe.matmul(ps[:, 3, P:2 * P], chunk(q, c), state[:, (c - 1) % 2], start=True, stop=True)\
                            .then_inc(s["o1_ps"], 1)
                        pe.wait_ge(s["o_ready"], h * 4 + c)
                    if c < CH - 1:
                        pe.matmul(ps[:, 7, 0:P], kdec[:, c], vnew[:, c], start=True, stop=True).then_inc(s["st_ps"], 1)
                        if c == 0 and not last:
                            decay_sums(h + 1, 0)
                        fill(F_C)
                        pe.wait_ge(s["st_ready"], h * 3 + c + 1)
                    pe.matmul(ps[:, 7, P:2 * P], attnT[:, c], vnew[:, c], start=True, stop=True)\
                        .then_inc(s["o_ps"], 1)
                    if c == 1 and not last:
                        decay_sums(h + 1, 1)
                    if c < 3:
                        fill(F_C)
                if not last:
                    pair_products(h + 1, qT[1 - par], kT[1 - par])
                fill(96)

            decay_sums(0, 0)
            decay_sums(0, 1)
            pair_products(0, qT[0], kT[0])
            head(0, 0, False)
            with pe.Fori(0, H // 2 - 1) as j:
                head(j * 2 + 1, 1, False)
                head(j * 2 + 2, 0, False)
            head(H - 1, 1, True)
            out_turn(H - 1)

            def stat1(m, k):
                pe.wait_ge(s["n_sq"], m * KT + k + 1)
                pe.matmul(ps[:, 2, :], K["mean"], nsq[:, k % 2], start=(k == 0), stop=(k == KT - 1))\
                    .then_inc(s["n_stat"], 1)

            pe.wait_ge(s["z_ready"], H)
            for m in range(KT):
                if m >= 2:
                    pe.wait_ge(s["res"], m - 1)
                unit(U_OUT + m, (U_OUT + m) % RING, ahi[0], alo[0],
                     ready=(lambda k: pe.wait_ge(s["g_lo"], k + 1)) if m == 0 else None)
                if m:
                    stat1(1, m - 1)
            stat1(1, KT - 1)

            def quarter(q, par):
                n0 = U_MLP + q * 16
                for m in range(KT):
                    pe.wait_ge(s["mlp_relu"], q * KT + m - 1) if m >= 2 else pe.wait_ge(s["res"], q * KT + KT - 1 + m)
                    unit(n0 + m, (U_MLP + m) % RING, hhi, hlo,
                         ready=(lambda k: pe.wait_ge(s["n_lo"], KT + k + 1)) if m == 0 else None)
                for m in range(KT):
                    pe.wait_ge(s["mlp_relu"], q * KT + KT - 1 + m) if m < 2 else \
                        pe.wait_ge(s["res"], KT + q * KT + m - 1)
                    unit(n0 + KT + m, (U_MLP + m) % RING, ahi[par], alo[par],
                         ready=(lambda k: pe.wait_ge(s["mlp_lo"], q * KT + k + 1)) if m == 0 else None)

            with pe.Fori(0, QUARTERS // 2) as j:
                quarter(j * 2, 0)
                quarter(j * 2 + 1, 1)

            done = lane("pe")
            pe.wait_ge(s["mod_done"], 3 * (KT + 1))
            for m in range(3 * KT):
                mm = pe.matmul(ps[:, 7, m:m + 1], mod_acc[:, m * P:(m + 1) * P], K["ones"][:, 0:1], start=True, stop=True)
            done(mm, "modulation")
            pe.wait_ge(s["e_add"], QUARTERS * KT)
            pe.matmul(ps[:, 2, :], K["mean"], hf1[:, 0], start=True, stop=True)
            done(pe.matmul(ps[:, 3, :], K["mean"], hf1[:, 1], start=True, stop=True), "square sums")

            def aux(name):
                x = AUX.index(name)
                after(pe, "act", f"ev {name}")
                if x >= 2:
                    after(pe, "dve", f"post {AUX[x - 2]}")
                if x == 4:
                    after(pe, "dve", "var 2")
                bank, src = ps[:, 2 + x % 2, :], raw[:, x % 3]
                if name == "gate":
                    after(pe, "dve", "var 1")
                    for c in range(CH):
                        mm = pe.transpose(bank[:, c * 3 * QH:(c + 1) * 3 * QH], src[0:3 * QH, c * P:(c + 1) * P],
                                          ident[0:3 * QH, 0:3 * QH])
                elif name[0] == "v":
                    if name == "vs":
                        after(pe, "dve", "var 2")
                    for c in range(CH):
                        mm = pe.transpose(bank[:, c * P:(c + 1) * P], src[:, c * P:(c + 1) * P], ident)
                elif name == "kr":
                    mm = pe.matmul(bank[0:MD], K2["rot_m"][MN:MD, 0:MD], src[MN:MD], start=True, stop=True)
                else:
                    mm = pe.matmul(bank, K2["rot"], src, start=True, stop=True)
                done(mm, f"aux {name}")

            def hidden(w):
                pe.wait_ge(w1_in[w], 32)
                after(pe, "dve", ("window k", "window v")[w])
                for l in range(CMP_BLOCK):
                    mm = pe.matmul(ps[:, 4 + w, 0:2 * NCP], w1[w][:, l], xb[:, l].rearrange("p g n -> p (g n)"),
                                   start=(l == 0), stop=(l == CMP_BLOCK - 1))
                done(mm, ("hidden k", "hidden v")[w])

            pe.wait_ge(s["c2_in"], 16)
            for a, name in enumerate(TWO):
                if a >= 2:
                    after(pe, "act", f"ev {TWO[a - 2]}")
                n = U_TWO + a
                unit(n, n % RING, hhi, hlo, ready=(lambda k: after(pe, "dve", f"norm low {k}")) if a == 0 else None)
                if a == 1:
                    pe.wait_ge(s["cpos_in"], 32)
                    after(pe, "dve", "mod")
                    done(pe.transpose(ps[:, 7, P:P + CMP_BLOCK], cpos[0:CMP_BLOCK, :], ident[0:CMP_BLOCK, 0:CMP_BLOCK]),
                         "positions turned")
                if TWO[a - 1] in AUX and a:
                    aux(TWO[a - 1])
                if name == "q1":
                    hidden(0)
                if name == "q3":
                    hidden(1)
                if name == "kw":
                    pe.wait_ge(s["w2_in"], 48)
                    after(pe, "dve", "hidden v 4")
                    pe.matmul(ps[:, 6, 0:2 * NCP], w2c[:, 0:2].rearrange("p a c -> p (a c)"),
                              hid[:, 0, 1].rearrange("p g n -> p (g n)"), start=True, stop=True)
                    for g in range(2):
                        mm = pe.matmul(ps[:, 6, 2 * NCP + g * DK:2 * NCP + (g + 1) * DK],
                                       hid4[:, g].rearrange("p r n -> p (r n)"), w2c[:, 2], start=True, stop=True)
                    done(mm, "second layer")
                if name == "cq0":
                    after(pe, "dve", "kc")
                    after(pe, "dve", "positions")
                    done(pe.matmul(ps[:, 7, 0:2 * NCP], K2["rot"], ktmp[:, 0].rearrange("p g n -> p (g n)"),
                                   start=True, stop=True), "rotate kc")
                if name == "cq1":
                    after(pe, "dve", "kc rotated")
                    for h in range(QH):
                        g, r = h // 4, slice(h // 4 * DK, (h // 4 + 1) * DK)
                        for c in range(CH):
                            mm = pe.matmul(ps[:, 4 + g, c * P + h % 4 * NCP:c * P + (h % 4 + 1) * NCP],
                                           q2T[r, h % 4, c * P:(c + 1) * P], kcr[r, g], start=True, stop=True)
                    done(mm, "block scores")
                if name == "ckv":
                    for w in range(2):
                        after(pe, "act", f"square cq{w}")
                        mm = pe.matmul(ps[:, 6, :], K["mean"], csq[:, w], start=(w == 0), stop=(w == 1))
                    done(mm, "sum cq")
            aux("kr")
            after(pe, "act", "square ckv")
            done(pe.matmul(ps[:, 7, :], K["mean"], csq[:, 0], start=True, stop=True), "sum ckv")
            after(pe, "act", "root ckv")
            after(pe, "dve", "probs")
            for g in range(2):
                for c in range(CH):
                    mm = pe.transpose(ps[:, 6 + g, c * P:(c + 1) * P], csc[:, g, c * P:(c + 1) * P], ident)
            done(mm, "block turned")
            after(pe, "act", "block turned")
            after(pe, "dve", "post kr")
            for g in range(2):
                for c in range(CH):
                    mm = pe.matmul(ps[:, 2 + c, g * 256:(g + 1) * 256], cpT[:, g, c * P:(c + 1) * P],
                                   vbd[:, g].rearrange("p h d -> p (h d)"), start=True, stop=True)
            done(mm, "block values")

            def attend(first, count, q_of, k_of, v_of, stream, bank_of=score_bank, bank_free=None, between=lambda i: None):
                def fill(n):
                    for _ in range(n):
                        next(stream, None)

                for i in range(count + 3):
                    if i < count:
                        n, qt = first + i, i % 4
                        if bank_free:
                            bank_free(i)
                        elif i >= 3:
                            pe.wait_ge(s["at_exp"], n - 2)
                        bank = bank_of(i)
                        pe.matmul(ps[:, bank, 0:(qt + 1) * P], q_of(i), k_of(i), start=True, stop=False)
                        pe.matmul(ps[:, bank, qt * P:(qt + 1) * P], identb[:, :], negb[:, :], start=False, stop=True)                            .then_inc(s["at_s"], 1)
                        fill(3 if i % 2 else 2)
                        between(i)
                    if 2 <= i < count + 2:
                        k, n, qt = i - 2, first + i - 2, (i - 2) % 4
                        pe.wait_ge(s["at_exp"], n + 1)
                        if k >= 2:
                            pe.wait_ge(s["at_tev"], n - 1)
                        for c in range(qt + 1):
                            mm = pe.transpose(ps[:, 5 + k % 2, c * P:(c + 1) * P], prob[:, k % 2, c * P:(c + 1) * P], ident)
                        mm.then_inc(s["at_t"], 1)
                        fill(1)
                    if i >= 3:
                        k, n, qt = i - 3, first + i - 3, (i - 3) % 4
                        pe.wait_ge(s["at_tev"], n + 1)
                        pe.wait_ge(s["at_done"], n + 1)
                        for c in range(qt + 1):
                            mm = pe.matmul(ps[:, 7, 0:DK], probT[:, k % 2, c * P:(c + 1) * P], v_of(k, c),
                                           start=(c == 0), stop=(c == qt))
                        mm.then_inc(s["at_o"], 1)

            def group(i):
                return slice(i // 8 % 2 * DK, (i // 8 % 2 + 1) * DK)

            after(pe, "dve", "block out")
            after(pe, "act", "ev kr")
            with pe.Fori(0, 2) as j:
                def z_units():
                    for u in range(4):
                        if u >= 2:
                            pe.wait_ge(s["z_done"], j * 4 + u - 1)
                        yield from unit_parts(j * 4 + U_Z + u, u, hhi, hlo)

                pe.wait_ge(s["q_staged"], j * 2 + 2)
                attend(j * 32, 32, lambda i: qh[group(i), i // 16, i % 4 * P:(i % 4 + 1) * P],
                       lambda i: kT2[i // 4 % 2][group(i), 0:(i % 4 + 1) * P],
                       lambda i, c: v2[i // 4 % 2][:, c, group(i)], z_units())
                pe.wait_ge(s["z_done"], j * 4 + 4)
            pe.wait_ge(s["at_done"], 65)

            def turn_mixed(k):
                if k >= 4:
                    after(pe, "dve", f"mixed {k - 4}")
                o = (o_nsa, o_mla)[k // 4]
                for c in range(CH):
                    mm = pe.transpose(ps[:, 2 + k % 4, c * P:(c + 1) * P], o[:, c, k % 4 * P:(k % 4 + 1) * P], ident)
                done(mm, f"turned {k}")

            for k in range(KH):
                turn_mixed(k)
            for k in range(2):
                after(pe, "dve", f"mixed {k}")
            pe.wait_ge(s["wv_in"], 16)
            for c in range(CH):
                mm = pe.matmul(ps[:, c, :], cn[:, 2, c * P:(c + 1) * P], wv[:, :, :].rearrange("p h d -> p (h d)"),
                               start=True, stop=True)
            done(mm, "latent values")
            after(pe, "act", "latent values")
            after(pe, "dve", "rotated keys")
            with pe.Fori(0, 2) as j:
                def out_units():
                    for u in range(4):
                        if u >= 2:
                            pe.wait_ge(s["xa_done"], j * 4 + u - 1)
                        yield from unit_parts(j * 4 + U_OUT2 + u, u, hhi, hlo, ks=range(KH),
                                              ready=(lambda k: after(pe, "pool", f"mix low {k}")) if u == 0 else None)

                def bank_free(what, i):
                    t = TURNS.index((what, i)) - 3
                    if t >= 0:
                        kind, e = TURNS[t]
                        if kind == "s":
                            pe.wait_ge(s["at_exp"], j * 16 + 64 + e + 1)
                        else:
                            pe.wait_ge(s["p_sin" if kind == "rot" else "p_ev"], j * 4 + e + 1)

                def project(hh):
                    par = hh % 2
                    pe.wait_ge(wq_in[par], j * 64 + hh // 2 * 32 + 32)
                    bank_free("q", hh)
                    for k in range(2):
                        pe.matmul(ps[0:MD, turn_bank("q", hh), :], wq[:, par, k], cn[:, k], start=(k == 0), stop=(k == 1))
                    bank_free("k", hh)
                    pe.matmul(ps[0:MN, turn_bank("k", hh), :], wk[:, par], cn[:, 2], start=True, stop=True)\
                        .then_inc(s["p_ps"], 1)

                def swap(hh):
                    pe.wait_ge(s["p_ev"], j * 4 + hh + 1)
                    bank_free("rot", hh)
                    pe.matmul(ps[0:MD, turn_bank("rot", hh), :], K2["rot_m"][0:MD, 0:MD], qraw[0:MD, hh % 2],
                              start=True, stop=True).then_inc(s["p_rot"], 1)

                def between(i):
                    if i < 12 and i % 4 == 0:
                        project(i // 4 + 1)
                    if i < 12 and i % 4 == 1:
                        swap(i // 4 + 1)

                def scores_free(i):
                    bank_free("s", i)
                    if i % 4 == 0:
                        pe.wait_ge(s["p_q"], j * 4 + i // 4 + 1)

                stream = out_units()
                pe.wait_ge(s["at_done"], j * 16 + 65)
                project(0)
                for _ in range(6):
                    next(stream, None)
                swap(0)
                for _ in range(6):
                    next(stream, None)
                attend(j * 16 + 64, 16, lambda i: qm[0:MD, i // 4 % 2, i % 4 * P:(i % 4 + 1) * P],
                       lambda i: km[0:MD, i // 4 % 2, 0:(i % 4 + 1) * P],
                       lambda i, c: v_mla[:, c, bass.ds(j * 4 * DK + i // 4 * DK, DK)], stream,
                       lambda i: turn_bank("s", i), scores_free, between)
                for _ in range(48):
                    next(stream, None)
                pe.wait_ge(s["xa_done"], j * 4 + 4)
            pe.wait_ge(s["at_done"], 97)
            for k in range(KH, KT):
                turn_mixed(k)
            for m in range(KT):
                if m >= 2:
                    after(pe, "dve", f"x {m - 2}")
                unit(U_OUT2 + KT + m, m % RING, hhi, hlo, ks=range(KH, KT),
                     ready=(lambda k: after(pe, "pool", f"mix low {k}")) if m == 0 else None)
                if m:
                    after(pe, "act", f"out squares {m - 1}")
                    done(pe.matmul(ps[:, 2, :], K["mean"], osqr[:, (m - 1) % 2], start=(m == 1), stop=False),
                         f"out sums {m - 1}")
            after(pe, "act", f"out squares {KT - 1}")
            done(pe.matmul(ps[:, 2, :], K["mean"], osqr[:, (KT - 1) % 2], start=False, stop=True), f"out sums {KT - 1}")
            for k in range(KT):
                after(pe, "dve", f"y {k}")
                if k >= 2:
                    after(pe, "act", f"out rows {k - 2}")
                for c in range(CH):
                    mm = pe.transpose(ps[:, 4 + k % 2, c * P:(c + 1) * P], onorm[:, k % 2, c * P:(c + 1) * P], ident)
                done(mm, f"back {k}")


_INS = ["x", "norm_mix", "norm_mlp", "norm_final", "dn_w_in", "dn_conv_w", "dn_a_log", "dn_dt_bias", "dn_norm_w",
        "dn_w_out", "mlp_w_up", "mlp_w_down", "c_2", "positions_2", "ada_w_2", "ada_b_2", "norm_g_2", "w_in_2",
        "cmp_pos_2", "cmp_k_w1_2", "cmp_k_w2_2", "cmp_v_w1_2", "cmp_v_w2_2", "q_norm_g_2", "w_q_up_2",
        "kv_norm_g_2", "w_kv_up_2", "w_out_2", "final_norm_g_2"]


def kernel(**inputs):
    import concourse.bacc as bacc
    from concourse.bass_utils import run_bass_kernel_spmd

    nc = bacc.Bacc("TRN2", target_bir_lowering=False, num_devices=1)
    arrays, A = {}, {}

    def give(name, a):
        arrays[name] = a
        A[name] = nc.dram_tensor(name, a.shape, mybir.dt.from_np(a.dtype), kind="ExternalInput").ap()

    for name in _INS:
        give(name, np.ascontiguousarray(inputs[name]))
    consts, cols = shape_constants()
    give("consts", consts)
    consts2, cols2 = shape_constants_2()
    give("consts2", consts2)
    out = nc.dram_tensor("out", (T, D), mybir.dt.float32, kind="ExternalOutput").ap()
    build(nc, A, out, cols, cols2)
    r = run_bass_kernel_spmd(nc, [arrays], core_ids=[0])
    return r.results[0]["out"].reshape(1, T, D)
```
